# Optimizing a Trainium2 kernel written in Bass

```python
import math
import jax, jax.numpy as jnp
from jax import lax
import numpy as np

D_MODEL = 1024
BATCH = 1
SEQ = 1024
DEPTH = 2

N_A = DEPTH // 2
N_B = DEPTH - N_A

E_A = D_MODEL
CONV_WIDTH = 3
CONV_GROUPS = 16

N_HEADS = 8
QK_NOPE = 64
QK_ROPE = 32
V_HEAD = 64
KV_RANK = 256
Q_RANK = 384
E_B = N_HEADS * V_HEAD
ROPE_THETA = 10000.0
Q_BLOCK = 128
SOFTMAX_SCALE = 1.0 / math.sqrt(QK_NOPE + QK_ROPE)

EPS = 1e-6

kernel_name = "yoco_shortconv_mla_hybrid"

def rms_norm(x, g):
    xf = x.astype(jnp.float32)
    y = xf * lax.rsqrt(jnp.mean(xf * xf, axis=-1, keepdims=True) + EPS)
    return (y * g.astype(jnp.float32)).astype(x.dtype)

def rope_tables(positions, dtype):
    inv_freq = ROPE_THETA ** (-jnp.arange(0, QK_ROPE, 2, dtype=jnp.float32) / QK_ROPE)
    ang = positions.astype(jnp.float32)[..., None] * inv_freq
    return jnp.cos(ang).astype(dtype), jnp.sin(ang).astype(dtype)

def apply_rope(x, cos, sin):
    x1, x2 = jnp.split(x, 2, axis=-1)
    return jnp.concatenate([x1 * cos - x2 * sin, x1 * sin + x2 * cos], axis=-1)

def conv_mixer(x, norm_g, w_in, conv_w, w_out):
    S = x.shape[1]
    h = rms_norm(x, norm_g)
    proj = h @ w_in
    b, c, u, g = jnp.split(proj, 4, axis=-1)
    v = c * u
    vp = jnp.pad(v, ((0, 0), (CONV_WIDTH - 1, 0), (0, 0)))
    conv = conv_w[0] * vp[:, 0:S]
    for k in range(1, CONV_WIDTH):
        conv = conv + conv_w[k] * vp[:, k:k + S]
    y = jax.nn.silu(g) * b * conv
    return y @ w_out

def shared_kv(s, kv_norm, w_dkv, ckv_norm, w_ukv, cos, sin):
    Bsz, S, _ = s.shape
    h = rms_norm(s, kv_norm)
    ckr = h @ w_dkv
    c_kv, k_rope = ckr[..., :KV_RANK], ckr[..., KV_RANK:]
    c_kv = rms_norm(c_kv, ckv_norm)
    kv = (c_kv @ w_ukv).reshape(Bsz, S, N_HEADS, QK_NOPE + V_HEAD)
    k_nope, v = kv[..., :QK_NOPE], kv[..., QK_NOPE:]
    k_rope = apply_rope(k_rope, cos, sin)
    return k_nope, k_rope, v

def causal_attention(q_nope, q_rope, k_nope, k_rope, v):
    Bsz, S, H, _ = q_nope.shape
    nb = S // Q_BLOCK
    kpos = jnp.arange(S)

    def one_block(args):
        qn, qr, i = args
        sc = (jnp.einsum('bqhd,bkhd->bhqk', qn, k_nope)
              + jnp.einsum('bqhr,bkr->bhqk', qr, k_rope))
        sc = sc.astype(jnp.float32) * SOFTMAX_SCALE
        qpos = i * Q_BLOCK + jnp.arange(Q_BLOCK)
        mask = kpos[None, :] <= qpos[:, None]
        sc = jnp.where(mask[None, None], sc, -jnp.inf)
        p = jax.nn.softmax(sc, axis=-1).astype(v.dtype)
        return jnp.einsum('bhqk,bkhv->bqhv', p, v)

    qn_b = q_nope.reshape(Bsz, nb, Q_BLOCK, H, QK_NOPE).transpose(1, 0, 2, 3, 4)
    qr_b = q_rope.reshape(Bsz, nb, Q_BLOCK, H, QK_ROPE).transpose(1, 0, 2, 3, 4)
    out = lax.map(one_block, (qn_b, qr_b, jnp.arange(nb)))
    return out.transpose(1, 0, 2, 3, 4).reshape(Bsz, S, H, V_HEAD)

def mla_layer(x, norm_g, w_in, q_norm, w_uq, w_out, k_nope, k_rope, v, cos, sin):
    Bsz, S, _ = x.shape
    h = rms_norm(x, norm_g)
    proj = h @ w_in
    c_q, g = proj[..., :Q_RANK], proj[..., Q_RANK:]
    q = (rms_norm(c_q, q_norm) @ w_uq).reshape(Bsz, S, N_HEADS, QK_NOPE + QK_ROPE)
    q_nope, q_rope = q[..., :QK_NOPE], q[..., QK_NOPE:]
    q_rope = apply_rope(q_rope, cos[:, :, None, :], sin[:, :, None, :])
    o = causal_attention(q_nope, q_rope, k_nope, k_rope, v).reshape(Bsz, S, E_B)
    return (o * jax.nn.silu(g)) @ w_out

def setup_inputs(seed: int = 0) -> dict:
    key = jax.random.key(seed)
    ks = jax.random.split(key, 16)
    f32 = jnp.float32

    def w(k, shape, fan_in):
        return jax.random.normal(k, shape, f32) * (fan_in ** -0.5)

    def gain(k, shape):
        return 1.0 + 0.1 * jax.random.normal(k, shape, f32)

    x = jax.random.normal(ks[0], (BATCH, SEQ, D_MODEL), f32)
    positions = jnp.broadcast_to(jnp.arange(SEQ, dtype=jnp.int32), (BATCH, SEQ))
    return {
        "x": x,
        "positions": positions,
        "a_norm": gain(ks[1], (N_A, D_MODEL)),
        "a_w_in": w(ks[2], (N_A, D_MODEL, 4 * E_A), D_MODEL),
        "a_conv": w(ks[3], (N_A, CONV_WIDTH, E_A), CONV_WIDTH),
        "a_w_out": w(ks[4], (N_A, E_A, D_MODEL), E_A),
        "kv_norm": gain(ks[5], (D_MODEL,)),
        "w_dkv": w(ks[6], (D_MODEL, KV_RANK + QK_ROPE), D_MODEL),
        "ckv_norm": gain(ks[7], (KV_RANK,)),
        "w_ukv": w(ks[8], (KV_RANK, N_HEADS * (QK_NOPE + V_HEAD)), KV_RANK),
        "b_norm": gain(ks[9], (N_B, D_MODEL)),
        "b_w_in": w(ks[10], (N_B, D_MODEL, Q_RANK + E_B), D_MODEL),
        "b_q_norm": gain(ks[11], (N_B, Q_RANK)),
        "b_w_uq": w(ks[12], (N_B, Q_RANK, N_HEADS * (QK_NOPE + QK_ROPE)), Q_RANK),
        "b_w_out": w(ks[13], (N_B, E_B, D_MODEL), E_B),
        "final_norm": gain(ks[14], (D_MODEL,)),
    }

def reference(x, positions, a_norm, a_w_in, a_conv, a_w_out, kv_norm, w_dkv, ckv_norm,
              w_ukv, b_norm, b_w_in, b_q_norm, b_w_uq, b_w_out, final_norm):
    cos, sin = rope_tables(positions, x.dtype)
    k_nope = k_rope = v = None
    for layer in range(DEPTH):
        if layer < N_A:
            x = x + conv_mixer(x, a_norm[layer], a_w_in[layer], a_conv[layer], a_w_out[layer])
            if layer == N_A - 1:
                k_nope, k_rope, v = shared_kv(x, kv_norm, w_dkv, ckv_norm, w_ukv, cos, sin)
        else:
            j = layer - N_A
            x = x + mla_layer(x, b_norm[j], b_w_in[j], b_q_norm[j], b_w_uq[j], b_w_out[j],
                              k_nope, k_rope, v, cos, sin)
    return rms_norm(x, final_norm)


_drawn_inputs = setup_inputs


def setup_inputs(seed=0):
    import zlib

    import numpy as np

    out = dict(_drawn_inputs(seed))
    spreads = {}
    factors = {'kv_norm': 6.12, 'ckv_norm': 6.095, 'b_norm': 6.09, 'b_q_norm': 8.0}
    for name, (base, spread) in spreads.items():
        noise = np.random.default_rng([zlib.crc32(name.encode()), seed]).standard_normal(out[name].shape)
        drawn = base * np.exp(spread * noise) if base else spread * noise
        out[name] = __import__('jax').numpy.asarray(drawn.astype(out[name].dtype))
    for name, factor in factors.items():
        out[name] = (out[name] * factor).astype(out[name].dtype)
    return out
```

```python
from contextlib import ExitStack

import numpy as np

import concourse.bass as bass
from concourse import mybir

F32 = mybir.dt.float32
F32R = mybir.dt.float32r
BF16 = mybir.dt.bfloat16
I32 = mybir.dt.int32
ALU = mybir.AluOpType
ACT = mybir.ActivationFunctionType
AX_X = mybir.AxisListType.X

P = 128
S = 1024
D = 1024
KC = D // P
TB = S // P
HALF = 512
CONV_WIDTH = 3
HEADS = 8
PAIRS = HEADS // 2
NOPE, ROPE, VH = 64, 32, 64
RH = ROPE // 2
KV_RANK, Q_RANK = 256, 384
CKV, CQ = KV_RANK // P, Q_RANK // P
GC = HEADS * VH // P
SCALE = 1.0 / float(np.sqrt(np.float64(NOPE + ROPE)))
EPS = 1e-6
THETA = 10000.0
MASK = -3.0e38
ROUND = 1.5 * 2.0 ** 23
TWO_PI_A = 6.28125
TWO_PI_B = float(np.float32(2 * np.pi - TWO_PI_A))
TWO_PI_C = float(2 * np.pi - TWO_PI_A - np.float64(np.float32(2 * np.pi - TWO_PI_A)))
PI_IN = 3.1415925

C_ID, C_SEL, C_ONE, C_FREQ, C_TURN, C_PHASE, C_POW, C_MASK = 0, 128, 256, 257, 258, 259, 260, 261
C_END = C_MASK + 4 * P


def constants():
    c = np.zeros((P, C_END), np.float32)
    c[:, C_ID:C_ID + P] = np.eye(P)
    for r in range(2 * ROPE):
        c[r, C_SEL:C_SEL + P] = [r % ROPE == m % ROPE for m in range(P)]
    c[:, C_ONE] = 1.0
    freq = np.float32(THETA) ** (-np.arange(0, ROPE, 2, dtype=np.float32) / np.float32(ROPE))
    for r in range(ROPE):
        c[r, C_FREQ] = freq[r % RH]
        c[r, C_PHASE] = np.pi / 2
        c[r, C_TURN] = 0.25
        c[ROPE + r, C_FREQ] = freq[r % RH] * (-1 if r < RH else 1)
    c[:, C_POW] = -0.5
    mask = np.zeros((P, 2, 2 * P), np.float32)
    above = np.triu(np.ones((P, P), bool), 1)
    mask[:, 0, 0:P][above] = MASK
    mask[:, 0, P:] = MASK
    mask[:, 1, P:][above] = MASK
    c[:, C_MASK:] = mask.reshape(P, 4 * P)
    return c


def trunk(nc, x, positions, a_norm, a_w_in, a_conv, a_w_out, kv_norm, w_dkv, ckv_norm, w_ukv,
          b_norm, b_w_in, b_q_norm, b_w_uq, b_w_out, final_norm, const, out):
    x_d = x.rearrange("a (t p) d -> p (a t) d", p=P)
    out_d = out.rearrange("a (t p) d -> p (a t) d", p=P)
    w_in_d = a_w_in.rearrange("a (k p) n -> p (a k) n", p=P)
    w_out_d = a_w_out.rearrange("a (k p) n -> p (a k) n", p=P)
    w_dkv_d = w_dkv.rearrange("(k p) n -> p k n", p=P)
    w_b_d = b_w_in.rearrange("a (k p) n -> p (a k) n", p=P)
    w_uq_d = b_w_uq.rearrange("a (k p) n -> p (a k) n", p=P)
    w_ukv_d = w_ukv.rearrange("(k p) n -> p k n", p=P)
    w_bo_d = b_w_out.rearrange("a (k p) n -> p (a k) n", p=P)
    x2_d = nc.dram_tensor("x2_scratch", [S, D], F32, kind="Internal").ap()
    x2_d = x2_d.rearrange("(t p) d -> p t d", p=P)

    with ExitStack() as ctx:
        def sem(name):
            return ctx.enter_context(nc.semaphore(name))

        base = (nc.sbuf_base + 31) // 32 * 32
        small = [base]

        def const_sb(name, shape, dt=F32):
            n = int(np.prod(shape[1:])) * (2 if dt == BF16 else 4)
            t = nc.alloc_sbuf_tensor_at(name, shape, dt, offset=small[0])
            small[0] += (n + 31) // 32 * 32
            return t

        cst = const_sb("cst", [P, C_END])
        maskb = const_sb("maskb", [P, 2, 2 * P], BF16)
        identb = const_sb("identb", [P, P], BF16)
        g_a = const_sb("g_a", [P, KC])
        g_kv = const_sb("g_kv", [P, KC])
        g_b = const_sb("g_b", [P, KC])
        g_ckv = const_sb("g_ckv", [P, CKV])
        g_q = const_sb("g_q", [P, CQ])
        conv_w = const_sb("conv_w", [P, CONV_WIDTH, KC])
        ssq = const_sb("ssq", [P, 2 * TB])
        msq = const_sb("msq", [P, 2 * TB])
        rms = const_sb("rms", [P, 2 * TB])
        smax = const_sb("smax", [P, 4])
        smaxn = const_sb("smaxn", [P, 4])
        rsum = const_sb("rsum", [P, 2, TB])
        rrec = const_sb("rrec", [P, 2, TB])
        arena = small[0]
        K = 1024

        def at(name, kib, shape, dt=F32):
            return nc.alloc_sbuf_tensor_at(name, shape, dt, offset=arena + kib * K)

        act_h = at("act_h", 0, [P, KC, S], F32R)
        act_l = at("act_l", 32, [P, KC, S], F32R)
        xt = at("xt", 64, [P, KC, S])
        y_h = at("y_h", 96, [P, KC, S], F32R)
        y_l = at("y_l", 128, [P, KC, S], F32R)
        x_in = at("x_in", 96, [P, TB, D])
        junk = at("junk", 128, [P, TB, D])
        raw = at("raw", 160, [P, 2, KC, P])
        w_h = at("w_h", 168, [P, 2, KC, P], F32R)
        w_l = at("w_l", 176, [P, 2, KC, P], F32R)
        r_bc = at("r_bc", 184, [P, S])
        r2_bc = at("r2_bc", 188, [P, S])
        cr = at("cr", 192, [P, S])
        v = at("v", 196, [P, S + CONV_WIDTH - 1])
        cv = at("cv", 201, [P, S])
        gr = at("gr", 205, [P, S])
        sg = at("sg", 209, [P, S])
        r_wide = at("r_wide", 209, [P, TB, P])
        sq = [at("sq0", 192, [P, S]), at("sq1", 201, [P, S])]
        acc = at("acc", 205, [P, S])
        gate = at("gate", 96, [P, GC, S])
        zc = at("zc", 112, [P, CKV + CQ, S])
        tq = [at("tq0", 132, [P, S]), at("tq1", 136, [P, S])]
        pos_i = at("pos_i", 140, [P, S], I32)
        pos_f = at("pos_f", 144, [P, S])
        turns = at("turns", 148, [P, S])
        angle = at("angle", 152, [P, S])
        acc_q = at("acc_q", 209, [P, S])
        rk_wide = at("rk_wide", 188, [P, TB, P])
        rq_wide = at("rq_wide", 196, [P, TB, P])
        zk = at("zk", 201, [2 * ROPE, S])
        ckv_h = at("ckv_h", 140, [P, CKV, S], F32R)
        ckv_l = at("ckv_l", 148, [P, CKV, S], F32R)
        cq_h = at("cq_h", 188, [P, CQ, S], F32R)
        cq_l = [at(f"cq_l{k}", o, [P, S], F32R) for k, o in enumerate((156, 205, 209))]
        x2_st = [at("x2_st0", 32, [P, D]), at("x2_st1", 36, [P, D])]
        q_h = [at("qe_h", 0, [P, S], F32R), at("qo_h", 8, [P, S], F32R)]
        q_l = [at("qe_l", 4, [P, S], F32R), at("qo_l", 12, [P, S], F32R)]
        k_h = [at("ke_h", 16, [P, S], F32R), at("ko_h", 24, [P, S], F32R)]
        k_l = [at("ke_l", 20, [P, S], F32R), at("ko_l", 28, [P, S], F32R)]
        pt_h = at("pt_h", 32, [P, TB, 2 * P], F32R)
        pt_l = at("pt_l", 40, [P, TB, 2 * P], F32R)
        prob = [at("prob0", 48, [P, S]), at("prob1", 52, [P, S])]
        vv = [at("v_e", 56, [P, TB, 2 * VH], F32R), at("v_o", 60, [P, TB, 2 * VH], F32R)]
        q_f = [at("q_fe", 64, [P, S]), at("q_fo", 68, [P, S])]
        k_f = at("k_f", 72, [P, S])
        v_t = at("v_t", 76, [P, S])
        v_f = at("v_f", 80, [P, TB, P])
        o_t = at("o_t", 84, [P, S])
        rs_wide = at("rs_wide", 88, [P, TB, 2, VH])
        gs = at("gs", 92, [P, S])
        og = at("og", 112, [P, GC, S])
        u_raw = at("u_raw", 160, [P, 10, P])
        u_h = at("u_h", 165, [P, 10, P], F32R)
        u_l = at("u_l", 170, [P, 10, P], F32R)
        o_lo = at("o_lo", 180, [VH, 2 * P])
        og_h = at("og_h", 0, [P, GC, S], F32R)
        og_l = at("og_l", 16, [P, GC, S], F32R)
        wb_raw = [at("wb_raw0", 205, [P, D]), at("wb_raw1", 209, [P, D])]
        wb_h = at("wb_h", 140, [P, GC, D], F32R)
        wb_l = at("wb_l", 64, [P, GC, D], F32R)
        g_f = at("g_f", 128, [P, D])
        x2_r = [at("x2_r0", 48, [P, D]), at("x2_r1", 52, [P, D])]
        x3 = [at("x3_0", 40, [P, D]), at("x3_1", 44, [P, D])]
        x3_sq = at("x3_sq", 56, [P, D])
        y_out = [at("y_out0", 32, [P, D]), at("y_out1", 36, [P, D])]

        ident = cst[:, C_ID:C_ID + P]
        ones = cst[:, C_ONE:C_ONE + 1]

        ps = ctx.enter_context(nc.psum_tensor("ps", [P, 4, 2 * HALF], F32))

        s_const = sem("const_in")
        s_x = [sem(f"x_in{t}") for t in range(TB)]
        s_raw = [sem("raw_in0"), sem("raw_in1")]
        s_pos = sem("pos_in")
        s_whi = sem("w_hi")
        s_wlo = sem("w_lo")
        s_wg = sem("w_gain")
        s_tile = sem("tile_done")
        s_ev = sem("ps_evacuated")
        s_xtp = sem("x_transposed")
        s_xhi = sem("x_hi")
        s_xcp = sem("x_copied")
        s_xlo = sem("x_lo")
        s_xsq = sem("x_squares")
        s_init = sem("dve_init")
        s_ms = sem("mean_square")
        s_pow = sem("rsqrt_done")
        s_rw = sem("r_widened")
        s_rt = sem("r_transposed")
        s_rsb = sem("r_in_sbuf")
        s_cv = sem("conv_step")
        s_silu = sem("silu_done")
        s_yhi = sem("y_hi")
        s_ylo = sem("y_lo")
        s_x2hi = sem("x2_hi")
        s_x2lo = sem("x2_lo")
        s_x2sq = sem("x2_square")
        s_acc = sem("acc_step")
        s_ss = sem("ss_product")
        s_tab = sem("table_step")
        s_sin = sem("sin_done")
        s_csq = sem("c_square")
        s_cacc = sem("c_acc")
        s_gsilu = sem("gate_silu")
        s_cn = sem("c_normed")
        s_chi = sem("c_hi")
        s_clo = sem("c_lo")
        s_kr = sem("k_rope_step")
        s_krp = sem("k_rope_product")
        s_krhi = sem("k_rope_hi")
        s_krlo = sem("k_rope_lo")
        s_x2t = sem("x2_transposed")
        s_x2s = sem("x2_staged")
        s_x2w = [sem("x2_written0"), sem("x2_written1")]
        s_u = sem("u_in")
        s_uhi = sem("u_hi")
        s_ulo = sem("u_lo")
        s_pj = sem("proj_product")
        s_pja = sem("proj_evac_act")
        s_pjv = sem("proj_evac_dve")
        s_sphi = sem("split_hi")
        s_splo = sem("split_lo")
        s_s = sem("scores_done")
        s_mxr = sem("row_max")
        s_mx = sem("row_max_scaled")
        s_exp = sem("exp_done")
        s_t = sem("p_transposed")
        s_th = sem("pt_hi")
        s_tl = sem("pt_lo")
        s_pv = sem("pv_done")
        s_om = sem("o_low_moved")
        s_o = sem("o_added")
        s_rr = sem("rsum_inverted")
        s_rsw = sem("rsum_widened")
        s_og = sem("og_done")
        s_ogh = sem("og_hi")
        s_ogl = sem("og_lo")
        s_wb = [sem("wb_in0"), sem("wb_in1")]
        s_wbh = sem("wb_hi")
        s_wbl = sem("wb_lo")
        s_gf = sem("gf_in")
        s_x2r = [sem("x2_read0"), sem("x2_read1")]
        s_fin = sem("last_product")
        s_x3 = sem("x3_done")
        s_x3q = sem("x3_squared")
        s_fms = sem("final_ms")
        s_fr = sem("final_rsqrt")
        s_y = sem("y_normed")
        s_out = [sem("out_written0"), sem("out_written1")]

        N_A, N_O = 4 * KC, KC
        OUT0, B0 = N_A, N_A + N_O
        b_tiles = [("dkv", c * P, g_kv, p) for c, p in ((0, 0), (1, 1))]
        b_tiles += [("b", c * P, g_b, p) for c, p in enumerate((2, 0, 1, 2, 0, 2, 0))]
        b_tiles += [("rope", KV_RANK, g_kv, 1)]
        N_B = len(b_tiles)
        LAST = B0 + N_B - 1
        raw_before_rope = 16 * (LAST // 2)

        def lo_done(n):
            return n + 3

        def tile_done(n):
            return n + 3

        def slot_free(n):
            return n + 1

        def evacuated(n):
            return n + 5

        CONSTS = 9

        block = ctx.enter_context(nc.Block())

        @block.sync
        def _(sp):
            gains = [(cst[:, :], const), (g_a[:], a_norm.rearrange("a (k p) -> p (a k)", p=P)),
                     (g_kv[:], kv_norm.rearrange("(k p) -> p k", p=P)),
                     (g_b[:], b_norm.rearrange("a (k p) -> p (a k)", p=P)),
                     (g_ckv[:], ckv_norm.rearrange("(k p) -> p k", p=P)),
                     (g_q[:], b_q_norm.rearrange("a (k p) -> p (a k)", p=P))]
            gains += [(conv_w[:, w, :], a_conv[0, w, :].rearrange("(k p) -> p k", p=P))
                      for w in range(CONV_WIDTH)]
            assert len(gains) == CONSTS
            sp.dma_start(*gains[0]).then_inc(s_const, 16)
            for t in range(4):
                sp.dma_start(x_in[:, t, :], x_d[:, t, :]).then_inc(s_x[t], 16)
            with nc.allow_non_contiguous_dma(reason="gains by feature, 4 bytes each, loaded once"):
                for dst, src in gains[1:]:
                    sp.dma_start(dst, src).then_inc(s_const, 16)
            for t in range(4, TB):
                sp.dma_start(x_in[:, t, :], x_d[:, t, :]).then_inc(s_x[t], 16)

            with sp.Fori(1, KC + 1) as j:
                for t, part in enumerate((1, 2, 3, 0)):
                    sp.wait_ge(s_wlo, slot_free(4 * j + (t - 4)))
                    sp.dma_start(raw[:, t % 2], w_in_d[:, :, bass.ds(j * P + (part * D - P), P)]
                                 ).then_inc(s_raw[t % 2], 16)
            with sp.Fori(1, KC // 2 + 1) as i:
                for t in range(2):
                    sp.wait_ge(s_wlo, slot_free(2 * i + (OUT0 + t - 2)))
                    sp.dma_start(raw[:, t], w_out_d[:, :, bass.ds(i * 2 * P + (t - 2) * P, P)]
                                 ).then_inc(s_raw[t], 16)
            for e, (kind, col, _, _) in enumerate(b_tiles):
                n = B0 + e
                sp.wait_ge(s_wlo, slot_free(n))
                dst = raw[:, n % 2]
                if kind == "rope":
                    cols = [(0, col, ROPE), (ROPE, col + RH, RH), (ROPE + RH, col, RH)]
                    for to, frm, m in cols:
                        sp.dma_start(dst[:, :, to:to + m], w_dkv_d[:, :, frm:frm + m]
                                     ).then_inc(s_raw[n % 2], 16)
                else:
                    src = w_dkv_d if kind == "dkv" else w_b_d
                    sp.dma_start(dst, src[:, :, col:col + P]).then_inc(s_raw[n % 2], 16)
                if e == 0:
                    sp.wait_ge(s_tile, tile_done(B0 - 1))
                    sp.dma_start(pos_i[:], positions[0:1, :].broadcast_to([P, S])).then_inc(s_pos, 16)

            def load_pair(c):
                per = NOPE + ROPE
                for odd, base_col in ((0, 0), (1, P // 2)):
                    rope = NOPE if odd == 0 else 0
                    parts = [(0 if odd == 0 else NOPE, 0, NOPE), (rope, NOPE, ROPE),
                             (rope + ROPE, NOPE + RH, RH), (rope + ROPE + RH, NOPE, RH)]
                    for to, frm, m in parts:
                        sp.dma_start(u_raw[:, odd * CQ:(odd + 1) * CQ, to:to + m],
                                     w_uq_d[:, :, bass.ds(c * 2 * per + odd * per + frm, m)]
                                     ).then_inc(s_u, 16)
                for what in range(2):
                    for odd in range(2):
                        sp.dma_start(u_raw[:, 2 * CQ + what * CKV:2 * CQ + (what + 1) * CKV,
                                           odd * NOPE:(odd + 1) * NOPE],
                                     w_ukv_d[:, :, bass.ds(c * 4 * NOPE + (2 * odd + what) * NOPE, NOPE)]
                                     ).then_inc(s_u, 16)

            sp.wait_ge(s_wlo, lo_done(LAST))
            load_pair(0)
            for t in range(TB):
                sp.wait_ge(s_x2s, t + 1)
                sp.dma_start(x2_d[:, t, :], x2_st[t % 2][:]).then_inc(s_x2w[t % 2], 16)
            sp.wait_ge(s_clo, CKV + CQ)
            sp.dma_start(g_f[:], final_norm.rearrange("(a d) -> a d", a=1).broadcast_to([P, D])
                         ).then_inc(s_gf, 16)
            with sp.Fori(0, PAIRS - 1) as c:
                sp.wait_ge(s_ulo, c + 1)
                load_pair(c + 1)
            sp.wait_ge(s_pj, 10 + 12 * (PAIRS - 1))
            for k in range(GC):
                if k >= 2:
                    sp.wait_ge(s_wbl, k - 1)
                sp.dma_start(wb_raw[k % 2][:], w_bo_d[:, k, :]).then_inc(s_wb[k % 2], 16)
            for w in s_x2w:
                sp.wait_ge(w, 16 * TB // 2)
            sp.wait_ge(s_t, 20 * PAIRS)
            for t in range(TB):
                if t >= 2:
                    sp.wait_ge(s_x3, t - 1)
                sp.dma_start(x2_r[t % 2][:], x2_d[:, t, :]).then_inc(s_x2r[t % 2], 16)
                if t >= 2:
                    sp.wait_ge(s_y, t - 1)
                    sp.dma_start(out_d[:, t - 2, :], y_out[t % 2][:]).then_inc(s_out[t % 2], 16)
            for t in (TB, TB + 1):
                sp.wait_ge(s_y, t - 1)
                sp.dma_start(out_d[:, t - 2, :], y_out[t % 2][:]).then_inc(s_out[t % 2], 16)
            for w in s_out:
                sp.wait_ge(w, 16 * TB // 2)

        STEPS = [(h, g) for h in range(2) for g in range(4)]
        UNITS = {1: (["k0"], ["k1"]), 2: (["qe0"], ["qe1"]), 3: (["v0"], ["v1"]),
                 4: (["vt0"], ["vt1"]), 5: (["qo0"], ["qo1"]), 7: ([], ["r0", "r1"])}
        PROJ = [u for s in (1, 2, 3, 4, 5) for part in UNITS[s] for u in part]
        ORDER = PROJ + ["r0", "r1"]
        BY_ACT = ("k0", "k1", "v0", "v1", "vt0", "vt1")
        BY_DVE = ("qe0", "qe1", "qo0", "qo1", "r0", "r1")

        def units_of(step, last):
            return UNITS.get(step, ([], [])) if not last or step == 7 else ([], [])

        def pj_count(c, name):
            if c is None:
                return PROJ.index(name) + 1
            return 12 * c + (10 + ORDER.index(name) + 1)

        def pj_count_last(name):
            return 10 + 12 * (PAIRS - 1) + ("r0", "r1").index(name) + 1

        def act_count(c, name):
            return BY_ACT.index(name) + 1 if c is None else 6 * c + (6 + BY_ACT.index(name) + 1)

        def dve_count(c, name, last=False):
            if c is None:
                return BY_DVE.index(name) + 1
            if last:
                return 4 + 6 * (PAIRS - 1) + ("r0", "r1").index(name) + 1
            return 6 * c + (4 + BY_DVE.index(name) + 1)

        def next_scores(step, last):
            if step < 7:
                return STEPS[step + 1] + (2 * (step + 1),)
            return None if last else (0, 0, 16)

        def t_before(step):
            return sum(g + 1 for _, g in STEPS[:step])

        def split_done(c, what):
            return 6 * c + (("qe", "ke", "ve", "qo", "ko", "vo").index(what) + 1)

        @block.tensor
        def _(pe):
            def products(dst, wh, wl, xh, xl, nk, before=None):
                for half in range(2):
                    cols = slice(half * HALF, (half + 1) * HALF)
                    for k in range(nk):
                        if before is not None and half == 0:
                            before(k)
                        for i, (w, z) in enumerate(((wh, xh), (wh, xl), (wl, xh))):
                            mm = nc.tensor.matmul(dst[:, cols], w(k), z(k, cols),
                                                  start=(k == 0 and i == 0),
                                                  stop=(k == nk - 1 and i == 2))
                return mm

            def tile(slot, pair, xh, xl, before=None):
                return products(ps[:, pair], lambda k: w_h[:, slot, k, :], lambda k: w_l[:, slot, k, :],
                                lambda k, c: xh[:, k, c], lambda k, c: xl[:, k, c], KC, before)

            def widened(dst, wide):
                for t in range(TB):
                    mm = nc.tensor.transpose(dst[:, t * P:(t + 1) * P], wide[:, t, :], ident)
                return mm

            def square_sums(dst, of, first):
                for t in range(TB):
                    mm = nc.tensor.matmul(dst[:, first + t:first + t + 1], of[:, t * P:(t + 1) * P],
                                          ones, start=True, stop=True)
                return mm

            pe.sem_inc(s_tile, 2)
            pe.wait_ge(s_const, 16 * CONSTS)
            for u in range(2 * KC):
                half, k = u // KC, u % KC
                bank = ps[:, 2 + u % 4 // 2, u % 2 * HALF:(u % 2 + 1) * HALF]
                if u >= 4:
                    pe.wait_ge(s_xlo, u - 3)
                for t in range(4):
                    if k == 0:
                        pe.wait_ge(s_x[4 * half + t], 16)
                    mm = nc.tensor.transpose(bank[:, t * P:(t + 1) * P],
                                             x_in[:, 4 * half + t, k * P:(k + 1) * P], ident)
                mm.then_inc(s_xtp, 1)
            pe.wait_ge(s_xlo, 2 * KC)
            pe.wait_ge(s_rw, 1)
            widened(ps[:, 3], r_wide).then_inc(s_rt, 1)

            with pe.Fori(0, KC) as j:
                for t in range(4):
                    pe.wait_ge(s_wlo, lo_done(4 * j + t))
                    pe.wait_ge(s_ev, slot_free(4 * j + t))
                    tile(t % 2, t, act_h, act_l).then_inc(s_tile, 1)

            def y_ready(k):
                if k in (0, KC - 1):
                    pe.wait_ge(s_ylo, KC - 1 if k == 0 else KC)

            with pe.Fori(0, KC // 2) as i:
                for t in range(2):
                    pe.wait_ge(s_wlo, lo_done(OUT0 + 2 * i + t))
                    pe.wait_ge(s_ev, evacuated(OUT0 + 2 * i + t - 2))
                    tile(t, t, y_h, y_l, y_ready).then_inc(s_tile, 1)

            def x2_ready(k):
                if k in (0, KC - 1):
                    pe.wait_ge(s_x2lo, KC - 1 if k == 0 else KC)

            def b_tile(e, freed_by):
                n = B0 + e
                pe.wait_ge(s_wlo, lo_done(n))
                pe.wait_ge(s_ev, evacuated(B0 + freed_by))
                tile(n % 2, b_tiles[e][3], act_h, act_l, x2_ready).then_inc(s_tile, 1)

            b_tile(0, -2)
            pe.wait_ge(s_acc, KC + 2)
            square_sums(ps[:, 3], acc, 0).then_inc(s_ss, 1)
            b_tile(1, -1)
            pe.wait_ge(s_rw, 2)
            widened(ps[:, 3], r_wide).then_inc(s_rt, 1)
            b_tile(2, -1)
            b_tile(3, 0)
            b_tile(4, 1)
            with pe.Fori(0, 2) as i:
                for t, pair in ((0, 2), (1, 0)):
                    pe.wait_ge(s_wlo, lo_done(B0 + 5 + 2 * i + t))
                    pe.wait_ge(s_ev, 3 * i + evacuated(B0 + 2 + t))
                    tile((B0 + 5 + t) % 2, pair, act_h, act_l).then_inc(s_tile, 1)
            pe.wait_ge(s_cacc, CKV - 1 + CQ - 1)
            pe.wait_ge(s_rsb, 2)
            square_sums(ps[:, 3], acc, 0)
            square_sums(ps[:, 3], acc_q, TB).then_inc(s_ss, 1)
            b_tile(9, 4)
            pe.wait_ge(s_rw, 4)
            widened(ps[:, 3], rk_wide).then_inc(s_rt, 1)
            pe.wait_ge(s_ev, evacuated(B0 + 7))
            widened(ps[:, 2], rq_wide).then_inc(s_rt, 1)

            def stream_back(t):
                if t >= 2:
                    pe.wait_ge(s_x2s, t - 1)
                for k in range(KC):
                    mm = nc.tensor.transpose(ps[:, t % 2, k * P:(k + 1) * P],
                                             xt[:, k, t * P:(t + 1) * P], ident)
                mm.then_inc(s_x2t, 1)

            pe.wait_ge(s_ev, evacuated(B0 + 8))
            stream_back(0)
            pe.wait_ge(s_kr, 1)
            for half in range(2):
                mm = nc.tensor.matmul(ps[:, 1, half * HALF:(half + 1) * HALF],
                                      cst[0:2 * ROPE, C_SEL:C_SEL + P],
                                      zk[:, half * HALF:(half + 1) * HALF], start=True, stop=True)
            mm.then_inc(s_krp, 1)
            pe.wait_ge(s_krlo, 2)
            for t in range(1, TB):
                stream_back(t)

            def project(name, c, bank):
                dst = ps[:, bank // 2, bank % 2 * HALF:(bank % 2 + 1) * HALF]
                half = int(name[-1])
                cols = slice(half * HALF, (half + 1) * HALF)
                if name[0] == "r":
                    for t in range(4):
                        mm = nc.tensor.transpose(dst[:, t * P:(t + 1) * P],
                                                 rs_wide[:, 4 * half + t].rearrange("p a b -> p (a b)"),
                                                 ident)
                elif name[:2] == "vt":
                    for t in range(4):
                        kb = 4 * half + t
                        mm = nc.tensor.transpose(dst[:, t * P:(t + 1) * P],
                                                 v_t[:, kb * P:(kb + 1) * P], ident)
                else:
                    first, nk = {"qe": (0, CQ), "qo": (CQ, CQ), "k": (2 * CQ, CKV),
                                 "v": (2 * CQ + CKV, CKV)}[name[:-1]]
                    for k in range(nk):
                        xh = cq_h[:, k, cols] if nk == CQ else ckv_h[:, k, cols]
                        xl = cq_l[k][:, cols] if nk == CQ else ckv_l[:, k, cols]
                        passes = ((u_h, xh), (u_h, xl), (u_l, xh))
                        for i, (w, z) in enumerate(passes):
                            mm = nc.tensor.matmul(dst, w[:, first + k, :], z,
                                                  start=(k == 0 and i == 0),
                                                  stop=(k == nk - 1 and i == 2))
                mm.then_inc(s_pj, 1)

            def scores(h, g, q):
                width = (g + 1) * 2 * P
                qs = slice((2 * g + q) * P, (2 * g + q + 1) * P)
                for at0 in range(0, width, HALF):
                    w = min(HALF, width - at0)
                    dst = ps[:, q, at0:at0 + w]
                    last = at0 + w == width
                    for i, (a, b) in enumerate(((q_h, k_h), (q_h, k_l), (q_l, k_h))):
                        mm = nc.tensor.matmul(dst, a[h][:, qs], b[h][:, at0:at0 + w],
                                              start=(i == 0), stop=(i == 2 and not last))
                    if last:
                        mm = nc.tensor.matmul(ps[:, q, width - 2 * P:width], identb[:], maskb[:, q, :],
                                              start=False, stop=True)
                mm.then_inc(s_s, 1)

            pe.wait_ge(s_clo, CKV + CQ)
            pe.wait_ge(s_ulo, 1)
            banks = (7, 6, 5, 4)
            for i, name in enumerate(PROJ):
                if i >= 4:
                    was = PROJ[i - 4]
                    if was in BY_ACT:
                        pe.wait_ge(s_pja, act_count(None, was))
                    else:
                        pe.wait_ge(s_pjv, dve_count(None, was))
                if name == "vt0":
                    pe.wait_ge(s_pja, act_count(None, "v1"))
                project(name, None, banks[i % 4])
            pe.wait_ge(s_x2s, TB)
            pe.wait_ge(s_splo, 2)
            scores(0, 0, 0)
            scores(0, 0, 1)
            pe.wait_ge(s_pja, 6)
            pe.wait_ge(s_pjv, 4)

            def attention(c, last):
                for step, (h, g) in enumerate(STEPS):
                    nxt = next_scores(step, last)

                    def turn(i):
                        n = t_before(step) + i
                        if i == 0:
                            pe.wait_ge(s_exp, 16 * c + (2 * step + 2))
                        pe.wait_ge(s_tl, 20 * c + (n + 1))
                        for j in range(2):
                            for q in range(2):
                                kb = 2 * i + j
                                mm = nc.tensor.transpose(
                                    ps[:, 2, (n % 2) * HALF + (2 * j + q) * P:
                                       (n % 2) * HALF + (2 * j + q + 1) * P],
                                    prob[q][:, kb * P:(kb + 1) * P], ident)
                        mm.then_inc(s_t, 1)

                    def score(q):
                        if nxt is not None:
                            nh, ng, number = nxt
                            if q == 0 and ng == 0:
                                pe.wait_ge(s_splo, split_done(c, "ko") if nh else split_done(c, "ke") + 6)
                            pe.wait_ge(s_exp, 16 * c + (number + q - 1))
                            scores(nh, ng, q)

                    def unit(name):
                        if name[0] == "r":
                            if name == "r0":
                                pe.wait_ge(s_rsw, c + 1)
                                pe.wait_ge(s_pjv, dve_count(c, "qo1") if not last else 4 + 6 * c)
                            else:
                                pe.wait_ge(s_pjv, dve_count(c, "r0", last))
                        elif name == "k0":
                            pe.wait_ge(s_ulo, c + 2)
                            pe.wait_ge(s_pjv, 6 * c + 4)
                        else:
                            was = ORDER[ORDER.index(name) - 1]
                            if was in BY_ACT:
                                pe.wait_ge(s_pja, act_count(c, was))
                            else:
                                pe.wait_ge(s_pjv, dve_count(c, was))
                        project(name, c, 7)

                    before, after = units_of(step, last)
                    for i in range(min(2, g + 1)):
                        turn(i)
                    score(0)
                    for i in range(2, g + 1):
                        turn(i)
                    score(1)
                    for name in before:
                        unit(name)
                    pe.wait_ge(s_o, 8 * c + (step + 1))
                    pe.wait_ge(s_splo, split_done(c, "vo" if h else "ve"))
                    for kb in range(2 * g + 2):
                        if kb % 2 == 0:
                            pe.wait_ge(s_tl, 20 * c + (2 + t_before(step) + kb // 2 + 1))
                        for part in (pt_h, pt_l):
                            mm = nc.tensor.matmul(ps[:, 3, 0:2 * P], vv[h][:, kb, :], part[:, kb, :],
                                                  start=(kb == 0 and part is pt_h),
                                                  stop=(kb == 2 * g + 1 and part is pt_l))
                    mm.then_inc(s_pv, 1)
                    for name in after:
                        unit(name)

            with pe.Fori(0, PAIRS - 1) as c:
                attention(c, False)
            attention(PAIRS - 1, True)

            pe.wait_ge(s_wbl, GC)
            pe.wait_ge(s_ogl, GC)
            for t in range(TB):
                if t >= 2:
                    pe.wait_ge(s_x3, t - 1)
                for half in range(2):
                    for k in range(GC):
                        rows = slice(t * P, (t + 1) * P)
                        cols = slice(half * HALF, (half + 1) * HALF)
                        for i, (a, b) in enumerate(((og_h, wb_h), (og_h, wb_l), (og_l, wb_h))):
                            mm = nc.tensor.matmul(ps[:, t % 2, cols], a[:, k, rows], b[:, k, cols],
                                                  start=(k == 0 and i == 0),
                                                  stop=(k == GC - 1 and i == 2))
                mm.then_inc(s_fin, 1)

        @block.scalar
        def _(act):
            def copy(dst, src, **more):
                return nc.scalar.activation(dst, src, ACT.Copy, **more)

            def weight_hi(n, slot, fills):
                act.wait_ge(s_raw[slot], fills)
                act.wait_ge(s_tile, slot_free(n))
                copy(w_h[:, slot], raw[:, slot]).then_inc(s_whi, 1)

            for half in range(2):
                for t in range(4 * half, 4 * half + 4):
                    act.wait_ge(s_x[t], 16)
                    nc.scalar.activation(junk[:, t, :], x_in[:, t, :], ACT.Square,
                                         accum_out=ssq[:, t:t + 1]).then_inc(s_xsq, 1)
                if half == 0:
                    act.wait_ge(s_const, 16 * CONSTS)
                for k in range(KC):
                    u = half * KC + k
                    bank = ps[:, 2 + u % 4 // 2, u % 2 * HALF:(u % 2 + 1) * HALF]
                    act.wait_ge(s_xtp, u + 1)
                    copy(act_h[:, k, half * HALF:(half + 1) * HALF], bank,
                         scale=g_a[:, k:k + 1]).then_inc(s_xhi, 1)
            act.wait_ge(s_rt, 1)
            copy(r_bc[:], ps[:, 3]).then_inc(s_rsb, 1)
            weight_hi(0, 0, 16)

            with act.Fori(0, KC) as j:
                for t in range(4):
                    if t == 3:
                        act.wait_ge(s_ev, evacuated(4 * j + 2))
                        nc.scalar.activation(sg[:], gr[:], ACT.Silu).then_inc(s_silu, 1)
                    weight_hi(4 * j + t + 1, (t + 1) % 2, 32 * j + 16 * ((t + 1) // 2 + 1))
                act.wait_ge(s_ev, evacuated(4 * j + 3))
                copy(y_h[:, j, :], cv[:]).then_inc(s_yhi, 1)

            def stream(i, t, last):
                n0, m = OUT0 + t, 2 * i + t
                if last and t == 1:
                    act.wait_ge(s_wg, 1)
                weight_hi(2 * i + n0 + 1, (t + 1) % 2, 16 * i + 16 * ((n0 + 1) // 2 + 1))
                act.wait_ge(s_acc, m + 1)
                act.wait_ge(s_ev, evacuated(2 * i + n0))
                copy(act_h[:, m, :], xt[:, m, :]).then_inc(s_x2hi, 1)
                nc.scalar.activation(sq[t][:], xt[:, m, :], ACT.Square).then_inc(s_x2sq, 1)

            with act.Fori(0, KC // 2 - 1) as i:
                for t in range(2):
                    stream(i, t, False)
            for t in range(2):
                stream(KC // 2 - 1, t, True)

            def b_weight(e):
                n = B0 + e
                act.wait_ge(s_wg, e + 1)
                weight_hi(n, n % 2, 16 * (n // 2 + 1) + (32 if e == N_B - 1 else 0))

            b_weight(1)
            b_weight(2)
            act.wait_ge(s_rt, 2)
            copy(r_bc[:], ps[:, 3]).then_inc(s_rsb, 1)
            squares = [acc, sq[0], acc_q, sq[1], sq[0]]
            act.wait_ge(s_ss, 1)
            for e in range(3, N_B):
                b_weight(e)
                if e - 3 < CKV + CQ:
                    z = e - 3
                    act.wait_ge(s_ev, evacuated(B0 + z))
                    if z == 4:
                        act.wait_ge(s_cacc, 1)
                    nc.scalar.activation(squares[z][:], zc[:, z, :], ACT.Square).then_inc(s_csq, 1)
                if e == 6:
                    act.wait_ge(s_tab, 8)
                    nc.scalar.activation(tq[1][0:2 * ROPE, :], angle[0:2 * ROPE, :], ACT.Sin
                                         ).then_inc(s_sin, 1)
                if e >= 8:
                    z = e - 8
                    act.wait_ge(s_ev, evacuated(B0 + 5 + z))
                    nc.scalar.activation(gate[:, z, :], gate[:, z, :], ACT.Silu).then_inc(s_gsilu, 1)
            for z in (2, 3):
                act.wait_ge(s_ev, evacuated(B0 + 5 + z))
                nc.scalar.activation(gate[:, z, :], gate[:, z, :], ACT.Silu).then_inc(s_gsilu, 1)

            def staged(t):
                act.wait_ge(s_x2t, t + 1)
                if t >= 2:
                    act.wait_ge(s_x2w[t % 2], 16 * (t // 2))
                copy(x2_st[t % 2][:], ps[:, t % 2]).then_inc(s_x2s, 1)

            def pair_weights(c):
                act.wait_ge(s_u, 12 * 16 * (c + 1))
                copy(u_h[:], u_raw[:]).then_inc(s_uhi, 1)

            act.wait_ge(s_tile, tile_done(LAST))
            staged(0)
            act.wait_ge(s_cn, 1)
            copy(ckv_h[:, 0, :], zc[:, 0, :]).then_inc(s_chi, 1)
            act.wait_ge(s_cn, 2)
            copy(ckv_h[:, 1, :], zc[:, 1, :]).then_inc(s_chi, 1)
            act.wait_ge(s_krp, 1)
            copy(k_h[0][NOPE:P, :], ps[NOPE:P, 1]).then_inc(s_krhi, 1)
            copy(k_h[1][0:NOPE, :], ps[0:NOPE, 1]).then_inc(s_krhi, 1)
            for k in range(CQ):
                act.wait_ge(s_cn, CKV + k + 1)
                if k == 0:
                    act.wait_ge(s_rt, 4)
                copy(cq_h[:, k, :], zc[:, CKV + k, :]).then_inc(s_chi, 1)
            pair_weights(0)
            for t in range(1, TB):
                staged(t)

            def proj_evac(name, c, last=False):
                if name not in BY_ACT:
                    return
                half = int(name[-1])
                bank = (7, 6, 5, 4)[PROJ.index(name) % 4] if c is None else 7
                src = ps[:, bank // 2, bank % 2 * HALF:(bank % 2 + 1) * HALF]
                act.wait_ge(s_pj, pj_count(c, name))
                if c is not None and half == 0:
                    if name == "k0":
                        act.wait_ge(s_splo, 6 * c + 5)
                    if name == "vt0":
                        act.wait_ge(s_splo, 6 * c + 6)
                if name[:2] == "vt":
                    dst = v_f[:, 4 * half:4 * half + 4, :].rearrange("p a b -> p (a b)")
                else:
                    dst = (k_f if name[0] == "k" else v_t)[:, half * HALF:(half + 1) * HALF]
                copy(dst, src).then_inc(s_pja, 1)

            def split_hi(c, what):
                odd = 1 if what[1] == "o" else 0
                rows = slice(NOPE, P) if odd else slice(0, NOPE)
                if what[0] == "q":
                    act.wait_ge(s_pjv, dve_count(c, "qo1" if odd else "qe1"))
                    op = copy(q_h[odd][:], q_f[odd][:])
                elif what[0] == "k":
                    act.wait_ge(s_pja, act_count(c, "k1"))
                    op = copy(k_h[odd][rows, :], k_f[rows, :])
                else:
                    act.wait_ge(s_pja, act_count(c, "vt1"))
                    op = copy(vv[odd][:, :, 0:VH], v_f[:, :, odd * VH:(odd + 1) * VH])
                op.then_inc(s_sphi, 1)

            for name in PROJ:
                proj_evac(name, None)
                if name == "qe1":
                    split_hi(None, "qe")
                    split_hi(None, "ke")
                if name == "vt1":
                    split_hi(None, "ve")
            split_hi(None, "qo")
            split_hi(None, "ko")
            split_hi(None, "vo")

            def exps(number, c, h, g, q):
                width = (g + 1) * 2 * P
                act.wait_ge(s_mx, 16 * c + (number + 1))
                slot = (2 * g + q) % 4
                nc.scalar.activation(prob[q][:, 0:width], ps[:, q, 0:width], ACT.Exp,
                                     bias=smaxn[:, slot:slot + 1], scale=SCALE,
                                     accum_out=rsum[:, h, 2 * g + q:2 * g + q + 1]).then_inc(s_exp, 1)

            exps(0, 0, 0, 0, 0)
            exps(1, 0, 0, 0, 1)
            for w in s_x2w:
                act.wait_ge(w, 16 * TB // 2)

            def attention(c, last):
                for step, (h, g) in enumerate(STEPS):
                    for i in range(g + 1):
                        n = t_before(step) + i
                        act.wait_ge(s_t, 20 * c + (n + 1))
                        copy(pt_h[:, 2 * i:2 * i + 2, :].rearrange("p a b -> p (a b)"),
                             ps[:, 2, n % 2 * HALF:(n % 2 + 1) * HALF]).then_inc(s_th, 1)
                    nxt = next_scores(step, last)
                    if nxt is not None:
                        nh, ng, number = nxt
                        act.wait_ge(s_t, 20 * c + (t_before(step) + g + 1))
                        if number == 16:
                            act.wait_ge(s_rr, c + 1)
                        exps(number, c, nh, ng, 0)
                        exps(number + 1, c, nh, ng, 1)
                    before, after = units_of(step, last)
                    for name in before:
                        proj_evac(name, c)
                    act.wait_ge(s_pv, 8 * c + (step + 1))
                    copy(o_lo[:], ps[VH:P, 3, 0:2 * P]).then_inc(s_om, 1)
                    for name in after:
                        proj_evac(name, c)
                    if not last:
                        if step == 0:
                            act.wait_ge(s_u, 192 * c + 384)
                            act.wait_ge(s_pj, 12 * c + 10)
                            copy(u_h[:], u_raw[:]).then_inc(s_uhi, 1)
                        if step == 3:
                            act.wait_ge(s_s, 16 * c + 8)
                            split_hi(c, "qe")
                            split_hi(c, "ke")
                        if step == 5:
                            split_hi(c, "ve")
                        if step == 7:
                            act.wait_ge(s_s, 16 * c + 16)
                            split_hi(c, "qo")
                            split_hi(c, "ko")
                            split_hi(c, "vo")
                    elif step < 4:
                        act.wait_ge(s_wb[step % 2], 16 * (step // 2 + 1))
                        copy(wb_h[:, step, :], wb_raw[step % 2][:]).then_inc(s_wbh, 1)
                    elif step == 6:
                        act.wait_ge(s_s, 16 * PAIRS)
                        for k in range(PAIRS - 1):
                            act.wait_ge(s_og, k + 1)
                            copy(og_h[:, k, :], og[:, k, :]).then_inc(s_ogh, 1)

            with act.Fori(0, PAIRS - 1) as c:
                attention(c, False)
            attention(PAIRS - 1, True)
            act.wait_ge(s_og, PAIRS)
            copy(og_h[:, PAIRS - 1, :], og[:, PAIRS - 1, :]).then_inc(s_ogh, 1)
            for t in range(TB):
                act.wait_ge(s_x3, t + 1)
                if t >= 1:
                    act.wait_ge(s_x3q, t)
                nc.scalar.activation(x3_sq[:], x3[t % 2][:], ACT.Square,
                                     accum_out=ssq[:, t:t + 1]).then_inc(s_x3q, 1)

        @block.gpsimd
        def _(pool):
            def rsqrt(first, n, waited):
                pool.wait_ge(s_ms, waited)
                nc.gpsimd.tensor_tensor(rms[:, first:first + n], msq[:, first:first + n],
                                        cst[:, C_POW:C_POW + 1].broadcast_to([P, n]),
                                        ALU.pow).then_inc(s_pow, 1)

            pool.wait_ge(s_const, 16 * CONSTS)
            rsqrt(0, TB, 1)
            rsqrt(0, TB, 2)
            rsqrt(0, 2 * TB, 4)

            def split_lo(c, what, number):
                odd = 1 if what[1] == "o" else 0
                rows = slice(NOPE, P) if odd else slice(0, NOPE)
                pool.wait_ge(s_sphi, number + 1 if c is None else 6 * c + (6 + number + 1))
                if c is not None or number > 0:
                    pool.wait_ge(s_splo, number if c is None else 6 * c + (6 + number))
                if c is not None and what == "qo":
                    pool.wait_ge(s_rsw, c + 1)
                if what[0] == "q":
                    dst, src, hi = q_l[odd][:], q_f[odd][:], q_h[odd][:]
                elif what[0] == "k":
                    dst, src, hi = k_l[odd][rows, :], k_f[rows, :], k_h[odd][rows, :]
                else:
                    dst, src = vv[odd][:, :, VH:2 * VH], v_f[:, :, odd * VH:(odd + 1) * VH]
                    hi = vv[odd][:, :, 0:VH]
                nc.gpsimd.tensor_tensor(dst, src, hi.bitcast(F32), ALU.subtract).then_inc(s_splo, 1)

            for number, what in enumerate(("qe", "ke", "ve", "qo", "ko", "vo")):
                split_lo(None, what, number)

            def widen(c, done):
                pool.wait_ge(s_rr, c + 1)
                pool.wait_ge(s_splo, done)
                wide = [P, TB, 2, VH]
                nc.gpsimd.tensor_tensor(
                    rs_wide[:], rrec[:].rearrange("p h t -> p t h").unsqueeze(3).broadcast_to(wide),
                    ones.unsqueeze(2).unsqueeze(3).broadcast_to(wide), ALU.mult).then_inc(s_rsw, 1)

            with pool.Fori(0, PAIRS - 1) as c:
                split_lo(c, "qe", 0)
                split_lo(c, "ke", 1)
                split_lo(c, "ve", 2)
                widen(c, 6 * c + 9)
                split_lo(c, "qo", 3)
                split_lo(c, "ko", 4)
                split_lo(c, "vo", 5)
            for k in range(GC):
                pool.wait_ge(s_wbh, k + 1)
                nc.gpsimd.tensor_tensor(wb_l[:, k, :], wb_raw[k % 2][:], wb_h[:, k, :].bitcast(F32),
                                        ALU.subtract).then_inc(s_wbl, 1)
            widen(PAIRS - 1, 6 * PAIRS)
            for k in range(PAIRS - 1):
                pool.wait_ge(s_ogh, k + 1)
                nc.gpsimd.tensor_tensor(og_l[:, k, :], og[:, k, :], og_h[:, k, :].bitcast(F32),
                                        ALU.subtract).then_inc(s_ogl, 1)
            for t in range(TB):
                pool.wait_ge(s_fms, t + 1)
                nc.gpsimd.tensor_tensor(rms[:, t:t + 1], msq[:, t:t + 1], cst[:, C_POW:C_POW + 1],
                                        ALU.pow).then_inc(s_fr, 1)

        @block.vector
        def _(dve):
            tt, ts, stt = nc.vector.tensor_tensor, nc.vector.tensor_scalar, nc.vector.scalar_tensor_tensor

            def weight_lo(n, slot):
                dve.wait_ge(s_whi, n + 1)
                tt(w_l[:, slot], raw[:, slot], w_h[:, slot].bitcast(F32), ALU.subtract
                   ).then_inc(s_wlo, 1)

            def weight_gain(e):
                n = B0 + e
                dve.wait_ge(s_raw[n % 2], 16 * (n // 2 + 1) + (32 if e == N_B - 1 else 0))
                gain = b_tiles[e][2][:].unsqueeze(2).broadcast_to([P, KC, P])
                tt(raw[:, n % 2], raw[:, n % 2], gain, ALU.mult).then_inc(s_wg, 1)

            def mean_square(src, first, n, width):
                ts(msq[:, first:first + n], src, 1.0 / width, EPS, ALU.mult, ALU.add).then_inc(s_ms, 1)

            def widen(wide, first, waited):
                dve.wait_ge(s_pow, waited)
                nc.vector.tensor_copy(wide[:], rms[:, first:first + TB].unsqueeze(2)
                                      .broadcast_to([P, TB, P])).then_inc(s_rw, 1)

            dve.sem_inc(s_wlo, 2)
            dve.sem_inc(s_ev, 3)
            dve.sem_inc(s_tl, 2)
            dve.sem_inc(s_o, 1)
            nc.vector.memset(v[:, 0:CONV_WIDTH - 1], 0.0).then_inc(s_init, 1)
            dve.wait_ge(s_const, 16 * CONSTS)
            nc.vector.tensor_copy(identb[:], ident).then_inc(s_init, 1)
            nc.vector.tensor_copy(maskb[:].rearrange("p a b -> p (a b)"), cst[:, C_MASK:C_END]
                                  ).then_inc(s_init, 1)
            for u in range(2 * KC):
                half, k = u // KC, u % KC
                cols = slice(half * HALF, (half + 1) * HALF)
                bank = ps[:, 2 + u % 4 // 2, u % 2 * HALF:(u % 2 + 1) * HALF]
                dve.wait_ge(s_xhi, u + 1)
                nc.vector.tensor_copy(xt[:, k, cols], bank).then_inc(s_xcp, 1)
                stt(act_l[:, k, cols], bank, g_a[:, k:k + 1], act_h[:, k, cols].bitcast(F32),
                    ALU.mult, ALU.subtract).then_inc(s_xlo, 1)
                if u == 12:
                    dve.wait_ge(s_xsq, TB)
                    mean_square(ssq[:, 0:TB], 0, TB, D)
            widen(r_wide, 0, 1)
            weight_lo(0, 0)
            dve.wait_ge(s_rsb, 1)
            tt(r2_bc[:], r_bc[:], r_bc[:], ALU.mult).then_inc(s_ev, 1)

            with dve.Fori(0, KC) as j:
                weight_lo(4 * j + 1, 1)
                dve.wait_ge(s_tile, tile_done(4 * j))
                dve.wait_ge(s_ev, evacuated(4 * j - 1))
                tt(cr[:], ps[:, 0], r2_bc[:], ALU.mult).then_inc(s_ev, 1)
                weight_lo(4 * j + 2, 0)
                dve.wait_ge(s_tile, tile_done(4 * j + 1))
                dve.wait_ge(s_ev, evacuated(4 * j))
                tt(v[:, 2:2 + S], ps[:, 1], cr[:], ALU.mult).then_inc(s_ev, 1)
                dve.wait_ge(s_ev, evacuated(4 * j + 1))
                ts(cv[:], v[:, 0:S], conv_w[:, 0, bass.ds(j, 1)], None, ALU.mult).then_inc(s_cv, 1)
                for w in range(1, CONV_WIDTH):
                    dve.wait_ge(s_cv, 5 * j + w)
                    stt(cv[:], v[:, w:w + S], conv_w[:, w, bass.ds(j, 1)], cv[:], ALU.mult, ALU.add
                        ).then_inc(s_cv, 1)
                weight_lo(4 * j + 3, 1)
                dve.wait_ge(s_tile, tile_done(4 * j + 2))
                tt(gr[:], ps[:, 2], r_bc[:], ALU.mult).then_inc(s_ev, 1)
                dve.wait_ge(s_cv, 5 * j + 3)
                tt(cv[:], cv[:], r_bc[:], ALU.mult).then_inc(s_cv, 1)
                weight_lo(4 * j + 4, 0)
                dve.wait_ge(s_silu, j + 1)
                dve.wait_ge(s_cv, 5 * j + 4)
                tt(cv[:], cv[:], sg[:], ALU.mult).then_inc(s_cv, 1)
                dve.wait_ge(s_tile, tile_done(4 * j + 3))
                dve.wait_ge(s_cv, 5 * j + 5)
                tt(cv[:], cv[:], ps[:, 3], ALU.mult).then_inc(s_ev, 1)
                dve.wait_ge(s_yhi, j + 1)
                tt(y_l[:, j, :], cv[:], y_h[:, j, :].bitcast(F32), ALU.subtract).then_inc(s_ylo, 1)

            nc.vector.memset(acc[:], 0.0).then_inc(s_acc, 2)

            def stream(i, t, last):
                n0, m = OUT0 + t, 2 * i + t
                if last and t == 1:
                    weight_gain(0)
                weight_lo(2 * i + n0 + 1, (t + 1) % 2)
                dve.wait_ge(s_tile, tile_done(2 * i + n0))
                tt(xt[:, m, :], xt[:, m, :], ps[:, t], ALU.add).then_inc(s_ev, 1)
                dve.wait_ge(s_x2hi, m + 1)
                tt(act_l[:, m, :], xt[:, m, :], act_h[:, m, :].bitcast(F32), ALU.subtract
                   ).then_inc(s_x2lo, 1)
                dve.wait_ge(s_x2sq, m + 1)
                dve.wait_ge(s_acc, m + 2)
                tt(acc[:], acc[:], sq[t][:], ALU.add).then_inc(s_acc, 1)

            with dve.Fori(0, KC // 2 - 1) as i:
                for t in range(2):
                    stream(i, t, False)
            for t in range(2):
                stream(KC // 2 - 1, t, True)

            weight_gain(1)
            weight_lo(B0 + 1, 1)
            dve.wait_ge(s_ss, 1)
            mean_square(ps[:, 3, 0:TB], 0, TB, D)
            widen(r_wide, 0, 2)
            weight_gain(2)
            weight_lo(B0 + 2, 0)
            dve.wait_ge(s_rsb, 2)

            def evacuate(e):
                n, pair = B0 + e, b_tiles[e][3]
                dve.wait_ge(s_tile, tile_done(n))
                if e < CKV + CQ:
                    tt(zc[:, e, :], ps[:, pair], r_bc[:], ALU.mult).then_inc(s_ev, 1)
                elif e < N_B - 1:
                    tt(gate[:, e - CKV - CQ, :], ps[:, pair], r_bc[:], ALU.mult).then_inc(s_ev, 1)
                else:
                    tt(zk[:], ps[0:2 * ROPE, pair], r_bc[0:2 * ROPE, :], ALU.mult).then_inc(s_ev, 1)

            def sum_squares(into, frm, squares_done):
                dve.wait_ge(s_csq, squares_done)
                if squares_done == 5:
                    dve.wait_ge(s_cacc, 2)
                tt(into[:], into[:], frm[:], ALU.add).then_inc(s_cacc, 1)

            def table_step(op):
                op.then_inc(s_tab, 1)
                table[0] += 1
                dve.wait_ge(s_tab, table[0])

            def tables():
                rows = slice(0, 2 * ROPE)
                freq = cst[rows, C_FREQ:C_FREQ + 1]
                dve.wait_ge(s_pos, 16)
                table_step(nc.vector.tensor_copy(pos_f[rows, :], pos_i[rows, :]))
                table_step(ts(pos_f[rows, :], pos_f[rows, :], freq, None, ALU.mult))
                table_step(ts(turns[rows, :], pos_f[rows, :], 1 / (2 * np.pi),
                              cst[rows, C_TURN:C_TURN + 1], ALU.mult, ALU.add))
                table_step(ts(turns[rows, :], turns[rows, :], ROUND, ROUND, ALU.add, ALU.subtract))
                for i, part in enumerate((TWO_PI_A, TWO_PI_B, TWO_PI_C)):
                    src = pos_f if i == 0 else angle
                    table_step(stt(angle[rows, :], turns[rows, :], -part, src[rows, :],
                                   ALU.mult, ALU.add))
                table_step(ts(angle[rows, :], angle[rows, :], cst[rows, C_PHASE:C_PHASE + 1], PI_IN,
                              ALU.add, ALU.min))

            table = [0]
            for e in range(3, N_B):
                weight_gain(e)
                weight_lo(B0 + e, (B0 + e) % 2)
                evacuate(e - 3)
                if e == 3:
                    tables()
                if e == 5:
                    sum_squares(acc, sq[0], 2)
                if e == 7:
                    dve.wait_ge(s_sin, 1)
                    nc.vector.tensor_copy(tq[0][NOPE:P, :], tq[1][0:2 * ROPE, :]).then_inc(s_tab, 1)
                    nc.vector.memset(tq[0][0:NOPE, :], 1.0).then_inc(s_tab, 1)
                    nc.vector.memset(tq[1][NOPE:P, :], 1.0).then_inc(s_tab, 1)
                    sum_squares(acc_q, sq[1], 4)
                if e == 8:
                    sum_squares(acc_q, sq[0], 5)
            evacuate(7)
            evacuate(8)
            dve.wait_ge(s_ss, 2)
            mean_square(ps[:, 3, 0:TB], 0, TB, KV_RANK)
            mean_square(ps[:, 3, TB:2 * TB], TB, TB, Q_RANK)
            widen(rk_wide, 0, 3)
            widen(rq_wide, TB, 3)
            evacuate(9)
            dve.wait_ge(s_ev, evacuated(LAST))
            dve.wait_ge(s_tab, table[0] + 3)
            tt(zk[:], zk[:], tq[1][0:2 * ROPE, :], ALU.mult).then_inc(s_kr, 1)
            dve.wait_ge(s_rt, 3)
            for k in range(CKV):
                stt(zc[:, k, :], zc[:, k, :], g_ckv[:, k:k + 1], ps[:, 3], ALU.mult, ALU.mult
                    ).then_inc(s_cn, 1)
            for k in range(CKV):
                dve.wait_ge(s_chi, k + 1)
                tt(ckv_l[:, k, :], zc[:, k, :], ckv_h[:, k, :].bitcast(F32), ALU.subtract
                   ).then_inc(s_clo, 1)
            dve.wait_ge(s_rt, 4)
            for k in range(CQ):
                stt(zc[:, CKV + k, :], zc[:, CKV + k, :], g_q[:, k:k + 1], ps[:, 2], ALU.mult, ALU.mult
                    ).then_inc(s_cn, 1)
            dve.wait_ge(s_krhi, 2)
            tt(k_l[0][NOPE:P, :], ps[NOPE:P, 1], k_h[0][NOPE:P, :].bitcast(F32), ALU.subtract
               ).then_inc(s_krlo, 1)
            tt(k_l[1][0:NOPE, :], ps[0:NOPE, 1], k_h[1][0:NOPE, :].bitcast(F32), ALU.subtract
               ).then_inc(s_krlo, 1)
            for k in range(CQ):
                dve.wait_ge(s_chi, CKV + k + 1)
                tt(cq_l[k][:], zc[:, CKV + k, :], cq_h[:, k, :].bitcast(F32), ALU.subtract
                   ).then_inc(s_clo, 1)
            dve.wait_ge(s_uhi, 1)
            tt(u_l[:], u_raw[:], u_h[:].bitcast(F32), ALU.subtract).then_inc(s_ulo, 1)

            def proj_evac(name, c, last=False):
                if name not in BY_DVE:
                    return
                half = int(name[-1])
                cols = slice(half * HALF, (half + 1) * HALF)
                bank = (7, 6, 5, 4)[PROJ.index(name) % 4] if c is None else 7
                src = ps[:, bank // 2, bank % 2 * HALF:(bank % 2 + 1) * HALF]
                dve.wait_ge(s_pj, pj_count_last(name) if last else pj_count(c, name))
                if name[0] == "r":
                    tt(gs[:, cols], src, gate[:, c, cols], ALU.mult).then_inc(s_pjv, 1)
                    return
                odd = 1 if name[1] == "o" else 0
                if c is not None and half == 0:
                    dve.wait_ge(s_splo, split_done(c, "qo" if odd else "qe"))
                tt(q_f[odd][:, cols], src, tq[odd][:, cols], ALU.mult).then_inc(s_pjv, 1)

            for name in PROJ:
                proj_evac(name, None)

            def row_max(number, c, g, q):
                slot = (2 * g + q) % 4
                dve.wait_ge(s_s, 16 * c + (number + 1))
                nc.vector.reduce_max(smax[:, slot:slot + 1], ps[:, q, 0:(g + 1) * 2 * P], AX_X
                                     ).then_inc(s_mxr, 1)
                dve.wait_ge(s_mxr, 16 * c + (number + 1))
                ts(smaxn[:, slot:slot + 1], smax[:, slot:slot + 1], -SCALE, None, ALU.mult
                   ).then_inc(s_mx, 1)

            row_max(0, 0, 0, 0)
            row_max(1, 0, 0, 1)

            def attention(c, last):
                for step, (h, g) in enumerate(STEPS):
                    nxt = next_scores(step, last)

                    def lo(i):
                        n = t_before(step) + i
                        dve.wait_ge(s_th, 20 * c + (n + 1))
                        dst = pt_l[:, 2 * i:2 * i + 2, :].rearrange("p a b -> p (a b)")
                        hi = pt_h[:, 2 * i:2 * i + 2, :].rearrange("p a b -> p (a b)")
                        tt(dst, ps[:, 2, n % 2 * HALF:(n % 2 + 1) * HALF], hi.bitcast(F32),
                           ALU.subtract).then_inc(s_tl, 1)

                    if step == 7:
                        dve.wait_ge(s_exp, 16 * c + 16)
                        nc.vector.reciprocal(rrec[:], rsum[:]).then_inc(s_rr, 1)
                    for i in range(min(2, g + 1)):
                        lo(i)
                    if nxt is not None:
                        row_max(nxt[2], c, nxt[1], 0)
                    for i in range(2, g + 1):
                        lo(i)
                    if nxt is not None:
                        row_max(nxt[2] + 1, c, nxt[1], 1)
                    before, after = units_of(step, last)
                    for name in before:
                        proj_evac(name, c, last)
                    dve.wait_ge(s_om, 8 * c + (step + 1))
                    tt(o_t[h * VH:(h + 1) * VH, g * 2 * P:(g + 1) * 2 * P], ps[0:VH, 3, 0:2 * P],
                       o_lo[:], ALU.add).then_inc(s_o, 1)
                    for name in after:
                        proj_evac(name, c, last)
                    if step == 0 and not last:
                        dve.wait_ge(s_uhi, c + 2)
                        tt(u_l[:], u_raw[:], u_h[:].bitcast(F32), ALU.subtract).then_inc(s_ulo, 1)
                dve.wait_ge(s_pjv, dve_count(c, "r1", last))
                dve.wait_ge(s_o, 8 * c + 9)
                tt(og[:, c, :], o_t[:], gs[:], ALU.mult).then_inc(s_og, 1)

            dve.wait_ge(s_gsilu, GC)
            with dve.Fori(0, PAIRS - 1) as c:
                attention(c, False)
            attention(PAIRS - 1, True)
            dve.wait_ge(s_ogh, PAIRS)
            tt(og_l[:, PAIRS - 1, :], og[:, PAIRS - 1, :], og_h[:, PAIRS - 1, :].bitcast(F32),
               ALU.subtract).then_inc(s_ogl, 1)

            def normed(t):
                dve.wait_ge(s_fr, t + 1)
                if t == 0:
                    dve.wait_ge(s_gf, 16)
                if t >= 2:
                    dve.wait_ge(s_out[t % 2], 16 * (t // 2))
                stt(y_out[t % 2][:], x3[t % 2][:], rms[:, t:t + 1], g_f[:], ALU.mult, ALU.mult
                    ).then_inc(s_y, 1)

            def mean(t):
                dve.wait_ge(s_x3q, t + 1)
                ts(msq[:, t:t + 1], ssq[:, t:t + 1], 1.0 / D, EPS, ALU.mult, ALU.add
                   ).then_inc(s_fms, 1)

            for t in range(TB):
                dve.wait_ge(s_fin, t + 1)
                dve.wait_ge(s_x2r[t % 2], 16 * (t // 2 + 1))
                if t >= 2:
                    dve.wait_ge(s_y, t - 1)
                tt(x3[t % 2][:], x2_r[t % 2][:], ps[:, t % 2], ALU.add).then_inc(s_x3, 1)
                if t >= 1:
                    normed(t - 1)
                mean(t)
            normed(TB - 1)


_INS = ["x", "positions", "a_norm", "a_w_in", "a_conv", "a_w_out", "kv_norm", "w_dkv", "ckv_norm",
        "w_ukv", "b_norm", "b_w_in", "b_q_norm", "b_w_uq", "b_w_out", "final_norm"]


def kernel(**inputs):
    import concourse.bacc as bacc
    from concourse.bass_utils import run_bass_kernel_spmd

    nc = bacc.Bacc("TRN2", target_bir_lowering=False, num_devices=1, dynamic_dma_scratch_size=1024)
    given = {name: np.ascontiguousarray(inputs[name]) for name in _INS}
    given["const"] = constants()
    arrays, args = {}, []
    for name, a in given.items():
        arrays[f"in_{name}"] = a
        args.append(nc.dram_tensor(f"in_{name}", a.shape, mybir.dt.from_np(a.dtype),
                                   kind="ExternalInput").ap())
    args.append(nc.dram_tensor("out", (1, S, D), F32, kind="ExternalOutput").ap())
    trunk(nc, *args)
    r = run_bass_kernel_spmd(nc, [arrays], core_ids=[0])
    return r.results[0]["out"]
```

```python
from contextlib import ExitStack

import numpy as np

import concourse.bass as bass
from concourse import mybir

F32 = mybir.dt.float32
F32R = mybir.dt.float32r
BF16 = mybir.dt.bfloat16
I32 = mybir.dt.int32
ALU = mybir.AluOpType
ACT = mybir.ActivationFunctionType
AX_X = mybir.AxisListType.X

P = 128
S = 1024
D = 1024
KC = D // P
TB = S // P
HALF = 512
CONV_WIDTH = 3
HEADS = 8
PAIRS = HEADS // 2
NOPE, ROPE, VH = 64, 32, 64
RH = ROPE // 2
KV_RANK, Q_RANK = 256, 384
CKV, CQ = KV_RANK // P, Q_RANK // P
GC = HEADS * VH // P
SCALE = 1.0 / float(np.sqrt(np.float64(NOPE + ROPE)))
EPS = 1e-6
THETA = 10000.0
MASK = -3.0e38
ROUND = 1.5 * 2.0 ** 23
TWO_PI_A = 6.28125
TWO_PI_B = float(np.float32(2 * np.pi - TWO_PI_A))
TWO_PI_C = float(2 * np.pi - TWO_PI_A - np.float64(np.float32(2 * np.pi - TWO_PI_A)))
PI_IN = 3.1415925

C_ID, C_SEL, C_ONE, C_FREQ, C_TURN, C_PHASE, C_POW, C_MASK = 0, 128, 256, 257, 258, 259, 260, 261
C_END = C_MASK + 4 * P

G_OFF = [0, KC, 2 * KC, 3 * KC, 3 * KC + CKV, 3 * KC + CKV + CQ]
G_ROWS = G_OFF[-1] + CONV_WIDTH * KC


def constants():
    c = np.zeros((P, C_END), np.float32)
    c[:, C_ID:C_ID + P] = np.eye(P)
    for r in range(2 * ROPE):
        c[r, C_SEL:C_SEL + P] = [r % ROPE == m % ROPE for m in range(P)]
    c[:, C_ONE] = 1.0
    freq = np.float32(THETA) ** (-np.arange(0, ROPE, 2, dtype=np.float32) / np.float32(ROPE))
    for r in range(ROPE):
        c[r, C_FREQ] = freq[r % RH]
        c[r, C_PHASE] = np.pi / 2
        c[r, C_TURN] = 0.25
        c[ROPE + r, C_FREQ] = freq[r % RH] * (-1 if r < RH else 1)
    c[:, C_POW] = -0.5
    mask = np.zeros((P, 2, 2 * P), np.float32)
    above = np.triu(np.ones((P, P), bool), 1)
    mask[:, 0, 0:P][above] = MASK
    mask[:, 0, P:] = MASK
    mask[:, 1, P:][above] = MASK
    c[:, C_MASK:] = mask.reshape(P, 4 * P)
    return c


def trunk(nc, x, positions, a_norm, a_w_in, a_conv, a_w_out, kv_norm, w_dkv, ckv_norm, w_ukv,
          b_norm, b_w_in, b_q_norm, b_w_uq, b_w_out, final_norm, const, out):
    x_d = x.rearrange("a (t p) d -> p (a t) d", p=P)
    out_d = out.rearrange("a (t p) d -> p (a t) d", p=P)
    w_in_d = a_w_in.rearrange("a (k p) n -> p (a k) n", p=P)
    w_out_d = a_w_out.rearrange("a (k p) n -> p (a k) n", p=P)
    w_dkv_d = w_dkv.rearrange("(k p) n -> p k n", p=P)
    w_b_d = b_w_in.rearrange("a (k p) n -> p (a k) n", p=P)
    w_uq_d = b_w_uq.rearrange("a (k p) n -> p (a k) n", p=P)
    w_ukv_d = w_ukv.rearrange("(k p) n -> p k n", p=P)
    w_bo_d = b_w_out.rearrange("a (k p) n -> p (a k) n", p=P)
    x2_d = nc.dram_tensor("x2_scratch", [S, D], F32, kind="Internal").ap()
    x2_d = x2_d.rearrange("(t p) d -> p t d", p=P)

    with ExitStack() as ctx:
        def sem(name):
            return ctx.enter_context(nc.semaphore(name))

        base = (nc.sbuf_base + 31) // 32 * 32
        small = [base]

        def const_sb(name, shape, dt=F32):
            n = int(np.prod(shape[1:])) * (2 if dt == BF16 else 4)
            t = nc.alloc_sbuf_tensor_at(name, shape, dt, offset=small[0])
            small[0] += (n + 31) // 32 * 32
            return t

        cst = const_sb("cst", [P, C_END])
        maskb = const_sb("maskb", [P, 2, 2 * P], BF16)
        identb = const_sb("identb", [P, P], BF16)
        gt = const_sb("gt", [P, G_ROWS])
        g_a, g_kv, g_b, g_ckv, g_q = (gt[:, a:b] for a, b in zip(G_OFF, G_OFF[1:]))
        conv_w = gt[:, G_OFF[-1]:].rearrange("p (w k) -> p w k", w=CONV_WIDTH)
        ssq = const_sb("ssq", [P, 2 * TB])
        msq = const_sb("msq", [P, 2 * TB])
        rms = const_sb("rms", [P, 2 * TB])
        smax = const_sb("smax", [P, 4])
        smaxn = const_sb("smaxn", [P, 4])
        rsum = const_sb("rsum", [P, 2, TB])
        rrec = const_sb("rrec", [P, 2, TB])
        arena = small[0]
        K = 1024

        def at(name, kib, shape, dt=F32):
            return nc.alloc_sbuf_tensor_at(name, shape, dt, offset=arena + kib * K)

        act_h = at("act_h", 0, [P, KC, S], F32R)
        act_l = at("act_l", 32, [P, KC, S], F32R)
        xt = at("xt", 64, [P, KC, S])
        y_h = at("y_h", 96, [P, KC, S], F32R)
        y_l = at("y_l", 128, [P, KC, S], F32R)
        x_in = at("x_in", 96, [P, TB, D])
        junk = at("junk", 128, [P, TB, D])
        g_rows = at("g_rows", 205, [G_ROWS, P])
        raw = at("raw", 160, [P, 2, KC, P])
        w_h = at("w_h", 168, [P, 2, KC, P], F32R)
        w_l = at("w_l", 176, [P, 2, KC, P], F32R)
        r_bc = at("r_bc", 184, [P, S])
        r2_bc = at("r2_bc", 188, [P, S])
        cr = at("cr", 192, [P, S])
        v = at("v", 196, [P, S + CONV_WIDTH - 1])
        cv = at("cv", 201, [P, S])
        gr = at("gr", 205, [P, S])
        sg = at("sg", 209, [P, S])
        r_wide = at("r_wide", 209, [P, TB, P])
        sq = [at("sq0", 192, [P, S]), at("sq1", 201, [P, S])]
        acc = at("acc", 205, [P, S])
        gate = at("gate", 96, [P, GC, S])
        zc = at("zc", 112, [P, CKV + CQ, S])
        tq = [at("tq0", 132, [P, S]), at("tq1", 136, [P, S])]
        pos_i = at("pos_i", 140, [P, S], I32)
        pos_f = at("pos_f", 144, [P, S])
        turns = at("turns", 148, [P, S])
        angle = at("angle", 152, [P, S])
        acc_q = at("acc_q", 209, [P, S])
        rk_wide = at("rk_wide", 205, [P, TB, P])
        rq_wide = at("rq_wide", 209, [P, TB, P])
        zk = at("zk", 213, [2 * ROPE, S])
        ckv_h = at("ckv_h", 140, [P, CKV, S], F32R)
        ckv_l = at("ckv_l", 148, [P, CKV, S], F32R)
        cq_h = at("cq_h", 188, [P, CQ, S], F32R)
        cq_l = [at(f"cq_l{k}", o, [P, S], F32R) for k, o in enumerate((156, 205, 209))]
        x2_st = [at("x2_st0", 156, [P, D]), at("x2_st1", 188, [P, D])]
        q_h = [at("qe_h", 0, [P, S], F32R), at("qo_h", 8, [P, S], F32R)]
        q_l = [at("qe_l", 4, [P, S], F32R), at("qo_l", 12, [P, S], F32R)]
        k_h = [at("ke_h", 16, [P, S], F32R), at("ko_h", 24, [P, S], F32R)]
        k_l = [at("ke_l", 20, [P, S], F32R), at("ko_l", 28, [P, S], F32R)]
        pt_h = [at("pt_h0", 32, [P, TB, 2 * P], F32R), at("pt_h1", 80, [P, TB // 2, 2 * P], F32R)]
        pt_l = [at("pt_l0", 40, [P, TB, 2 * P], F32R), at("pt_l1", 182, [P, TB // 2, 2 * P], F32R)]
        prob = [at("prob0", 48, [P, S]), at("prob1", 52, [P, S])]
        vv = [at("v_e", 56, [P, TB, 2 * VH], F32R), at("v_o", 60, [P, TB, 2 * VH], F32R)]
        q_f = [at("q_fe", 160, [P, S]), at("q_fo", 164, [P, S])]
        k_f = at("k_f", 168, [P, S])
        v_t = at("v_t", 172, [P, S])
        v_f = at("v_f", 176, [P, TB, P])
        o_t = at("o_t", 84, [P, S])
        rs_wide = at("rs_wide", 88, [P, TB, 2, VH])
        gs = at("gs", 92, [P, S])
        og = at("og", 112, [P, GC, S])
        u_raw = at("u_raw", 64, [P, 10, P])
        u_h = at("u_h", 69, [P, 10, P], F32R)
        u_l = at("u_l", 74, [P, 10, P], F32R)
        o_lo = at("o_lo", 180, [VH, 2 * P])
        og_h = at("og_h", 0, [P, GC, S], F32R)
        og_l = at("og_l", 16, [P, GC, S], F32R)
        wb_raw = [at("wb_raw0", 205, [P, D]), at("wb_raw1", 209, [P, D])]
        wb_h = at("wb_h", 140, [P, GC, D], F32R)
        wb_l = at("wb_l", 64, [P, GC, D], F32R)
        g_f = at("g_f", 128, [P, D])
        x2_r = [at("x2_r0", 48, [P, D]), at("x2_r1", 52, [P, D])]
        x3 = [at("x3_0", 40, [P, D]), at("x3_1", 44, [P, D])]
        x3_sq = at("x3_sq", 56, [P, D])
        y_out = [at("y_out0", 32, [P, D]), at("y_out1", 36, [P, D])]

        ident = cst[:, C_ID:C_ID + P]
        ones = cst[:, C_ONE:C_ONE + 1]

        ps = ctx.enter_context(nc.psum_tensor("ps", [P, 4, 2 * HALF], F32))

        s_ident = sem("identity_in")
        s_ga = sem("a_norm_in")
        s_const = sem("const_in")
        s_gtp = sem("gains_transposed")
        s_gt = sem("gains_in_sbuf")
        s_x = [sem(f"x_in{t}") for t in range(TB)]
        s_raw = [sem("raw_in0"), sem("raw_in1")]
        s_pos = sem("pos_in")
        s_whi = sem("w_hi")
        s_wlo = sem("w_lo")
        s_wg = sem("w_gain")
        s_tile = sem("tile_done")
        s_ev = sem("ps_evacuated")
        s_xtp = sem("x_transposed")
        s_xhi = sem("x_hi")
        s_xlo = sem("x_lo")
        s_xsq = sem("x_squares")
        s_init = sem("dve_init")
        s_ms = sem("mean_square")
        s_pow = sem("rsqrt_done")
        s_rw = sem("r_widened")
        s_rt = sem("r_transposed")
        s_rsb = sem("r_in_sbuf")
        s_cv = sem("conv_step")
        s_silu = sem("silu_done")
        s_yhi = sem("y_hi")
        s_ylo = sem("y_lo")
        s_xr = sem("x_restored")
        s_x2hi = sem("x2_hi")
        s_x2lo = sem("x2_lo")
        s_x2sq = sem("x2_square")
        s_acc = sem("acc_step")
        s_ss = sem("ss_product")
        s_tab = sem("table_step")
        s_sin = sem("sin_done")
        s_csq = sem("c_square")
        s_cacc = sem("c_acc")
        s_gsilu = sem("gate_silu")
        s_cn = sem("c_normed")
        s_chi = sem("c_hi")
        s_clo = sem("c_lo")
        s_kr = sem("k_rope_step")
        s_krp = sem("k_rope_product")
        s_krhi = sem("k_rope_hi")
        s_krlo = sem("k_rope_lo")
        s_x2t = sem("x2_transposed")
        s_x2s = sem("x2_staged")
        s_x2w = [sem("x2_written0"), sem("x2_written1")]
        s_u = sem("u_in")
        s_uhi = sem("u_hi")
        s_ulo = sem("u_lo")
        s_pj = sem("proj_product")
        s_pja = sem("proj_evac_act")
        s_pjv = sem("proj_evac_dve")
        s_sphi = sem("split_hi")
        s_splo = sem("split_lo")
        s_s = sem("scores_done")
        s_mxr = sem("row_max")
        s_mx = sem("row_max_scaled")
        s_exp = sem("exp_done")
        s_t = sem("p_transposed")
        s_th = sem("pt_hi")
        s_tl = sem("pt_lo")
        s_pv = sem("pv_done")
        s_om = sem("o_low_moved")
        s_o = sem("o_added")
        s_rr = sem("rsum_inverted")
        s_rsw = sem("rsum_widened")
        s_og = sem("og_done")
        s_ogh = sem("og_hi")
        s_ogl = sem("og_lo")
        s_wb = [sem("wb_in0"), sem("wb_in1")]
        s_wbh = sem("wb_hi")
        s_wbl = sem("wb_lo")
        s_gf = sem("gf_in")
        s_x2r = [sem("x2_read0"), sem("x2_read1")]
        s_fin = sem("last_product")
        s_x3 = sem("x3_done")
        s_x3q = sem("x3_squared")
        s_fm = sem("final_ms_half")
        s_fms = sem("final_ms")
        s_fr = sem("final_rsqrt")
        s_y = sem("y_normed")
        s_out = [sem("out_written0"), sem("out_written1")]

        N_A, N_O = 4 * KC, KC
        OUT0, B0 = N_A, N_A + N_O
        b_tiles = [("dkv", c * P, g_kv) for c in range(CKV)] + [("rope", KV_RANK, g_kv)]
        b_tiles += [("b", c * P, g_b) for c in range(CQ + GC)]
        N_B = len(b_tiles)
        E_ROPE, E_Q, E_G = CKV, CKV + 1, CKV + 1 + CQ
        LAST = B0 + N_B - 1
        Z_TILES = [0, 1, E_Q, E_Q + 1, E_Q + 2]

        def fills(n):
            rope = B0 + E_ROPE
            return 16 * (n // 2 + 1) + (32 if n >= rope and n % 2 == rope % 2 else 0)

        def lo_done(n):
            return n + 3

        def tile_done(n):
            return n + 3

        def slot_free(n):
            return n + 1

        def evacuated(n):
            return n + 5

        CONSTS = 6

        block = ctx.enter_context(nc.Block())

        @block.sync
        def _(sp):
            def load_w_in(j, t, part):
                sp.dma_start(raw[:, t % 2], w_in_d[:, :, bass.ds(j * P + (part * D - P), P)]
                             ).then_inc(s_raw[t % 2], 16)

            def rows(n, source):
                return g_rows[G_OFF[n]:G_OFF[n] + source.shape[0], :], source

            sp.dma_start(cst[:, C_ID:C_ID + P], const[:, C_ID:C_ID + P]).then_inc(s_ident, 16)
            sp.dma_start(*rows(0, a_norm.rearrange("a (k p) -> (a k) p", p=P))).then_inc(s_ga, 16)
            load_w_in(1, 0, 1)
            for t in range(4):
                sp.dma_start(x_in[:, t, :], x_d[:, t, :]).then_inc(s_x[t], 16)
            load_w_in(1, 1, 2)
            for t in range(4, TB):
                sp.dma_start(x_in[:, t, :], x_d[:, t, :]).then_inc(s_x[t], 16)
            others = [rows(1, kv_norm.rearrange("(k p) -> k p", p=P)),
                      rows(2, b_norm.rearrange("a (k p) -> (a k) p", p=P)),
                      rows(3, ckv_norm.rearrange("(k p) -> k p", p=P)),
                      rows(4, b_q_norm.rearrange("a (k p) -> (a k) p", p=P)),
                      rows(5, a_conv.rearrange("a w (k p) -> (a w k) p", p=P)),
                      (cst[:, C_SEL:C_END], const[:, C_SEL:C_END])]
            assert len(others) == CONSTS
            for dst, src in others:
                sp.dma_start(dst, src).then_inc(s_const, 16)

            for t, part in ((2, 3), (3, 0)):
                sp.wait_ge(s_wlo, slot_free(t))
                load_w_in(1, t, part)
            with sp.Fori(2, KC + 1) as j:
                for t, part in enumerate((1, 2, 3, 0)):
                    sp.wait_ge(s_wlo, slot_free(4 * j + (t - 4)))
                    load_w_in(j, t, part)
            with sp.Fori(1, KC // 2 + 1) as i:
                for t in range(2):
                    sp.wait_ge(s_wlo, slot_free(2 * i + (OUT0 + t - 2)))
                    sp.dma_start(raw[:, t], w_out_d[:, :, bass.ds(i * 2 * P + (t - 2) * P, P)]
                                 ).then_inc(s_raw[t], 16)
            def load_b(e):
                kind, col, _ = b_tiles[e]
                n = B0 + e
                sp.wait_ge(s_wlo, slot_free(n))
                dst = raw[:, n % 2]
                if kind == "rope":
                    cols = [(0, col, ROPE), (ROPE, col + RH, RH), (ROPE + RH, col, RH)]
                    for to, frm, m in cols:
                        sp.dma_start(dst[:, :, to:to + m], w_dkv_d[:, :, frm:frm + m]
                                     ).then_inc(s_raw[n % 2], 16)
                else:
                    src = w_dkv_d if kind == "dkv" else w_b_d
                    sp.dma_start(dst, src[:, :, col:col + P]).then_inc(s_raw[n % 2], 16)

            def write_x2(t):
                sp.wait_ge(s_x2s, t + 1)
                sp.dma_start(x2_d[:, t, :], x2_st[t % 2][:]).then_inc(s_x2w[t % 2], 16)

            load_b(0)
            load_b(1)
            sp.wait_ge(s_tile, tile_done(B0 - 1))
            sp.dma_start(pos_i[:], positions[0:1, :].broadcast_to([P, S])).then_inc(s_pos, 16)
            for e in range(2, N_B):
                load_b(e)
                if e >= 6:
                    write_x2(2 * (e - 6))
                    write_x2(2 * (e - 6) + 1)

            def load_pair(c):
                per = NOPE + ROPE
                for odd, base_col in ((0, 0), (1, P // 2)):
                    rope = NOPE if odd == 0 else 0
                    parts = [(0 if odd == 0 else NOPE, 0, NOPE), (rope, NOPE, ROPE),
                             (rope + ROPE, NOPE + RH, RH), (rope + ROPE + RH, NOPE, RH)]
                    for to, frm, m in parts:
                        sp.dma_start(u_raw[:, odd * CQ:(odd + 1) * CQ, to:to + m],
                                     w_uq_d[:, :, bass.ds(c * 2 * per + odd * per + frm, m)]
                                     ).then_inc(s_u, 16)
                for what in range(2):
                    for odd in range(2):
                        sp.dma_start(u_raw[:, 2 * CQ + what * CKV:2 * CQ + (what + 1) * CKV,
                                           odd * NOPE:(odd + 1) * NOPE],
                                     w_ukv_d[:, :, bass.ds(c * 4 * NOPE + (2 * odd + what) * NOPE, NOPE)]
                                     ).then_inc(s_u, 16)

            load_pair(0)
            sp.wait_ge(s_clo, CKV + CQ)
            sp.dma_start(g_f[:], final_norm.rearrange("(a d) -> a d", a=1).broadcast_to([P, D])
                         ).then_inc(s_gf, 16)
            with sp.Fori(0, PAIRS - 1) as c:
                sp.wait_ge(s_ulo, c + 1)
                load_pair(c + 1)
            sp.wait_ge(s_pj, 10 + 12 * (PAIRS - 1))
            for k in range(GC):
                if k >= 2:
                    sp.wait_ge(s_wbl, k - 1)
                sp.dma_start(wb_raw[k % 2][:], w_bo_d[:, k, :]).then_inc(s_wb[k % 2], 16)
            for w in s_x2w:
                sp.wait_ge(w, 16 * TB // 2)
            sp.wait_ge(s_t, 20 * PAIRS)
            def write_out(t):
                sp.wait_ge(s_y, t + 1)
                sp.dma_start(out_d[:, t, :], y_out[t % 2][:]).then_inc(s_out[t % 2], 16)

            for t in range(TB):
                if t >= 2:
                    sp.wait_ge(s_x3, 2 * (t - 1))
                sp.dma_start(x2_r[t % 2][:], x2_d[:, t, :]).then_inc(s_x2r[t % 2], 16)
                if t >= 2:
                    write_out(t - 2)
            write_out(TB - 2)
            for half in range(2):
                cols = slice(half * HALF, (half + 1) * HALF)
                sp.wait_ge(s_y, TB + half)
                sp.dma_start(out_d[:, TB - 1, cols], y_out[(TB - 1) % 2][:, cols]
                             ).then_inc(s_out[(TB - 1) % 2], 16)
            sp.wait_ge(s_out[0], 16 * TB // 2)
            sp.wait_ge(s_out[1], 16 * (TB // 2 + 1))

        STEPS = [(h, g) for h in range(2) for g in (3, 0, 2, 1)]
        UNITS = {1: (["k0"], ["k1"]), 2: (["v0"], ["qe0"]), 3: ([], ["qe1"]), 4: (["v1"], ["qo0"]),
                 5: ([], ["vt0"]), 6: (["qo1"], ["vt1"]), 7: ([], ["r0", "r1"])}
        PROJ = [u for s in range(1, 7) for part in UNITS[s] for u in part]
        ORDER = PROJ + ["r0", "r1"]
        BY_ACT = ("k0", "k1", "v0", "v1", "vt0", "vt1")
        BY_DVE = ("qe0", "qe1", "qo0", "qo1", "r0", "r1")
        PRO_BANKS = (2, 3, 4, 5)

        def units_of(step, last):
            return UNITS.get(step, ([], [])) if not last or step == 7 else ([], [])

        def pj_count(c, name):
            if c is None:
                return PROJ.index(name) + 1
            return 12 * c + (10 + ORDER.index(name) + 1)

        def pj_count_last(name):
            return 10 + 12 * (PAIRS - 1) + ("r0", "r1").index(name) + 1

        def act_count(c, name):
            return BY_ACT.index(name) + 1 if c is None else 6 * c + (6 + BY_ACT.index(name) + 1)

        SPLITS = ("ke", "qe", "ve", "ko", "vo", "qo")

        def dve_count(c, name, last=False):
            if c is None:
                return BY_DVE.index(name) + 1
            if last:
                return 4 + 6 * (PAIRS - 1) + ("r0", "r1").index(name) + 1
            return 6 * c + (4 + BY_DVE.index(name) + 1)

        def next_scores(step, last):
            if step < 7:
                return STEPS[step + 1] + (2 * (step + 1),)
            return None if last else STEPS[0] + (16,)

        def t_before(step):
            return sum(g + 1 for _, g in STEPS[:step])

        def split_done(c, what):
            return 6 * c + (SPLITS.index(what) + 1)

        @block.tensor
        def _(pe):
            def products(dst, wh, wl, xh, xl, nk, before=None, halves=(0, 1), mid=None):
                for half in halves:
                    if half == 1 and mid is not None:
                        mid()
                    cols = slice(half * HALF, (half + 1) * HALF)
                    for k in range(nk):
                        if before is not None and half == halves[0]:
                            before(k)
                        for i, (w, z) in enumerate(((wh, xh), (wh, xl), (wl, xh))):
                            mm = nc.tensor.matmul(dst[:, cols], w(k), z(k, cols),
                                                  start=(k == 0 and i == 0),
                                                  stop=(k == nk - 1 and i == 2))
                return mm

            def tile(slot, pair, xh, xl, before=None, **more):
                return products(ps[:, pair], lambda k: w_h[:, slot, k, :], lambda k: w_l[:, slot, k, :],
                                lambda k, c: xh[:, k, c], lambda k, c: xl[:, k, c], KC, before,
                                **more)

            def widened(dst, wide):
                for t in range(TB):
                    mm = nc.tensor.transpose(dst[:, t * P:(t + 1) * P], wide[:, t, :], ident)
                return mm

            def square_sums(dst, of, first):
                for t in range(TB):
                    mm = nc.tensor.matmul(dst[:, first + t:first + t + 1], of[:, t * P:(t + 1) * P],
                                          ones, start=True, stop=True)
                return mm

            pe.sem_inc(s_tile, 2)
            pe.wait_ge(s_ident, 16)
            pe.wait_ge(s_ga, 16)
            nc.tensor.transpose(ps[:, 2, 0:KC], g_rows[0:KC, :], ident[0:KC, 0:KC]
                                ).then_inc(s_gtp, 1)
            pe.wait_ge(s_gt, 1)

            def x_units(first, last):
                for u in range(first, last):
                    half, k = u // KC, u % KC
                    bank = ps[:, 2 + u % 4 // 2, u % 2 * HALF:(u % 2 + 1) * HALF]
                    if u >= 4:
                        pe.wait_ge(s_xlo, u - 3)
                    for t in range(4):
                        if k == 0:
                            pe.wait_ge(s_x[4 * half + t], 16)
                        mm = nc.tensor.transpose(bank[:, t * P:(t + 1) * P],
                                                 x_in[:, 4 * half + t, k * P:(k + 1) * P], ident)
                    mm.then_inc(s_xtp, 1)

            def first_tiles(n, half):
                if half == 0:
                    pe.wait_ge(s_wlo, lo_done(n))
                def chunk_ready(k):
                    if (n, half) == (0, 0) and k < KC - 4:
                        x_units(k + 4, k + 5)
                    pe.wait_ge(s_xlo, half * KC + k + 1)

                return tile(n % 2, n, act_h, act_l, halves=(half,), before=chunk_ready)

            x_units(0, 4)
            first_tiles(0, 0)
            x_units(KC, KC + KC // 2)
            first_tiles(1, 0)
            x_units(KC + KC // 2, 2 * KC)
            first_tiles(0, 1).then_inc(s_tile, 1)
            pe.wait_ge(s_xlo, 2 * KC)
            pe.wait_ge(s_const, 16 * CONSTS)
            nc.tensor.transpose(ps[:, 2, 0:G_ROWS], g_rows[:], ident[0:G_ROWS, 0:G_ROWS]
                                ).then_inc(s_gtp, 1)
            pe.wait_ge(s_rw, 1)
            widened(ps[:, 3], r_wide).then_inc(s_rt, 1)
            first_tiles(1, 1).then_inc(s_tile, 1)
            pe.wait_ge(s_gt, 2)

            def a_tile(j, t):
                pe.wait_ge(s_wlo, lo_done(4 * j + t))
                pe.wait_ge(s_ev, slot_free(4 * j + t))
                tile(t % 2, t, act_h, act_l).then_inc(s_tile, 1)

            a_tile(0, 2)
            a_tile(0, 3)
            with pe.Fori(1, KC) as j:
                for t in range(4):
                    a_tile(j, t)

            def y_ready(k):
                if k in (0, KC - 1):
                    pe.wait_ge(s_ylo, KC - 1 if k == 0 else KC)

            with pe.Fori(0, KC // 2) as i:
                for t in range(2):
                    pe.wait_ge(s_wlo, lo_done(OUT0 + 2 * i + t))
                    pe.wait_ge(s_ev, evacuated(OUT0 + 2 * i + t - 2))
                    tile(t, t, y_h, y_l, y_ready).then_inc(s_tile, 1)

            def x2_ready(k):
                if k in (0, KC - 1):
                    pe.wait_ge(s_x2lo, KC - 1 if k == 0 else KC)

            def b_tile(e, mid=None):
                n = B0 + e
                pe.wait_ge(s_wlo, lo_done(n))
                if e != 2:
                    pe.wait_ge(s_ev, evacuated(n - (2 if e < 2 else 3)))
                tile(n % 2, e % 3, act_h, act_l, x2_ready if e == 0 else None, mid=mid
                     ).then_inc(s_tile, 1)

            def stream_back(t):
                if t >= 1:
                    pe.wait_ge(s_x2s, t)
                for k in range(KC):
                    mm = nc.tensor.transpose(ps[:, 3, k * P:(k + 1) * P],
                                             xt[:, k, t * P:(t + 1) * P], ident)
                mm.then_inc(s_x2t, 1)

            def q_rms():
                pe.wait_ge(s_cn, CKV)
                widened(ps[:, 3], rq_wide).then_inc(s_rt, 1)

            def rotated_key():
                pe.wait_ge(s_kr, 1)
                pe.wait_ge(s_cn, CKV + CQ)
                for half in range(2):
                    mm = nc.tensor.matmul(ps[:, 3, half * HALF:(half + 1) * HALF],
                                          cst[0:2 * ROPE, C_SEL:C_SEL + P],
                                          zk[:, half * HALF:(half + 1) * HALF], start=True, stop=True)
                mm.then_inc(s_krp, 1)

            b_tile(0)
            pe.wait_ge(s_acc, KC + 2)
            square_sums(ps[:, 3], acc, 0).then_inc(s_ss, 1)
            b_tile(1)
            pe.wait_ge(s_rw, 2)
            widened(ps[:, 3], r_wide).then_inc(s_rt, 1)
            b_tile(2)
            pe.wait_ge(s_rsb, 2)
            for i in range(TB // 2):
                stream_back(2 * i)
                b_tile(3 + i, mid=lambda: stream_back(2 * i + 1))
            pe.wait_ge(s_cacc, CKV - 1 + CQ - 1)
            pe.wait_ge(s_x2s, TB)
            square_sums(ps[:, 3], acc, 0)
            square_sums(ps[:, 3], acc_q, TB).then_inc(s_ss, 1)
            b_tile(7)
            pe.wait_ge(s_rw, 4)
            widened(ps[:, 3], rk_wide).then_inc(s_rt, 1)
            b_tile(8, mid=q_rms)
            b_tile(9, mid=rotated_key)

            def project(name, c, bank):
                dst = ps[:, bank // 2, bank % 2 * HALF:(bank % 2 + 1) * HALF]
                half = int(name[-1])
                cols = slice(half * HALF, (half + 1) * HALF)
                if name[0] == "r":
                    for t in range(4):
                        mm = nc.tensor.transpose(dst[:, t * P:(t + 1) * P],
                                                 rs_wide[:, 4 * half + t].rearrange("p a b -> p (a b)"),
                                                 ident)
                elif name[:2] == "vt":
                    for t in range(4):
                        kb = 4 * half + t
                        mm = nc.tensor.transpose(dst[:, t * P:(t + 1) * P],
                                                 v_t[:, kb * P:(kb + 1) * P], ident)
                else:
                    first, nk = {"qe": (0, CQ), "qo": (CQ, CQ), "k": (2 * CQ, CKV),
                                 "v": (2 * CQ + CKV, CKV)}[name[:-1]]
                    for k in range(nk):
                        xh = cq_h[:, k, cols] if nk == CQ else ckv_h[:, k, cols]
                        xl = cq_l[k][:, cols] if nk == CQ else ckv_l[:, k, cols]
                        passes = ((u_h, xh), (u_h, xl), (u_l, xh))
                        for i, (w, z) in enumerate(passes):
                            mm = nc.tensor.matmul(dst, w[:, first + k, :], z,
                                                  start=(k == 0 and i == 0),
                                                  stop=(k == nk - 1 and i == 2))
                mm.then_inc(s_pj, 1)

            def scores(h, g, q):
                width = (g + 1) * 2 * P
                qs = slice((2 * g + q) * P, (2 * g + q + 1) * P)
                for at0 in range(0, width, HALF):
                    w = min(HALF, width - at0)
                    dst = ps[:, q, at0:at0 + w]
                    last = at0 + w == width
                    for i, (a, b) in enumerate(((q_h, k_h), (q_h, k_l), (q_l, k_h))):
                        mm = nc.tensor.matmul(dst, a[h][:, qs], b[h][:, at0:at0 + w],
                                              start=(i == 0), stop=(i == 2 and not last))
                    if last:
                        mm = nc.tensor.matmul(ps[:, q, width - 2 * P:width], identb[:], maskb[:, q, :],
                                              start=False, stop=True)
                mm.then_inc(s_s, 1)

            pe.wait_ge(s_clo, CKV)
            pe.wait_ge(s_ulo, 1)
            pe.wait_ge(s_ev, evacuated(B0 + 8))
            for i, name in enumerate(PROJ):
                if i >= 4:
                    was = PROJ[i - 4]
                    if was in BY_ACT:
                        pe.wait_ge(s_pja, act_count(None, was))
                    else:
                        pe.wait_ge(s_pjv, dve_count(None, was))
                if name == "qe0":
                    pe.wait_ge(s_clo, CKV + CQ)
                if name == "vt0":
                    pe.wait_ge(s_pja, act_count(None, "v1"))
                project(name, None, PRO_BANKS[i % 4])
            pe.wait_ge(s_ev, evacuated(LAST))
            pe.wait_ge(s_splo, split_done(0, "qe"))
            pe.wait_ge(s_krlo, 2)
            scores(0, 3, 0)
            pe.wait_ge(s_pja, 6)
            pe.wait_ge(s_pjv, 4)
            scores(0, 3, 1)

            def attention(c, last):
                def turn(step, i):
                    n = t_before(step) + i
                    if i == 0:
                        pe.wait_ge(s_exp, 16 * c + (2 * step + 2))
                    pe.wait_ge(s_tl, 20 * c + (n + 1))
                    for j in range(2):
                        for q in range(2):
                            kb = 2 * i + j
                            mm = nc.tensor.transpose(
                                ps[:, 2, (n % 2) * HALF + (2 * j + q) * P:
                                   (n % 2) * HALF + (2 * j + q + 1) * P],
                                prob[q][:, kb * P:(kb + 1) * P], ident)
                    mm.then_inc(s_t, 1)

                def score(step, q):
                    nxt = next_scores(step, last)
                    if nxt is not None:
                        nh, ng, number = nxt
                        if q == 0 and step == 3:
                            pe.wait_ge(s_splo, split_done(c, "qo"))
                        if q == 0 and step == 7:
                            pe.wait_ge(s_splo, 6 + split_done(c, "qe"))
                        pe.wait_ge(s_exp, 16 * c + (number + q - 1))
                        scores(nh, ng, q)

                def times_v(step):
                    h, g = STEPS[step]
                    pe.wait_ge(s_o, 8 * c + (step + 1))
                    pe.wait_ge(s_splo, split_done(c, "vo" if h else "ve"))
                    for kb in range(2 * g + 2):
                        if kb % 2 == 0:
                            pe.wait_ge(s_tl, 20 * c + (2 + t_before(step) + kb // 2 + 1))
                        for part in (pt_h[step % 2], pt_l[step % 2]):
                            mm = nc.tensor.matmul(ps[:, 3, 0:2 * P], vv[h][:, kb, :], part[:, kb, :],
                                                  start=(kb == 0 and part is pt_h[step % 2]),
                                                  stop=(kb == 2 * g + 1 and part is pt_l[step % 2]))
                    mm.then_inc(s_pv, 1)

                def unit(name):
                    if name == "r0":
                        pe.wait_ge(s_rsw, c + 1)
                    if name == "k0" or (last and name == "r0"):
                        pe.wait_ge(s_pjv, 6 * c + 4)
                    else:
                        was = ORDER[ORDER.index(name) - 1]
                        if was in BY_ACT:
                            pe.wait_ge(s_pja, act_count(c, was))
                        else:
                            pe.wait_ge(s_pjv, dve_count(c, was, last))
                    if name == "k0":
                        pe.wait_ge(s_ulo, c + 2)
                    if name == "vt0":
                        pe.wait_ge(s_pja, act_count(c, "v1"))
                    project(name, c, 7)

                for step, (_, g) in enumerate(STEPS):
                    before, after = units_of(step, last)
                    for i in range(min(2, g + 1)):
                        turn(step, i)
                    score(step, 0)
                    score(step, 1)
                    for name in before:
                        unit(name)
                    for i in range(2, g + 1):
                        turn(step, i)
                    if step >= 1:
                        times_v(step - 1)
                    for name in after[:1]:
                        unit(name)
                    if step == 7:
                        times_v(step)
                    for name in after[1:]:
                        unit(name)

            with pe.Fori(0, PAIRS - 1) as c:
                attention(c, False)
            attention(PAIRS - 1, True)

            def last_products(t, half, chunks):
                rows = slice(t * P, (t + 1) * P)
                cols = slice(half * HALF, (half + 1) * HALF)
                for k in chunks:
                    for i, (a, b) in enumerate(((og_h, wb_h), (og_h, wb_l), (og_l, wb_h))):
                        mm = nc.tensor.matmul(ps[:, t % 2, cols], a[:, k, rows], b[:, k, cols],
                                              start=(k == 0 and i == 0),
                                              stop=(k == GC - 1 and i == 2))
                return mm

            pe.wait_ge(s_wbl, GC)
            pe.wait_ge(s_ogl, GC - 1)
            for t in range(2):
                for half in range(2):
                    last_products(t, half, range(GC - 1))
            pe.wait_ge(s_ogl, GC)
            for t in range(TB):
                for half in range(2):
                    if t >= 2:
                        pe.wait_ge(s_x3, 2 * (t - 2) + half + 1)
                    last_products(t, half, range(GC) if t >= 2 else (GC - 1,)).then_inc(s_fin, 1)

        @block.scalar
        def _(act):
            def copy(dst, src, **more):
                return nc.scalar.activation(dst, src, ACT.Copy, **more)

            def weight_hi(n, slot):
                act.wait_ge(s_tile, slot_free(n))
                copy(w_h[:, slot], raw[:, slot]).then_inc(s_whi, 1)

            act.wait_ge(s_gtp, 1)
            copy(gt[:, 0:KC], ps[:, 2, 0:KC]).then_inc(s_gt, 1)

            def x_hi(u):
                half, k = u // KC, u % KC
                bank = ps[:, 2 + u % 4 // 2, u % 2 * HALF:(u % 2 + 1) * HALF]
                act.wait_ge(s_xtp, u + 1)
                copy(act_h[:, k, half * HALF:(half + 1) * HALF], bank).then_inc(s_xhi, 1)

            act.wait_ge(s_wg, 1)
            weight_hi(0, 0)
            for u in range(KC):
                x_hi(u)
            act.wait_ge(s_wg, 2)
            weight_hi(1, 1)
            for u in range(KC, KC + KC // 2):
                x_hi(u)
            for t in range(TB):
                nc.scalar.activation(junk[:, t, :], x_in[:, t, :], ACT.Square,
                                     accum_out=ssq[:, t:t + 1]).then_inc(s_xsq, 1)
            for u in range(KC + KC // 2, 2 * KC):
                x_hi(u)
            act.wait_ge(s_gtp, 2)
            copy(gt[:, KC:], ps[:, 2, KC:G_ROWS]).then_inc(s_gt, 1)
            act.wait_ge(s_rt, 1)
            copy(r_bc[:], ps[:, 3]).then_inc(s_rsb, 1)

            def gained_hi(n, slot):
                act.wait_ge(s_wg, n + 1)
                weight_hi(n, slot)

            def b_weight_hi(e):
                act.wait_ge(s_wg, N_A + 2 + e + 1)
                weight_hi(B0 + e, (B0 + e) % 2)

            with act.Fori(0, KC) as j:
                gained_hi(4 * j + 2, 0)
                gained_hi(4 * j + 3, 1)
                gained_hi(4 * j + 4, 0)
                act.wait_ge(s_ev, evacuated(4 * j + 2))
                nc.scalar.activation(sg[:], gr[:], ACT.Silu).then_inc(s_silu, 1)
                gained_hi(4 * j + 5, 1)
                act.wait_ge(s_ev, evacuated(4 * j + 3))
                copy(y_h[:, j, :], cv[:]).then_inc(s_yhi, 1)

            def stream(i, t, last):
                n0, m = OUT0 + t, 2 * i + t
                if last:
                    b_weight_hi(t)
                else:
                    act.wait_ge(s_raw[t], 16 * i + 16 * (n0 // 2 + 2))
                    weight_hi(2 * i + n0 + 2, t)
                act.wait_ge(s_acc, m + 1)
                act.wait_ge(s_ev, evacuated(2 * i + n0))
                copy(act_h[:, m, :], xt[:, m, :]).then_inc(s_x2hi, 1)
                nc.scalar.activation(sq[t][:], xt[:, m, :], ACT.Square).then_inc(s_x2sq, 1)

            with act.Fori(0, KC // 2 - 1) as i:
                for t in range(2):
                    stream(i, t, False)
            for t in range(2):
                stream(KC // 2 - 1, t, True)

            def staged(t):
                act.wait_ge(s_x2t, t + 1)
                if t >= 2:
                    act.wait_ge(s_x2w[t % 2], 16 * (t // 2))
                copy(x2_st[t % 2][:], ps[:, 3]).then_inc(s_x2s, 1)

            def gate_silu(z):
                act.wait_ge(s_ev, evacuated(B0 + E_G + z))
                nc.scalar.activation(gate[:, z, :], gate[:, z, :], ACT.Silu).then_inc(s_gsilu, 1)

            squares = [acc, sq[0], acc_q, sq[1], sq[0]]
            for e in range(2, N_B):
                b_weight_hi(e)
                if e == 3:
                    act.wait_ge(s_rt, 2)
                    copy(r_bc[:], ps[:, 3]).then_inc(s_rsb, 1)
                done = e - 2
                for z in ([0, 1] if e == 4 else [] if done < E_Q or done >= E_G else [done - 1]):
                    act.wait_ge(s_ev, evacuated(B0 + Z_TILES[z]))
                    if z == 0:
                        act.wait_ge(s_ss, 1)
                    if z == 4:
                        act.wait_ge(s_cacc, 1)
                    nc.scalar.activation(squares[z][:], zc[:, z, :], ACT.Square).then_inc(s_csq, 1)
                if 4 <= e < 8:
                    staged(2 * (e - 4))
                    staged(2 * (e - 4) + 1)
                if e == 6:
                    act.wait_ge(s_tab, 8)
                    nc.scalar.activation(tq[1][0:2 * ROPE, :], angle[0:2 * ROPE, :], ACT.Sin
                                         ).then_inc(s_sin, 1)
                if e == 8:
                    gate_silu(0)
            for k in range(CKV):
                act.wait_ge(s_cn, k + 1)
                copy(ckv_h[:, k, :], zc[:, k, :]).then_inc(s_chi, 1)
            gate_silu(1)
            act.wait_ge(s_u, 12 * 16)
            copy(u_h[:], u_raw[:]).then_inc(s_uhi, 1)
            for k in range(CQ):
                act.wait_ge(s_cn, CKV + k + 1)
                if k == 0:
                    for w in s_x2w:
                        act.wait_ge(w, 16 * TB // 2)
                copy(cq_h[:, k, :], zc[:, CKV + k, :]).then_inc(s_chi, 1)
            gate_silu(2)
            act.wait_ge(s_tile, tile_done(LAST))
            act.wait_ge(s_krp, 1)
            copy(k_h[0][NOPE:P, :], ps[NOPE:P, 3]).then_inc(s_krhi, 1)
            copy(k_h[1][0:NOPE, :], ps[0:NOPE, 3]).then_inc(s_krhi, 1)

            def proj_evac(name, c):
                if name not in BY_ACT:
                    return
                half = int(name[-1])
                bank = PRO_BANKS[PROJ.index(name) % 4] if c is None else 7
                src = ps[:, bank // 2, bank % 2 * HALF:(bank % 2 + 1) * HALF]
                act.wait_ge(s_pj, pj_count(c, name))
                if c is not None and name == "k0":
                    act.wait_ge(s_splo, split_done(c, "ko"))
                if c is not None and name == "vt0":
                    act.wait_ge(s_splo, split_done(c, "vo"))
                if name[:2] == "vt":
                    dst = v_f[:, 4 * half:4 * half + 4, :].rearrange("p a b -> p (a b)")
                else:
                    dst = (k_f if name[0] == "k" else v_t)[:, half * HALF:(half + 1) * HALF]
                copy(dst, src).then_inc(s_pja, 1)

            def split_hi(what):
                odd = 1 if what[1] == "o" else 0
                rows = slice(NOPE, P) if odd else slice(0, NOPE)
                if what[0] == "q":
                    op = copy(q_h[odd][:], q_f[odd][:])
                elif what[0] == "k":
                    op = copy(k_h[odd][rows, :], k_f[rows, :])
                else:
                    op = copy(vv[odd][:, :, 0:VH], v_f[:, :, odd * VH:(odd + 1) * VH])
                op.then_inc(s_sphi, 1)

            for name in PROJ:
                proj_evac(name, None)
                if name == "k1":
                    act.wait_ge(s_pja, act_count(None, "k1"))
                    split_hi("ke")
                if name == "qe1":
                    act.wait_ge(s_pjv, dve_count(None, "qe1"))
                    split_hi("qe")
            gate_silu(3)

            def exps(number, c, step, q):
                h, g = STEPS[step % 8]
                width = (g + 1) * 2 * P
                act.wait_ge(s_mx, 16 * c + (number + 1))
                slot = 2 * (step % 2) + q
                nc.scalar.activation(prob[q][:, 0:width], ps[:, q, 0:width], ACT.Exp,
                                     bias=smaxn[:, slot:slot + 1], scale=SCALE,
                                     accum_out=rsum[:, h, 2 * g + q:2 * g + q + 1]).then_inc(s_exp, 1)

            exps(0, 0, 0, 0)
            exps(1, 0, 0, 1)
            act.wait_ge(s_pja, act_count(None, "vt1"))
            split_hi("ve")

            def attention(c, last):
                def o_low(step):
                    act.wait_ge(s_pv, 8 * c + (step + 1))
                    copy(o_lo[:], ps[VH:P, 3, 0:2 * P]).then_inc(s_om, 1)

                def og_hi(k):
                    act.wait_ge(s_og, k + 2)
                    copy(og_h[:, k, :], og[:, k, :]).then_inc(s_ogh, 1)

                for step, (h, g) in enumerate(STEPS):
                    before, after = units_of(step, last)

                    def hi(i):
                        n = t_before(step) + i
                        act.wait_ge(s_t, 20 * c + (n + 1))
                        copy(pt_h[step % 2][:, 2 * i:2 * i + 2, :].rearrange("p a b -> p (a b)"),
                             ps[:, 2, n % 2 * HALF:(n % 2 + 1) * HALF]).then_inc(s_th, 1)

                    nxt = next_scores(step, last)

                    def next_exp(q):
                        number = nxt[2]
                        if q == 0:
                            act.wait_ge(s_t, 20 * c + (t_before(step) + g + 1))
                            if number == 16:
                                act.wait_ge(s_rr, c + 1)
                        exps(number + q, c, step + 1, q)

                    for i in range(min(2, g + 1)):
                        hi(i)
                    for name in before:
                        proj_evac(name, c)
                    for i in range(2, g + 1):
                        if i == 3:
                            next_exp(0)
                            next_exp(1)
                        hi(i)
                    if step == 0:
                        if not last:
                            act.wait_ge(s_u, 192 * c + 384)
                            act.wait_ge(s_pj, 12 * c + 10)
                            copy(u_h[:], u_raw[:]).then_inc(s_uhi, 1)
                        act.wait_ge(s_pja, 6 * c + 6)
                        split_hi("ko")
                        split_hi("vo")
                    if step == 1:
                        act.wait_ge(s_pjv, 6 * c + 4)
                        split_hi("qo")
                    if step == 3 and not last:
                        act.wait_ge(s_s, 16 * c + 8)
                        act.wait_ge(s_pja, act_count(c, "k1"))
                        split_hi("ke")
                    if step == 4 and not last:
                        act.wait_ge(s_pjv, dve_count(c, "qe1"))
                        split_hi("qe")
                    if step == 7 and not last:
                        act.wait_ge(s_pja, act_count(c, "vt1"))
                        split_hi("ve")
                    if last and 1 <= step <= GC:
                        k = step - 1
                        act.wait_ge(s_wb[k % 2], 16 * (k // 2 + 1))
                        copy(wb_h[:, k, :], wb_raw[k % 2][:]).then_inc(s_wbh, 1)
                    if nxt is not None and g != 3:
                        next_exp(0)
                        if step == 7:
                            o_low(6)
                        next_exp(1)
                    if last and step == 7:
                        act.wait_ge(s_s, 16 * PAIRS)
                        og_hi(0)
                    if 1 <= step < 7 or (last and step == 7):
                        o_low(step - 1)
                    for name in after:
                        proj_evac(name, c)
                    if last and step == 7:
                        og_hi(1)
                    if step == 7:
                        o_low(step)
                    if last and step == 7:
                        og_hi(2)
                        og_hi(3)

            with act.Fori(0, PAIRS - 1) as c:
                attention(c, False)
            attention(PAIRS - 1, True)
            for t in range(TB):
                for half in range(2):
                    cols = slice(half * HALF, (half + 1) * HALF)
                    n = 2 * t + half
                    act.wait_ge(s_x3, n + 1)
                    if n >= 2:
                        act.wait_ge(s_x3q, n - 1)
                    nc.scalar.activation(x3_sq[:, cols], x3[t % 2][:, cols], ACT.Square,
                                         accum_out=ssq[:, n:n + 1]).then_inc(s_x3q, 1)

        @block.gpsimd
        def _(pool):
            def rsqrt(first, n, waited):
                pool.wait_ge(s_ms, waited)
                nc.gpsimd.tensor_tensor(rms[:, first:first + n], msq[:, first:first + n],
                                        cst[:, C_POW:C_POW + 1].broadcast_to([P, n]),
                                        ALU.pow).then_inc(s_pow, 1)

            def weight_gain(n, fill, slot, gain):
                pool.wait_ge(s_raw[slot], fill)
                nc.gpsimd.tensor_tensor(raw[:, slot], raw[:, slot],
                                        gain.unsqueeze(2).broadcast_to([P, KC, P]), ALU.mult
                                        ).then_inc(s_wg, 1)

            pool.wait_ge(s_gt, 1)
            weight_gain(0, 16, 0, g_a)
            weight_gain(1, 16, 1, g_a)
            pool.wait_ge(s_const, 16 * CONSTS)
            rsqrt(0, TB, 1)
            with pool.Fori(0, KC - 1) as j:
                for t in range(4):
                    weight_gain(4 * j + 2 + t, 32 * j + 16 * (t // 2 + 2), t % 2, g_a)
            weight_gain(N_A - 2, fills(N_A - 2), 0, g_a)
            weight_gain(N_A - 1, fills(N_A - 1), 1, g_a)
            pool.wait_ge(s_wg, N_A)
            for n in (OUT0, OUT0 + 1):
                pool.wait_ge(s_raw[n % 2], fills(n))
                pool.sem_inc(s_wg, 1)
            pool.wait_ge(s_gt, 2)
            for e in range(N_B):
                n = B0 + e
                weight_gain(n, fills(n), n % 2, b_tiles[e][2])
                if e == 1:
                    rsqrt(0, TB, 2)
            rsqrt(0, 2 * TB, 4)

            def split_lo(what, number):
                odd = 1 if what[1] == "o" else 0
                rows = slice(NOPE, P) if odd else slice(0, NOPE)
                pool.wait_ge(s_sphi, number + 1)
                if not isinstance(number, int) or number > 0:
                    pool.wait_ge(s_splo, number)
                if what[0] == "q":
                    dst, src, hi = q_l[odd][:], q_f[odd][:], q_h[odd][:]
                elif what[0] == "k":
                    dst, src, hi = k_l[odd][rows, :], k_f[rows, :], k_h[odd][rows, :]
                else:
                    dst, src = vv[odd][:, :, VH:2 * VH], v_f[:, :, odd * VH:(odd + 1) * VH]
                    hi = vv[odd][:, :, 0:VH]
                nc.gpsimd.tensor_tensor(dst, src, hi.bitcast(F32), ALU.subtract).then_inc(s_splo, 1)

            for number, what in enumerate(("ke", "qe", "ve")):
                split_lo(what, number)

            def widen(c, done):
                pool.wait_ge(s_rr, c + 1)
                pool.wait_ge(s_splo, done)
                wide = [P, TB, 2, VH]
                nc.gpsimd.tensor_tensor(
                    rs_wide[:], rrec[:].rearrange("p h t -> p t h").unsqueeze(3).broadcast_to(wide),
                    ones.unsqueeze(2).unsqueeze(3).broadcast_to(wide), ALU.mult).then_inc(s_rsw, 1)

            with pool.Fori(0, PAIRS - 1) as c:
                for number, what in enumerate(("ko", "vo", "qo", "ke", "qe")):
                    split_lo(what, 6 * c + (3 + number))
                widen(c, 6 * c + 8)
                pool.wait_ge(s_rsw, c + 1)
                split_lo("ve", 6 * c + 8)
                pool.wait_ge(s_pjv, dve_count(c, "r1"))
                pool.wait_ge(s_o, 8 * c + 9)
                nc.gpsimd.tensor_tensor(og[:, c, :], o_t[:], gs[:], ALU.mult).then_inc(s_og, 1)
                pool.wait_ge(s_og, c + 2)
            for number, what in enumerate(("ko", "vo", "qo")):
                split_lo(what, 6 * (PAIRS - 1) + 3 + number)
            for k in range(GC):
                pool.wait_ge(s_wbh, k + 1)
                nc.gpsimd.tensor_tensor(wb_l[:, k, :], wb_raw[k % 2][:], wb_h[:, k, :].bitcast(F32),
                                        ALU.subtract).then_inc(s_wbl, 1)
            widen(PAIRS - 1, 6 * PAIRS)
            for t in range(TB):
                pool.wait_ge(s_fms, t + 1)
                nc.gpsimd.tensor_tensor(rms[:, t:t + 1], msq[:, 1:2], cst[:, C_POW:C_POW + 1],
                                        ALU.pow).then_inc(s_fr, 1)

        @block.vector
        def _(dve):
            tt, ts, stt = nc.vector.tensor_tensor, nc.vector.tensor_scalar, nc.vector.scalar_tensor_tensor

            def weight_lo(n, slot):
                dve.wait_ge(s_whi, n + 1)
                tt(w_l[:, slot], raw[:, slot], w_h[:, slot].bitcast(F32), ALU.subtract
                   ).then_inc(s_wlo, 1)

            def mean_square(src, first, n, width):
                ts(msq[:, first:first + n], src, 1.0 / width, EPS, ALU.mult, ALU.add).then_inc(s_ms, 1)

            def widen(wide, first, waited):
                dve.wait_ge(s_pow, waited)
                nc.vector.tensor_copy(wide[:], rms[:, first:first + TB].unsqueeze(2)
                                      .broadcast_to([P, TB, P])).then_inc(s_rw, 1)

            dve.sem_inc(s_wlo, 2)
            dve.sem_inc(s_ev, 3)
            dve.sem_inc(s_tl, 2)
            dve.sem_inc(s_o, 1)
            dve.sem_inc(s_og, 1)
            nc.vector.memset(v[:, 0:CONV_WIDTH - 1], 0.0).then_inc(s_init, 1)

            def x_lo(u):
                half, k = u // KC, u % KC
                cols = slice(half * HALF, (half + 1) * HALF)
                bank = ps[:, 2 + u % 4 // 2, u % 2 * HALF:(u % 2 + 1) * HALF]
                dve.wait_ge(s_xhi, u + 1)
                tt(act_l[:, k, cols], bank, act_h[:, k, cols].bitcast(F32), ALU.subtract
                   ).then_inc(s_xlo, 1)

            weight_lo(0, 0)
            for u in range(KC):
                x_lo(u)
            weight_lo(1, 1)
            for u in range(KC, KC + KC // 2):
                x_lo(u)
            dve.wait_ge(s_const, 16 * CONSTS)
            nc.vector.tensor_copy(identb[:], ident).then_inc(s_init, 1)
            nc.vector.tensor_copy(maskb[:].rearrange("p a b -> p (a b)"), cst[:, C_MASK:C_END]
                                  ).then_inc(s_init, 1)
            dve.wait_ge(s_xsq, TB)
            mean_square(ssq[:, 0:TB], 0, TB, D)
            for u in range(KC + KC // 2, 2 * KC):
                x_lo(u)
            widen(r_wide, 0, 1)
            dve.wait_ge(s_rsb, 1)
            tt(r2_bc[:], r_bc[:], r_bc[:], ALU.mult).then_inc(s_ev, 1)

            with dve.Fori(0, KC) as j:
                dve.wait_ge(s_tile, tile_done(4 * j))
                dve.wait_ge(s_ev, evacuated(4 * j - 1))
                tt(cr[:], ps[:, 0], r2_bc[:], ALU.mult).then_inc(s_ev, 1)
                weight_lo(4 * j + 2, 0)
                dve.wait_ge(s_tile, tile_done(4 * j + 1))
                dve.wait_ge(s_ev, evacuated(4 * j))
                tt(v[:, 2:2 + S], ps[:, 1], cr[:], ALU.mult).then_inc(s_ev, 1)
                weight_lo(4 * j + 3, 1)
                dve.wait_ge(s_ev, evacuated(4 * j + 1))
                ts(cv[:], v[:, 0:S], conv_w[:, 0, bass.ds(j, 1)], None, ALU.mult).then_inc(s_cv, 1)
                for w in range(1, CONV_WIDTH):
                    dve.wait_ge(s_cv, 5 * j + w)
                    stt(cv[:], v[:, w:w + S], conv_w[:, w, bass.ds(j, 1)], cv[:], ALU.mult, ALU.add
                        ).then_inc(s_cv, 1)
                dve.wait_ge(s_tile, tile_done(4 * j + 2))
                tt(gr[:], ps[:, 2], r_bc[:], ALU.mult).then_inc(s_ev, 1)
                weight_lo(4 * j + 4, 0)
                dve.wait_ge(s_cv, 5 * j + 3)
                tt(cv[:], cv[:], r_bc[:], ALU.mult).then_inc(s_cv, 1)
                dve.wait_ge(s_silu, j + 1)
                dve.wait_ge(s_cv, 5 * j + 4)
                tt(cv[:], cv[:], sg[:], ALU.mult).then_inc(s_cv, 1)
                dve.wait_ge(s_tile, tile_done(4 * j + 3))
                dve.wait_ge(s_cv, 5 * j + 5)
                tt(cv[:], cv[:], ps[:, 3], ALU.mult).then_inc(s_ev, 1)
                weight_lo(4 * j + 5, 1)
                dve.wait_ge(s_yhi, j + 1)
                tt(y_l[:, j, :], cv[:], y_h[:, j, :].bitcast(F32), ALU.subtract).then_inc(s_ylo, 1)

            nc.vector.memset(acc[:], 0.0).then_inc(s_acc, 2)

            def stream(i, t):
                n0, m = OUT0 + t, 2 * i + t
                tt(xt[:, m, :], act_h[:, m, :].bitcast(F32), act_l[:, m, :].bitcast(F32), ALU.add
                   ).then_inc(s_xr, 1)
                dve.wait_ge(s_xr, m + 1)
                dve.wait_ge(s_tile, tile_done(2 * i + n0))
                tt(xt[:, m, :], xt[:, m, :], ps[:, t], ALU.add).then_inc(s_ev, 1)
                weight_lo(2 * i + n0 + 2, t)
                dve.wait_ge(s_x2hi, m + 1)
                tt(act_l[:, m, :], xt[:, m, :], act_h[:, m, :].bitcast(F32), ALU.subtract
                   ).then_inc(s_x2lo, 1)
                dve.wait_ge(s_x2sq, m + 1)
                dve.wait_ge(s_acc, m + 2)
                tt(acc[:], acc[:], sq[t][:], ALU.add).then_inc(s_acc, 1)

            with dve.Fori(0, KC // 2) as i:
                for t in range(2):
                    stream(i, t)

            dve.wait_ge(s_ss, 1)
            mean_square(ps[:, 3, 0:TB], 0, TB, D)
            weight_lo(B0 + 2, 0)
            widen(r_wide, 0, 2)
            weight_lo(B0 + 3, 1)
            dve.wait_ge(s_rsb, 2)

            def evacuate(e):
                pair = ps[:, e % 3]
                dve.wait_ge(s_tile, tile_done(B0 + e))
                if e == E_ROPE:
                    tt(zk[:], pair[0:2 * ROPE, :], r_bc[0:2 * ROPE, :], ALU.mult).then_inc(s_ev, 1)
                elif e < E_G:
                    tt(zc[:, Z_TILES.index(e), :], pair, r_bc[:], ALU.mult).then_inc(s_ev, 1)
                else:
                    tt(gate[:, e - E_G, :], pair, r_bc[:], ALU.mult).then_inc(s_ev, 1)

            def sum_squares(into, frm, squares_done):
                dve.wait_ge(s_csq, squares_done)
                if squares_done == 5:
                    dve.wait_ge(s_cacc, 2)
                tt(into[:], into[:], frm[:], ALU.add).then_inc(s_cacc, 1)

            def table_step(op):
                op.then_inc(s_tab, 1)
                table[0] += 1
                dve.wait_ge(s_tab, table[0])

            rows = slice(0, 2 * ROPE)
            freq = cst[rows, C_FREQ:C_FREQ + 1]

            def whole_turns():
                dve.wait_ge(s_pos, 16)
                table_step(nc.vector.tensor_copy(pos_f[rows, :], pos_i[rows, :]))
                table_step(ts(pos_f[rows, :], pos_f[rows, :], freq, None, ALU.mult))
                table_step(ts(turns[rows, :], pos_f[rows, :], 1 / (2 * np.pi),
                              cst[rows, C_TURN:C_TURN + 1], ALU.mult, ALU.add))
                table_step(ts(turns[rows, :], turns[rows, :], ROUND, ROUND, ALU.add, ALU.subtract))

            def reduced():
                for i, part in enumerate((TWO_PI_A, TWO_PI_B, TWO_PI_C)):
                    src = pos_f if i == 0 else angle
                    table_step(stt(angle[rows, :], turns[rows, :], -part, src[rows, :],
                                   ALU.mult, ALU.add))
                table_step(ts(angle[rows, :], angle[rows, :], cst[rows, C_PHASE:C_PHASE + 1], PI_IN,
                              ALU.add, ALU.min))

            def rotary_tables():
                dve.wait_ge(s_sin, 1)
                nc.vector.tensor_copy(tq[0][NOPE:P, :], tq[1][rows, :]).then_inc(s_tab, 1)
                nc.vector.memset(tq[0][0:NOPE, :], 1.0).then_inc(s_tab, 1)
                nc.vector.memset(tq[1][NOPE:P, :], 1.0).then_inc(s_tab, 1)
                dve.wait_ge(s_ev, evacuated(B0 + E_ROPE))
                tt(zk[:], zk[:], tq[1][rows, :], ALU.mult).then_inc(s_kr, 1)

            table = [0]
            evacuate(0)
            evacuate(1)
            whole_turns()
            for e in range(4, N_B):
                evacuate(e - 2)
                weight_lo(B0 + e, (B0 + e) % 2)
                if e == 4:
                    reduced()
                if e == 5:
                    sum_squares(acc, sq[0], 2)
                if e == 6:
                    sum_squares(acc_q, sq[1], 4)
                if e == 7:
                    sum_squares(acc_q, sq[0], 5)
                    rotary_tables()
                if e == 8:
                    dve.wait_ge(s_ss, 2)
                    mean_square(ps[:, 3, 0:TB], 0, TB, KV_RANK)
                    mean_square(ps[:, 3, TB:2 * TB], TB, TB, Q_RANK)
                    widen(rk_wide, 0, 3)
                    widen(rq_wide, TB, 3)
            dve.wait_ge(s_rt, 3)
            for k in range(CKV):
                stt(zc[:, k, :], zc[:, k, :], g_ckv[:, k:k + 1], ps[:, 3], ALU.mult, ALU.mult
                    ).then_inc(s_cn, 1)
            for k in range(CKV):
                dve.wait_ge(s_chi, k + 1)
                tt(ckv_l[:, k, :], zc[:, k, :], ckv_h[:, k, :].bitcast(F32), ALU.subtract
                   ).then_inc(s_clo, 1)
            dve.wait_ge(s_rt, 4)
            for k in range(CQ):
                stt(zc[:, CKV + k, :], zc[:, CKV + k, :], g_q[:, k:k + 1], ps[:, 3], ALU.mult, ALU.mult
                    ).then_inc(s_cn, 1)
            dve.wait_ge(s_uhi, 1)
            tt(u_l[:], u_raw[:], u_h[:].bitcast(F32), ALU.subtract).then_inc(s_ulo, 1)
            evacuate(8)
            for k in range(CQ):
                dve.wait_ge(s_chi, CKV + k + 1)
                if k == 0:
                    for w in s_x2w:
                        dve.wait_ge(w, 16 * TB // 2)
                tt(cq_l[k][:], zc[:, CKV + k, :], cq_h[:, k, :].bitcast(F32), ALU.subtract
                   ).then_inc(s_clo, 1)
            evacuate(9)
            dve.wait_ge(s_krhi, 2)
            tt(k_l[0][NOPE:P, :], ps[NOPE:P, 3], k_h[0][NOPE:P, :].bitcast(F32), ALU.subtract
               ).then_inc(s_krlo, 1)
            tt(k_l[1][0:NOPE, :], ps[0:NOPE, 3], k_h[1][0:NOPE, :].bitcast(F32), ALU.subtract
               ).then_inc(s_krlo, 1)

            def proj_evac(name, c, last=False):
                if name not in BY_DVE:
                    return
                half = int(name[-1])
                cols = slice(half * HALF, (half + 1) * HALF)
                bank = PRO_BANKS[PROJ.index(name) % 4] if c is None else 7
                src = ps[:, bank // 2, bank % 2 * HALF:(bank % 2 + 1) * HALF]
                dve.wait_ge(s_pj, pj_count_last(name) if last else pj_count(c, name))
                if name[0] == "r":
                    tt(gs[:, cols], src, gate[:, c, cols], ALU.mult).then_inc(s_pjv, 1)
                    return
                odd = 1 if name[1] == "o" else 0
                if c is not None and half == 0:
                    dve.wait_ge(s_splo, split_done(c, "qo" if odd else "qe"))
                tt(q_f[odd][:, cols], src, tq[odd][:, cols], ALU.mult).then_inc(s_pjv, 1)

            for name in PROJ:
                proj_evac(name, None)

            def row_max(number, c, step, q):
                slot = 2 * (step % 2) + q
                g = STEPS[step % 8][1]
                dve.wait_ge(s_s, 16 * c + (number + 1))
                nc.vector.reduce_max(smax[:, slot:slot + 1], ps[:, q, 0:(g + 1) * 2 * P], AX_X
                                     ).then_inc(s_mxr, 1)
                dve.wait_ge(s_mxr, 16 * c + (number + 1))
                ts(smaxn[:, slot:slot + 1], smax[:, slot:slot + 1], -SCALE, None, ALU.mult
                   ).then_inc(s_mx, 1)

            row_max(0, 0, 0, 0)
            row_max(1, 0, 0, 1)

            def attention(c, last):
                def o_add(step):
                    h, g = STEPS[step]
                    if step == 0:
                        dve.wait_ge(s_og, c + 1)
                    dve.wait_ge(s_om, 8 * c + (step + 1))
                    tt(o_t[h * VH:(h + 1) * VH, g * 2 * P:(g + 1) * 2 * P], ps[0:VH, 3, 0:2 * P],
                       o_lo[:], ALU.add).then_inc(s_o, 1)

                def og_lo(k):
                    dve.wait_ge(s_ogh, k + 1)
                    tt(og_l[:, k, :], og[:, k, :], og_h[:, k, :].bitcast(F32), ALU.subtract
                       ).then_inc(s_ogl, 1)

                for step, (h, g) in enumerate(STEPS):
                    nxt = next_scores(step, last)
                    before, after = units_of(step, last)

                    def lo(i):
                        n = t_before(step) + i
                        dve.wait_ge(s_th, 20 * c + (n + 1))
                        dst = pt_l[step % 2][:, 2 * i:2 * i + 2, :].rearrange("p a b -> p (a b)")
                        hi = pt_h[step % 2][:, 2 * i:2 * i + 2, :].rearrange("p a b -> p (a b)")
                        tt(dst, ps[:, 2, n % 2 * HALF:(n % 2 + 1) * HALF], hi.bitcast(F32),
                           ALU.subtract).then_inc(s_tl, 1)

                    if step == 7:
                        dve.wait_ge(s_exp, 16 * c + 16)
                        nc.vector.reciprocal(rrec[:], rsum[:]).then_inc(s_rr, 1)
                    for i in range(min(2, g + 1)):
                        lo(i)
                    if nxt is not None:
                        row_max(nxt[2], c, step + 1, 0)
                        row_max(nxt[2] + 1, c, step + 1, 1)
                    for name in before:
                        proj_evac(name, c, last)
                    for i in range(2, g + 1):
                        lo(i)
                    if step == 0 and not last:
                        dve.wait_ge(s_uhi, c + 2)
                        tt(u_l[:], u_raw[:], u_h[:].bitcast(F32), ALU.subtract).then_inc(s_ulo, 1)
                    if last and step == 7:
                        og_lo(0)
                    if step >= 1:
                        o_add(step - 1)
                    for name in after[:1]:
                        proj_evac(name, c, last)
                    if last and step == 7:
                        og_lo(1)
                    if step == 7:
                        o_add(step)
                    for name in after[1:]:
                        proj_evac(name, c, last)
                if last:
                    dve.wait_ge(s_pjv, dve_count(c, "r1", last))
                    dve.wait_ge(s_o, 8 * c + 9)
                    tt(og[:, c, :], o_t[:], gs[:], ALU.mult).then_inc(s_og, 1)
                    og_lo(2)
                    og_lo(3)

            dve.wait_ge(s_gsilu, GC)
            with dve.Fori(0, PAIRS - 1) as c:
                attention(c, False)
            attention(PAIRS - 1, True)

            def normed(t, cols):
                dve.wait_ge(s_fr, t + 1)
                if t == 0:
                    dve.wait_ge(s_gf, 16)
                if t >= 2:
                    dve.wait_ge(s_out[t % 2], 16 * (t // 2))
                stt(y_out[t % 2][:, cols], x3[t % 2][:, cols], rms[:, t:t + 1], g_f[:, cols],
                    ALU.mult, ALU.mult).then_inc(s_y, 1)

            for t in range(TB):
                dve.wait_ge(s_x2r[t % 2], 16 * (t // 2 + 1))
                if t >= 2:
                    dve.wait_ge(s_y, t - 1)
                for half in range(2):
                    cols = slice(half * HALF, (half + 1) * HALF)
                    dve.wait_ge(s_fin, 2 * t + half + 1)
                    tt(x3[t % 2][:, cols], x2_r[t % 2][:, cols], ps[:, t % 2, cols], ALU.add
                       ).then_inc(s_x3, 1)
                    if t >= 1 and half == 0:
                        normed(t - 1, slice(0, D))
                dve.wait_ge(s_x3q, 2 * t + 1)
                ts(msq[:, 0:1], ssq[:, 2 * t:2 * t + 1], 1.0 / D, EPS, ALU.mult, ALU.add
                   ).then_inc(s_fm, 1)
                dve.wait_ge(s_x3q, 2 * t + 2)
                dve.wait_ge(s_fm, t + 1)
                stt(msq[:, 1:2], ssq[:, 2 * t + 1:2 * t + 2], 1.0 / D, msq[:, 0:1], ALU.mult, ALU.add
                    ).then_inc(s_fms, 1)
            normed(TB - 1, slice(0, HALF))
            normed(TB - 1, slice(HALF, D))


_INS = ["x", "positions", "a_norm", "a_w_in", "a_conv", "a_w_out", "kv_norm", "w_dkv", "ckv_norm",
        "w_ukv", "b_norm", "b_w_in", "b_q_norm", "b_w_uq", "b_w_out", "final_norm"]


def kernel(**inputs):
    import concourse.bacc as bacc
    from concourse.bass_utils import run_bass_kernel_spmd

    nc = bacc.Bacc("TRN2", target_bir_lowering=False, num_devices=1, dynamic_dma_scratch_size=1024)
    given = {name: np.ascontiguousarray(inputs[name]) for name in _INS}
    given["const"] = constants()
    arrays, args = {}, []
    for name, a in given.items():
        arrays[f"in_{name}"] = a
        args.append(nc.dram_tensor(f"in_{name}", a.shape, mybir.dt.from_np(a.dtype),
                                   kind="ExternalInput").ap())
    args.append(nc.dram_tensor("out", (1, S, D), F32, kind="ExternalOutput").ap())
    trunk(nc, *args)
    r = run_bass_kernel_spmd(nc, [arrays], core_ids=[0])
    return r.results[0]["out"]
```

```python
from contextlib import ExitStack

import numpy as np

import concourse.bass as bass
from concourse import mybir

F32 = mybir.dt.float32
F32R = mybir.dt.float32r
BF16 = mybir.dt.bfloat16
I32 = mybir.dt.int32
ALU = mybir.AluOpType
ACT = mybir.ActivationFunctionType
AX_X = mybir.AxisListType.X

P = 128
S = 1024
D = 1024
KC = D // P
TB = S // P
HALF = 512
CONV_WIDTH = 3
HEADS = 8
PAIRS = HEADS // 2
NOPE, ROPE, VH = 64, 32, 64
RH = ROPE // 2
KV_RANK, Q_RANK = 256, 384
CKV, CQ = KV_RANK // P, Q_RANK // P
GC = HEADS * VH // P
SCALE = 1.0 / float(np.sqrt(np.float64(NOPE + ROPE)))
EPS = 1e-6
THETA = 10000.0
MASK = -3.0e38
ROUND = 1.5 * 2.0 ** 23
TWO_PI_A = 6.28125
TWO_PI_B = float(np.float32(2 * np.pi - TWO_PI_A))
TWO_PI_C = float(2 * np.pi - TWO_PI_A - np.float64(np.float32(2 * np.pi - TWO_PI_A)))
PI_IN = 3.1415925

C_ID, C_SEL, C_ONE, C_FREQ, C_TURN, C_PHASE, C_POW, C_MASK = 0, 128, 256, 257, 258, 259, 260, 261
C_END = C_MASK + 4 * P

G_OFF = [0, KC, 2 * KC, 3 * KC, 3 * KC + CKV, 3 * KC + CKV + CQ]
G_ROWS = G_OFF[-1] + CONV_WIDTH * KC


def constants():
    c = np.zeros((P, C_END), np.float32)
    c[:, C_ID:C_ID + P] = np.eye(P)
    for r in range(2 * ROPE):
        c[r, C_SEL:C_SEL + P] = [r % ROPE == m % ROPE for m in range(P)]
    c[:, C_ONE] = 1.0
    freq = np.float32(THETA) ** (-np.arange(0, ROPE, 2, dtype=np.float32) / np.float32(ROPE))
    for r in range(ROPE):
        c[r, C_FREQ] = freq[r % RH]
        c[r, C_PHASE] = np.pi / 2
        c[r, C_TURN] = 0.25
        c[ROPE + r, C_FREQ] = freq[r % RH] * (-1 if r < RH else 1)
    c[:, C_POW] = -0.5
    mask = np.zeros((P, 2, 2 * P), np.float32)
    above = np.triu(np.ones((P, P), bool), 1)
    mask[:, 0, 0:P][above] = MASK
    mask[:, 0, P:] = MASK
    mask[:, 1, P:][above] = MASK
    c[:, C_MASK:] = mask.reshape(P, 4 * P)
    return c


def trunk(nc, x, positions, a_norm, a_w_in, a_conv, a_w_out, kv_norm, w_dkv, ckv_norm, w_ukv,
          b_norm, b_w_in, b_q_norm, b_w_uq, b_w_out, final_norm, const, out):
    x_d = x.rearrange("a (t p) d -> p (a t) d", p=P)
    out_d = out.rearrange("a (t p) d -> p (a t) d", p=P)
    w_in_d = a_w_in.rearrange("a (k p) n -> p (a k) n", p=P)
    w_out_d = a_w_out.rearrange("a (k p) n -> p (a k) n", p=P)
    w_dkv_d = w_dkv.rearrange("(k p) n -> p k n", p=P)
    w_b_d = b_w_in.rearrange("a (k p) n -> p (a k) n", p=P)
    w_uq_d = b_w_uq.rearrange("a (k p) n -> p (a k) n", p=P)
    w_ukv_d = w_ukv.rearrange("(k p) n -> p k n", p=P)
    w_bo_d = b_w_out.rearrange("a (k p) n -> p (a k) n", p=P)
    x2_d = nc.dram_tensor("x2_scratch", [S, D], F32, kind="Internal").ap()
    x2_d = x2_d.rearrange("(t p) d -> p t d", p=P)

    with ExitStack() as ctx:
        def sem(name):
            return ctx.enter_context(nc.semaphore(name))

        base = (nc.sbuf_base + 31) // 32 * 32
        small = [base]

        def const_sb(name, shape, dt=F32):
            n = int(np.prod(shape[1:])) * (2 if dt == BF16 else 4)
            t = nc.alloc_sbuf_tensor_at(name, shape, dt, offset=small[0])
            small[0] += (n + 31) // 32 * 32
            return t

        cst = const_sb("cst", [P, C_END])
        maskb = const_sb("maskb", [P, 2, 2 * P], BF16)
        identb = const_sb("identb", [P, P], BF16)
        gt = const_sb("gt", [P, G_ROWS])
        g_a, g_kv, g_b, g_ckv, g_q = (gt[:, a:b] for a, b in zip(G_OFF, G_OFF[1:]))
        conv_w = gt[:, G_OFF[-1]:].rearrange("p (w k) -> p w k", w=CONV_WIDTH)
        ssq = const_sb("ssq", [P, 2 * TB])
        msq = const_sb("msq", [P, 2 * TB])
        rms = const_sb("rms", [P, 2 * TB])
        smax = const_sb("smax", [P, 4])
        smaxn = const_sb("smaxn", [P, 4])
        rsum = const_sb("rsum", [P, 2, TB])
        rrec = const_sb("rrec", [P, 2, TB])
        arena = small[0]
        K = 1024

        def at(name, kib, shape, dt=F32):
            return nc.alloc_sbuf_tensor_at(name, shape, dt, offset=arena + kib * K)

        act_h = at("act_h", 0, [P, KC, S], F32R)
        act_l = at("act_l", 32, [P, KC, S], F32R)
        xt = at("xt", 64, [P, KC, S])
        y_h = at("y_h", 96, [P, KC, S], F32R)
        y_l = at("y_l", 128, [P, KC, S], F32R)
        x_in = at("x_in", 96, [P, TB, D])
        junk = at("junk", 128, [P, TB, D])
        g_rows = at("g_rows", 205, [G_ROWS, P])
        raw = at("raw", 160, [P, 2, KC, P])
        w_h = at("w_h", 168, [P, 2, KC, P], F32R)
        w_l = at("w_l", 176, [P, 2, KC, P], F32R)
        r_bc = at("r_bc", 184, [P, S])
        r2_bc = at("r2_bc", 188, [P, S])
        cr = at("cr", 192, [P, S])
        v = at("v", 196, [P, S + CONV_WIDTH - 1])
        cv = at("cv", 201, [P, S])
        gr = at("gr", 205, [P, S])
        sg = at("sg", 209, [P, S])
        r_wide = at("r_wide", 209, [P, TB, P])
        sq = [at("sq0", 192, [P, S]), at("sq1", 201, [P, S])]
        acc = at("acc", 205, [P, S])
        gate = at("gate", 96, [P, GC, S])
        zc = at("zc", 112, [P, CKV + CQ, S])
        tq = [at("tq0", 132, [P, S]), at("tq1", 136, [P, S])]
        pos_i = at("pos_i", 140, [P, S], I32)
        pos_f = at("pos_f", 144, [P, S])
        turns = at("turns", 148, [P, S])
        angle = at("angle", 152, [P, S])
        acc_q = at("acc_q", 209, [P, S])
        rk_wide = at("rk_wide", 205, [P, TB, P])
        rq_wide = at("rq_wide", 209, [P, TB, P])
        zk = at("zk", 213, [2 * ROPE, S])
        ckv_h = at("ckv_h", 140, [P, CKV, S], F32R)
        ckv_l = at("ckv_l", 148, [P, CKV, S], F32R)
        cq_h = at("cq_h", 188, [P, CQ, S], F32R)
        cq_l = [at(f"cq_l{k}", o, [P, S], F32R) for k, o in enumerate((156, 205, 209))]
        x2_st = [at("x2_st0", 156, [P, D]), at("x2_st1", 188, [P, D])]
        q_h = [at("qe_h", 0, [P, S], F32R), at("qo_h", 8, [P, S], F32R)]
        q_l = [at("qe_l", 4, [P, S], F32R), at("qo_l", 12, [P, S], F32R)]
        k_h = [at("ke_h", 16, [P, S], F32R), at("ko_h", 24, [P, S], F32R)]
        k_l = [at("ke_l", 20, [P, S], F32R), at("ko_l", 28, [P, S], F32R)]
        pt_h = [at("pt_h0", 32, [P, TB, 2 * P], F32R), at("pt_h1", 80, [P, TB // 2, 2 * P], F32R)]
        pt_l = [at("pt_l0", 40, [P, TB, 2 * P], F32R), at("pt_l1", 182, [P, TB // 2, 2 * P], F32R)]
        prob = [[at("prob00", 48, [P, S]), at("prob01", 52, [P, S])],
                [at("prob10", 201, [P, S]), at("prob11", 213, [P, S])]]
        vv = [at("v_e", 56, [P, TB, 2 * VH], F32R), at("v_o", 60, [P, TB, 2 * VH], F32R)]
        q_f = [at("q_fe", 160, [P, S]), at("q_fo", 164, [P, S])]
        k_f = at("k_f", 168, [P, S])
        v_t = at("v_t", 172, [P, S])
        v_f = at("v_f", 176, [P, TB, P])
        o_t = at("o_t", 84, [P, S])
        rs_wide = at("rs_wide", 88, [P, TB, 2, VH])
        gs = at("gs", 92, [P, S])
        og = at("og", 112, [P, GC, S])
        u_raw = at("u_raw", 64, [P, 10, P])
        u_h = at("u_h", 69, [P, 10, P], F32R)
        u_l = at("u_l", 74, [P, 10, P], F32R)
        o_lo = at("o_lo", 180, [VH, 2 * P])
        og_h = at("og_h", 188, [P, GC - 1, S], F32R)
        og_l = at("og_l", 160, [P, GC - 1, S], F32R)
        og_h3 = at("og_h3", 0, [P, S], F32R)
        og_l3 = at("og_l3", 4, [P, S], F32R)
        wb_raw = [at("wb_raw0", 205, [P, D]), at("wb_raw1", 209, [P, D])]
        wb_h = at("wb_h", 140, [P, GC, D], F32R)
        wb_l = at("wb_l", 64, [P, GC, D], F32R)
        g_f = at("g_f", 128, [P, D])
        x3 = [at(f"x3_{t}", o, [P, D]) for t, o in enumerate((132, 136, 156, 172, 176, 112, 201, 213))]
        x3_sq = at("x3_sq", 56, [P, D])
        y_out = [at(f"y_out{i}", 32 + 4 * i, [P, D]) for i in range(4)]

        ident = cst[:, C_ID:C_ID + P]
        ones = cst[:, C_ONE:C_ONE + 1]

        ps = ctx.enter_context(nc.psum_tensor("ps", [P, 4, 2 * HALF], F32))

        s_ident = sem("identity_in")
        s_ga = sem("a_norm_in")
        s_const = sem("const_in")
        s_gtp = sem("gains_transposed")
        s_gt = sem("gains_in_sbuf")
        s_x = [sem(f"x_in{t}") for t in range(TB)]
        s_raw = [sem("raw_in0"), sem("raw_in1")]
        s_pos = sem("pos_in")
        s_whi = sem("w_hi")
        s_wlo = sem("w_lo")
        s_wg = sem("w_gain")
        s_tile = sem("tile_done")
        s_ev = sem("ps_evacuated")
        s_xtp = sem("x_transposed")
        s_xhi = sem("x_hi")
        s_xlo = sem("x_lo")
        s_xsq = sem("x_squares")
        s_init = sem("dve_init")
        s_ms = sem("mean_square")
        s_pow = sem("rsqrt_done")
        s_rw = sem("r_widened")
        s_rt = sem("r_transposed")
        s_rsb = sem("r_in_sbuf")
        s_cv = sem("conv_step")
        s_silu = sem("silu_done")
        s_yhi = sem("y_hi")
        s_ylo = sem("y_lo")
        s_xr = sem("x_restored")
        s_x2hi = sem("x2_hi")
        s_x2lo = sem("x2_lo")
        s_x2sq = sem("x2_square")
        s_acc = sem("acc_step")
        s_ss = sem("ss_product")
        s_tab = sem("table_step")
        s_sin = sem("sin_done")
        s_csq = sem("c_square")
        s_cacc = sem("c_acc")
        s_gsilu = sem("gate_silu")
        s_cn = sem("c_normed")
        s_chi = sem("c_hi")
        s_clo = sem("c_lo")
        s_kr = sem("k_rope_step")
        s_krp = sem("k_rope_product")
        s_krhi = sem("k_rope_hi")
        s_krlo = sem("k_rope_lo")
        s_x2t = sem("x2_transposed")
        s_x2s = sem("x2_staged")
        s_x2w = [sem("x2_written0"), sem("x2_written1")]
        s_u = sem("u_in")
        s_uhi = sem("u_hi")
        s_ulo = sem("u_lo")
        s_pj = sem("proj_product")
        s_pja = sem("proj_evac_act")
        s_pjv = sem("proj_evac_dve")
        s_sphi = sem("split_hi")
        s_splo = sem("split_lo")
        s_s = sem("scores_done")
        s_mxr = sem("row_max")
        s_mx = sem("row_max_scaled")
        s_exp = sem("exp_done")
        s_t = sem("p_transposed")
        s_th = sem("pt_hi")
        s_tl = sem("pt_lo")
        s_pv = sem("pv_done")
        s_om = sem("o_low_moved")
        s_o = sem("o_added")
        s_rr = sem("rsum_inverted")
        s_rsw = sem("rsum_widened")
        s_og = sem("og_done")
        s_ogh = sem("og_hi")
        s_ogl = sem("og_lo")
        s_wb = [sem("wb_in0"), sem("wb_in1")]
        s_wbh = sem("wb_hi")
        s_wbl = sem("wb_lo")
        s_gf = sem("gf_in")
        s_x2r = [sem(f"x2_read{t}") for t in range(TB)]
        s_f = sem("early_product")
        s_fx = sem("early_added")
        s_fin = sem("last_product")
        s_x3 = sem("x3_done")
        s_x3q = sem("x3_squared")
        s_fm = sem("final_ms_half")
        s_fms = sem("final_ms")
        s_fr = sem("final_rsqrt")
        s_y = sem("y_normed")
        s_ya = sem("y_scaled")
        s_yp = sem("y_normed_pool")
        s_out = [sem(f"out_written{i}") for i in range(4)]

        N_A, N_O = 4 * KC, KC
        OUT0, B0 = N_A, N_A + N_O
        b_tiles = [("dkv", c * P, g_kv) for c in range(CKV)] + [("rope", KV_RANK, g_kv)]
        b_tiles += [("b", c * P, g_b) for c in range(CQ + GC)]
        N_B = len(b_tiles)
        E_ROPE, E_Q, E_G = CKV, CKV + 1, CKV + 1 + CQ
        LAST = B0 + N_B - 1
        Z_TILES = [0, 1, E_Q, E_Q + 1, E_Q + 2]

        def fills(n):
            rope = B0 + E_ROPE
            return 16 * (n // 2 + 1) + (32 if n >= rope and n % 2 == rope % 2 else 0)

        def lo_done(n):
            return n + 3

        def tile_done(n):
            return n + 3

        def slot_free(n):
            return n + 1

        def evacuated(n):
            return n + 5

        CONSTS = 6

        STEPS = [(h, g) for h in range(2) for g in (3, 0, 2, 1)]
        UNITS = {1: (["k0"], ["k1"]), 2: (["v0"], ["qe0"]), 3: ([], ["qe1"]), 4: (["v1"], ["qo0"]),
                 5: ([], ["vt0"]), 6: (["qo1"], ["vt1"]), 7: ([], ["r0", "r1"])}
        EARLY = 4
        LAST_UNITS = {4: (["f0"], ["f1"]), 5: (["f2"], ["f3"]), 6: (["f4"], ["f5"]),
                      7: (["f6", "f7"], ["r0", "r1"])}
        LAST_ORDER = (4, 5, 0, 1, 6, 2, 3, 7)
        BY_POOL = (1, 3, 5)
        BY_DVE_LAST = [i for i in range(TB) if i not in BY_POOL]
        PROJ = [u for s in range(1, 7) for part in UNITS[s] for u in part]
        ORDER = PROJ + ["r0", "r1"]
        BY_ACT = ("k0", "k1", "v0", "v1", "vt0", "vt1")
        BY_DVE = ("qe0", "qe1", "qo0", "qo1", "r0", "r1")
        PRO = ["qe0", "qe1", "k0", "k1", "v0", "v1", "qo0", "vt0", "qo1", "vt1"]
        PRO_BANKS = dict(zip(PRO, (2, 3, 4, 5, 6, 7, 4, 5, 6, 7)))

        def units_of(step, last):
            return (LAST_UNITS if last else UNITS).get(step, ([], []))

        def pj_count(c, name):
            if c is None:
                return PRO.index(name) + 1
            return 12 * c + (10 + ORDER.index(name) + 1)

        def pj_count_last(name):
            return 10 + 12 * (PAIRS - 1) + ("r0", "r1").index(name) + 1

        def act_count(c, name):
            return BY_ACT.index(name) + 1 if c is None else 6 * c + (6 + BY_ACT.index(name) + 1)

        SPLITS = ("ke", "qe", "ve", "ko", "vo", "qo")

        def dve_count(c, name, last=False):
            if c is None:
                return BY_DVE.index(name) + 1
            if last:
                return 4 + 6 * (PAIRS - 1) + ("r0", "r1").index(name) + 1
            return 6 * c + (4 + BY_DVE.index(name) + 1)

        def next_scores(step, last):
            if step < 7:
                return STEPS[step + 1] + (2 * (step + 1),)
            return None if last else STEPS[0] + (16,)

        def t_before(step):
            return sum(g + 1 for _, g in STEPS[:step])

        def split_done(c, what):
            return 6 * c + (SPLITS.index(what) + 1)

        block = ctx.enter_context(nc.Block())

        @block.sync
        def _(sp):
            def load_w_in(j, t, part):
                sp.dma_start(raw[:, t % 2], w_in_d[:, :, bass.ds(j * P + (part * D - P), P)]
                             ).then_inc(s_raw[t % 2], 16)

            def rows(n, source):
                return g_rows[G_OFF[n]:G_OFF[n] + source.shape[0], :], source

            sp.dma_start(cst[:, C_ID:C_ID + P], const[:, C_ID:C_ID + P]).then_inc(s_ident, 16)
            sp.dma_start(*rows(0, a_norm.rearrange("a (k p) -> (a k) p", p=P))).then_inc(s_ga, 16)
            load_w_in(1, 0, 1)
            for t in range(4):
                sp.dma_start(x_in[:, t, :], x_d[:, t, :]).then_inc(s_x[t], 16)
            load_w_in(1, 1, 2)
            for t in range(4, TB):
                sp.dma_start(x_in[:, t, :], x_d[:, t, :]).then_inc(s_x[t], 16)
            others = [rows(1, kv_norm.rearrange("(k p) -> k p", p=P)),
                      rows(2, b_norm.rearrange("a (k p) -> (a k) p", p=P)),
                      rows(3, ckv_norm.rearrange("(k p) -> k p", p=P)),
                      rows(4, b_q_norm.rearrange("a (k p) -> (a k) p", p=P)),
                      rows(5, a_conv.rearrange("a w (k p) -> (a w k) p", p=P)),
                      (cst[:, C_SEL:C_END], const[:, C_SEL:C_END])]
            assert len(others) == CONSTS
            for dst, src in others:
                sp.dma_start(dst, src).then_inc(s_const, 16)

            for t, part in ((2, 3), (3, 0)):
                sp.wait_ge(s_wlo, slot_free(t))
                load_w_in(1, t, part)
            with sp.Fori(2, KC + 1) as j:
                for t, part in enumerate((1, 2, 3, 0)):
                    sp.wait_ge(s_wlo, slot_free(4 * j + (t - 4)))
                    load_w_in(j, t, part)
            with sp.Fori(1, KC // 2 + 1) as i:
                for t in range(2):
                    sp.wait_ge(s_wlo, slot_free(2 * i + (OUT0 + t - 2)))
                    sp.dma_start(raw[:, t], w_out_d[:, :, bass.ds(i * 2 * P + (t - 2) * P, P)]
                                 ).then_inc(s_raw[t], 16)
            def load_b(e):
                kind, col, _ = b_tiles[e]
                n = B0 + e
                sp.wait_ge(s_wlo, slot_free(n))
                dst = raw[:, n % 2]
                if kind == "rope":
                    cols = [(0, col, ROPE), (ROPE, col + RH, RH), (ROPE + RH, col, RH)]
                    for to, frm, m in cols:
                        sp.dma_start(dst[:, :, to:to + m], w_dkv_d[:, :, frm:frm + m]
                                     ).then_inc(s_raw[n % 2], 16)
                else:
                    src = w_dkv_d if kind == "dkv" else w_b_d
                    sp.dma_start(dst, src[:, :, col:col + P]).then_inc(s_raw[n % 2], 16)

            def write_x2(t):
                sp.wait_ge(s_x2s, t + 1)
                sp.dma_start(x2_d[:, t, :], x2_st[t % 2][:]).then_inc(s_x2w[t % 2], 16)

            load_b(0)
            load_b(1)
            sp.wait_ge(s_tile, tile_done(B0 - 1))
            sp.dma_start(pos_i[:], positions[0:1, :].broadcast_to([P, S])).then_inc(s_pos, 16)
            for e in range(2, N_B):
                load_b(e)
                if e >= 6:
                    write_x2(2 * (e - 6))
                    write_x2(2 * (e - 6) + 1)

            def load_pair(c):
                per = NOPE + ROPE
                for odd, base_col in ((0, 0), (1, P // 2)):
                    rope = NOPE if odd == 0 else 0
                    parts = [(0 if odd == 0 else NOPE, 0, NOPE), (rope, NOPE, ROPE),
                             (rope + ROPE, NOPE + RH, RH), (rope + ROPE + RH, NOPE, RH)]
                    for to, frm, m in parts:
                        sp.dma_start(u_raw[:, odd * CQ:(odd + 1) * CQ, to:to + m],
                                     w_uq_d[:, :, bass.ds(c * 2 * per + odd * per + frm, m)]
                                     ).then_inc(s_u, 16)
                for what in range(2):
                    for odd in range(2):
                        sp.dma_start(u_raw[:, 2 * CQ + what * CKV:2 * CQ + (what + 1) * CKV,
                                           odd * NOPE:(odd + 1) * NOPE],
                                     w_ukv_d[:, :, bass.ds(c * 4 * NOPE + (2 * odd + what) * NOPE, NOPE)]
                                     ).then_inc(s_u, 16)

            load_pair(0)
            sp.wait_ge(s_clo, CKV + CQ)
            sp.dma_start(g_f[:], final_norm.rearrange("(a d) -> a d", a=1).broadcast_to([P, D])
                         ).then_inc(s_gf, 16)
            with sp.Fori(0, PAIRS - 1) as c:
                sp.wait_ge(s_ulo, c + 1)
                load_pair(c + 1)
            def load_wb(k):
                sp.dma_start(wb_raw[k % 2][:], w_bo_d[:, k, :]).then_inc(s_wb[k % 2], 16)

            def load_x2(t):
                sp.dma_start(x3[t][:], x2_d[:, t, :]).then_inc(s_x2r[t], 16)

            sp.wait_ge(s_pj, 10 + 12 * (PAIRS - 1))
            load_wb(0)
            load_wb(1)
            for w in s_x2w:
                sp.wait_ge(w, 16 * TB // 2)
            for t in (2, 3):
                load_x2(t)
            sp.wait_ge(s_pjv, 4 + 6 * (PAIRS - 1))
            load_x2(0)
            load_x2(1)
            for k in range(2, GC):
                sp.wait_ge(s_wbl, k - 1)
                load_wb(k)
            sp.wait_ge(s_splo, split_done(PAIRS - 1, "vo"))
            load_x2(4)
            sp.wait_ge(s_ogl, 1)
            load_x2(5)
            sp.wait_ge(s_t, 20 * PAIRS)
            load_x2(6)
            load_x2(7)

            for i, t in enumerate(LAST_ORDER[:-1]):
                if i in BY_POOL:
                    sp.wait_ge(s_yp, BY_POOL.index(i) + 1)
                else:
                    sp.wait_ge(s_y, BY_DVE_LAST.index(i) + 1)
                sp.dma_start(out_d[:, t, :], y_out[i % 4][:]).then_inc(s_out[i % 4], 16)
            for half in range(2):
                cols = slice(half * HALF, (half + 1) * HALF)
                sp.wait_ge(s_y, len(BY_DVE_LAST) + half)
                sp.dma_start(out_d[:, LAST_ORDER[-1], cols], y_out[(TB - 1) % 4][:, cols]
                             ).then_inc(s_out[(TB - 1) % 4], 16)
            for i in range(4):
                sp.wait_ge(s_out[i], 16 * (TB // 4 + (i == (TB - 1) % 4)))

        @block.tensor
        def _(pe):
            def products(dst, wh, wl, xh, xl, nk, before=None, halves=(0, 1), mid=None):
                for half in halves:
                    if half == 1 and mid is not None:
                        mid()
                    cols = slice(half * HALF, (half + 1) * HALF)
                    for k in range(nk):
                        if before is not None and half == halves[0]:
                            before(k)
                        for i, (w, z) in enumerate(((wh, xh), (wh, xl), (wl, xh))):
                            mm = nc.tensor.matmul(dst[:, cols], w(k), z(k, cols),
                                                  start=(k == 0 and i == 0),
                                                  stop=(k == nk - 1 and i == 2))
                return mm

            def tile(slot, pair, xh, xl, before=None, **more):
                return products(ps[:, pair], lambda k: w_h[:, slot, k, :], lambda k: w_l[:, slot, k, :],
                                lambda k, c: xh[:, k, c], lambda k, c: xl[:, k, c], KC, before,
                                **more)

            def widened(dst, wide):
                for t in range(TB):
                    mm = nc.tensor.transpose(dst[:, t * P:(t + 1) * P], wide[:, t, :], ident)
                return mm

            def square_sums(dst, of, first):
                for t in range(TB):
                    mm = nc.tensor.matmul(dst[:, first + t:first + t + 1], of[:, t * P:(t + 1) * P],
                                          ones, start=True, stop=True)
                return mm

            pe.sem_inc(s_tile, 2)
            pe.wait_ge(s_ident, 16)
            pe.wait_ge(s_ga, 16)
            nc.tensor.transpose(ps[:, 2, 0:KC], g_rows[0:KC, :], ident[0:KC, 0:KC]
                                ).then_inc(s_gtp, 1)
            pe.wait_ge(s_gt, 1)

            def x_units(first, last):
                for u in range(first, last):
                    half, k = u // KC, u % KC
                    bank = ps[:, 2 + u % 4 // 2, u % 2 * HALF:(u % 2 + 1) * HALF]
                    if u >= 4:
                        pe.wait_ge(s_xlo, u - 3)
                    for t in range(4):
                        if k == 0:
                            pe.wait_ge(s_x[4 * half + t], 16)
                        mm = nc.tensor.transpose(bank[:, t * P:(t + 1) * P],
                                                 x_in[:, 4 * half + t, k * P:(k + 1) * P], ident)
                    mm.then_inc(s_xtp, 1)

            def first_tiles(n, half):
                if half == 0:
                    pe.wait_ge(s_wlo, lo_done(n))
                def chunk_ready(k):
                    if (n, half) == (0, 0) and k < KC - 4:
                        x_units(k + 4, k + 5)
                    pe.wait_ge(s_xlo, half * KC + k + 1)

                return tile(n % 2, n, act_h, act_l, halves=(half,), before=chunk_ready)

            x_units(0, 4)
            first_tiles(0, 0)
            x_units(KC, KC + KC // 2)
            first_tiles(1, 0)
            x_units(KC + KC // 2, 2 * KC)
            first_tiles(0, 1).then_inc(s_tile, 1)
            pe.wait_ge(s_xlo, 2 * KC)
            pe.wait_ge(s_const, 16 * CONSTS)
            nc.tensor.transpose(ps[:, 2, 0:G_ROWS], g_rows[:], ident[0:G_ROWS, 0:G_ROWS]
                                ).then_inc(s_gtp, 1)
            pe.wait_ge(s_rw, 1)
            widened(ps[:, 3], r_wide).then_inc(s_rt, 1)
            first_tiles(1, 1).then_inc(s_tile, 1)
            pe.wait_ge(s_gt, 2)

            def a_tile(j, t):
                pe.wait_ge(s_wlo, lo_done(4 * j + t))
                pe.wait_ge(s_ev, slot_free(4 * j + t))
                tile(t % 2, t, act_h, act_l).then_inc(s_tile, 1)

            a_tile(0, 2)
            a_tile(0, 3)
            with pe.Fori(1, KC) as j:
                for t in range(4):
                    a_tile(j, t)

            def y_ready(k):
                if k in (0, KC - 1):
                    pe.wait_ge(s_ylo, KC - 1 if k == 0 else KC)

            with pe.Fori(0, KC // 2) as i:
                for t in range(2):
                    pe.wait_ge(s_wlo, lo_done(OUT0 + 2 * i + t))
                    pe.wait_ge(s_ev, evacuated(OUT0 + 2 * i + t - 2))
                    tile(t, t, y_h, y_l, y_ready).then_inc(s_tile, 1)

            def x2_ready(k):
                if k in (0, KC - 1):
                    pe.wait_ge(s_x2lo, KC - 1 if k == 0 else KC)

            def b_tile(e, mid=None):
                n = B0 + e
                pe.wait_ge(s_wlo, lo_done(n))
                if e != 2:
                    pe.wait_ge(s_ev, evacuated(n - (2 if e < 2 else 3)))
                tile(n % 2, e % 3, act_h, act_l, x2_ready if e == 0 else None, mid=mid
                     ).then_inc(s_tile, 1)

            def stream_back(t):
                if t >= 1:
                    pe.wait_ge(s_x2s, t)
                for k in range(KC):
                    mm = nc.tensor.transpose(ps[:, 3, k * P:(k + 1) * P],
                                             xt[:, k, t * P:(t + 1) * P], ident)
                mm.then_inc(s_x2t, 1)

            def q_rms():
                pe.wait_ge(s_cn, CKV)
                widened(ps[:, 3], rq_wide).then_inc(s_rt, 1)

            def rotated_key():
                pe.wait_ge(s_kr, 1)
                pe.wait_ge(s_cn, CKV + CQ)
                for half in range(2):
                    mm = nc.tensor.matmul(ps[:, 3, half * HALF:(half + 1) * HALF],
                                          cst[0:2 * ROPE, C_SEL:C_SEL + P],
                                          zk[:, half * HALF:(half + 1) * HALF], start=True, stop=True)
                mm.then_inc(s_krp, 1)

            b_tile(0)
            pe.wait_ge(s_acc, KC + 2)
            square_sums(ps[:, 3], acc, 0).then_inc(s_ss, 1)
            b_tile(1)
            pe.wait_ge(s_rw, 2)
            widened(ps[:, 3], r_wide).then_inc(s_rt, 1)
            b_tile(2)
            pe.wait_ge(s_rsb, 2)
            for i in range(TB // 2):
                stream_back(2 * i)
                b_tile(3 + i, mid=lambda: stream_back(2 * i + 1))
            pe.wait_ge(s_cacc, CKV - 1 + CQ - 1)
            pe.wait_ge(s_x2s, TB)
            square_sums(ps[:, 3], acc, 0)
            square_sums(ps[:, 3], acc_q, TB).then_inc(s_ss, 1)
            b_tile(7)
            pe.wait_ge(s_rw, 4)
            widened(ps[:, 3], rk_wide).then_inc(s_rt, 1)
            b_tile(8, mid=q_rms)
            b_tile(9, mid=rotated_key)

            def project(name, c, bank):
                dst = ps[:, bank // 2, bank % 2 * HALF:(bank % 2 + 1) * HALF]
                half = int(name[-1])
                cols = slice(half * HALF, (half + 1) * HALF)
                if name[0] == "r":
                    for t in range(4):
                        mm = nc.tensor.transpose(dst[:, t * P:(t + 1) * P],
                                                 rs_wide[:, 4 * half + t].rearrange("p a b -> p (a b)"),
                                                 ident)
                elif name[:2] == "vt":
                    for t in range(4):
                        kb = 4 * half + t
                        mm = nc.tensor.transpose(dst[:, t * P:(t + 1) * P],
                                                 v_t[:, kb * P:(kb + 1) * P], ident)
                else:
                    first, nk = {"qe": (0, CQ), "qo": (CQ, CQ), "k": (2 * CQ, CKV),
                                 "v": (2 * CQ + CKV, CKV)}[name[:-1]]
                    for k in range(nk):
                        xh = cq_h[:, k, cols] if nk == CQ else ckv_h[:, k, cols]
                        xl = cq_l[k][:, cols] if nk == CQ else ckv_l[:, k, cols]
                        passes = ((u_h, xh), (u_h, xl), (u_l, xh))
                        for i, (w, z) in enumerate(passes):
                            mm = nc.tensor.matmul(dst, w[:, first + k, :], z,
                                                  start=(k == 0 and i == 0),
                                                  stop=(k == nk - 1 and i == 2))
                mm.then_inc(s_pj, 1)

            def scores(h, g, q):
                width = (g + 1) * 2 * P
                qs = slice((2 * g + q) * P, (2 * g + q + 1) * P)
                for at0 in range(0, width, HALF):
                    w = min(HALF, width - at0)
                    dst = ps[:, q, at0:at0 + w]
                    last = at0 + w == width
                    for i, (a, b) in enumerate(((q_h, k_h), (q_h, k_l), (q_l, k_h))):
                        mm = nc.tensor.matmul(dst, a[h][:, qs], b[h][:, at0:at0 + w],
                                              start=(i == 0), stop=(i == 2 and not last))
                    if last:
                        first = q * P
                        mm = nc.tensor.matmul(ps[:, q, width - 2 * P + first:width], identb[:],
                                              maskb[:, q, first:], start=False, stop=True)
                mm.then_inc(s_s, 1)

            pe.wait_ge(s_clo, CKV)
            pe.wait_ge(s_ulo, 1)
            pe.wait_ge(s_ev, evacuated(B0 + 8))
            pe.wait_ge(s_clo, CKV + CQ)
            for i, name in enumerate(PRO):
                if name == "v0":
                    pe.wait_ge(s_krlo, 2)
                for was in PRO[:i]:
                    if PRO_BANKS[was] == PRO_BANKS[name] and was in BY_ACT:
                        pe.wait_ge(s_pja, act_count(None, was))
                    elif PRO_BANKS[was] == PRO_BANKS[name]:
                        pe.wait_ge(s_pjv, dve_count(None, was))
                if name == "vt0":
                    pe.wait_ge(s_ev, evacuated(LAST))
                    pe.wait_ge(s_splo, 2)
                    scores(0, 3, 0)
                    pe.wait_ge(s_pjv, dve_count(None, "qe1"))
                    scores(0, 3, 1)
                    pe.wait_ge(s_pja, act_count(None, "v1"))
                project(name, None, PRO_BANKS[name])
            pe.wait_ge(s_pja, 6)
            pe.wait_ge(s_pjv, 4)

            def last_products(dst, t, half, chunks, starts, stops):
                rows = slice(t * P, (t + 1) * P)
                cols = slice(half * HALF, (half + 1) * HALF)
                for k in chunks:
                    oh, ol = (og_h3, og_l3) if k == GC - 1 else (og_h[:, k, :], og_l[:, k, :])
                    for i, (a, b) in enumerate(((oh, wb_h), (oh, wb_l), (ol, wb_h))):
                        mm = nc.tensor.matmul(dst, a[:, rows], b[:, k, cols],
                                              start=(starts and k == chunks[0] and i == 0),
                                              stop=(stops and k == chunks[-1] and i == 2))
                return mm

            def attention(c, last):
                def turn(step, i):
                    n = t_before(step) + i
                    if i == 0:
                        pe.wait_ge(s_exp, 16 * c + (2 * step + 2))
                    pe.wait_ge(s_tl, 20 * c + (n + 1))
                    for j in range(2):
                        for q in range(2):
                            kb = 2 * i + j
                            mm = nc.tensor.transpose(
                                ps[:, 2, (n % 2) * HALF + (2 * j + q) * P:
                                   (n % 2) * HALF + (2 * j + q + 1) * P],
                                prob[step % 2][q][:, kb * P:(kb + 1) * P], ident)
                    mm.then_inc(s_t, 1)

                def score(step, q):
                    nxt = next_scores(step, last)
                    if nxt is not None:
                        nh, ng, number = nxt
                        if q == 0 and step == 3:
                            pe.wait_ge(s_splo, split_done(c, "qo"))
                        if q == 0 and step == 7:
                            pe.wait_ge(s_splo, 6 + split_done(c, "qe"))
                        pe.wait_ge(s_exp, 16 * c + (number + q - 1))
                        scores(nh, ng, q)

                def times_v(step):
                    h, g = STEPS[step]
                    pe.wait_ge(s_o, 8 * c + (step + 1))
                    pe.wait_ge(s_splo, split_done(c, "vo" if h else "ve"))
                    for kb in range(2 * g + 2):
                        if kb % 2 == 0:
                            pe.wait_ge(s_tl, 20 * c + (2 + t_before(step) + kb // 2 + 1))
                        for part in (pt_h[step % 2], pt_l[step % 2]):
                            mm = nc.tensor.matmul(ps[:, 3, 0:2 * P], vv[h][:, kb, :], part[:, kb, :],
                                                  start=(kb == 0 and part is pt_h[step % 2]),
                                                  stop=(kb == 2 * g + 1 and part is pt_l[step % 2]))
                    mm.then_inc(s_pv, 1)

                def unit(name):
                    if name[0] == "f":
                        n = int(name[1:])
                        if n == 0:
                            pe.wait_ge(s_wbl, GC - 1)
                            pe.wait_ge(s_ogl, GC - 1)
                            pe.wait_ge(s_pjv, 6 * c + 4)
                        else:
                            pe.wait_ge(s_fx, n)
                        last_products(ps[:, 3, HALF:], n // 2, n % 2, range(GC - 1), True, True
                                      ).then_inc(s_f, 1)
                        return
                    if name == "r0":
                        pe.wait_ge(s_rsw, c + 1)
                    if name == "k0":
                        pe.wait_ge(s_pjv, 6 * c + 4)
                    elif last and name == "r0":
                        pe.wait_ge(s_fx, 2 * EARLY)
                    else:
                        was = ORDER[ORDER.index(name) - 1]
                        if was in BY_ACT:
                            pe.wait_ge(s_pja, act_count(c, was))
                        else:
                            pe.wait_ge(s_pjv, dve_count(c, was, last))
                    if name == "k0":
                        pe.wait_ge(s_ulo, c + 2)
                    if name == "vt0":
                        pe.wait_ge(s_pja, act_count(c, "v1"))
                    project(name, c, 7)

                for step, (_, g) in enumerate(STEPS):
                    before, after = units_of(step, last)
                    for i in range(min(2, g + 1)):
                        turn(step, i)
                    score(step, 0)
                    score(step, 1)
                    for name in before:
                        unit(name)
                    for i in range(2, g + 1):
                        turn(step, i)
                    if step >= 1:
                        times_v(step - 1)
                    for name in after[:1]:
                        unit(name)
                    if step == 7:
                        times_v(step)
                    for name in after[1:]:
                        unit(name)

            with pe.Fori(0, PAIRS - 1) as c:
                attention(c, False)
            attention(PAIRS - 1, True)

            pe.wait_ge(s_wbl, GC)
            for i in range(2):
                for half in range(2):
                    last_products(ps[:, i, half * HALF:(half + 1) * HALF], LAST_ORDER[i], half,
                                  range(GC - 1), True, False)
            pe.wait_ge(s_ogl, GC)
            for i, t in enumerate(LAST_ORDER):
                some = i < 2 or t < EARLY
                for half in range(2):
                    if i >= 2:
                        pe.wait_ge(s_x3, 2 * (i - 2) + half + 1)
                    last_products(ps[:, i % 2, half * HALF:(half + 1) * HALF], t, half,
                                  (GC - 1,) if some else range(GC), i >= 2, True).then_inc(s_fin, 1)

        @block.scalar
        def _(act):
            def copy(dst, src, **more):
                return nc.scalar.activation(dst, src, ACT.Copy, **more)

            def weight_hi(n, slot):
                act.wait_ge(s_tile, slot_free(n))
                copy(w_h[:, slot], raw[:, slot]).then_inc(s_whi, 1)

            act.wait_ge(s_gtp, 1)
            copy(gt[:, 0:KC], ps[:, 2, 0:KC]).then_inc(s_gt, 1)

            def x_hi(u):
                half, k = u // KC, u % KC
                bank = ps[:, 2 + u % 4 // 2, u % 2 * HALF:(u % 2 + 1) * HALF]
                act.wait_ge(s_xtp, u + 1)
                copy(act_h[:, k, half * HALF:(half + 1) * HALF], bank).then_inc(s_xhi, 1)

            act.wait_ge(s_wg, 1)
            weight_hi(0, 0)
            for u in range(KC):
                x_hi(u)
            act.wait_ge(s_wg, 2)
            weight_hi(1, 1)
            for u in range(KC, KC + KC // 2):
                x_hi(u)
            for t in range(TB):
                nc.scalar.activation(junk[:, t, :], x_in[:, t, :], ACT.Square,
                                     accum_out=ssq[:, t:t + 1]).then_inc(s_xsq, 1)
            for u in range(KC + KC // 2, 2 * KC):
                x_hi(u)
            act.wait_ge(s_gtp, 2)
            copy(gt[:, KC:], ps[:, 2, KC:G_ROWS]).then_inc(s_gt, 1)
            act.wait_ge(s_rt, 1)
            copy(r_bc[:], ps[:, 3]).then_inc(s_rsb, 1)

            def gained_hi(n, slot):
                act.wait_ge(s_wg, n + 1)
                weight_hi(n, slot)

            def b_weight_hi(e):
                act.wait_ge(s_wg, N_A + 2 + e + 1)
                weight_hi(B0 + e, (B0 + e) % 2)

            with act.Fori(0, KC) as j:
                gained_hi(4 * j + 2, 0)
                gained_hi(4 * j + 3, 1)
                gained_hi(4 * j + 4, 0)
                act.wait_ge(s_ev, evacuated(4 * j + 2))
                nc.scalar.activation(sg[:], gr[:], ACT.Silu).then_inc(s_silu, 1)
                gained_hi(4 * j + 5, 1)
                act.wait_ge(s_ev, evacuated(4 * j + 3))
                copy(y_h[:, j, :], cv[:]).then_inc(s_yhi, 1)

            def stream(i, t, last):
                n0, m = OUT0 + t, 2 * i + t
                if last:
                    b_weight_hi(t)
                else:
                    act.wait_ge(s_raw[t], 16 * i + 16 * (n0 // 2 + 2))
                    weight_hi(2 * i + n0 + 2, t)
                act.wait_ge(s_acc, m + 1)
                act.wait_ge(s_ev, evacuated(2 * i + n0))
                copy(act_h[:, m, :], xt[:, m, :]).then_inc(s_x2hi, 1)
                nc.scalar.activation(sq[t][:], xt[:, m, :], ACT.Square).then_inc(s_x2sq, 1)

            with act.Fori(0, KC // 2 - 1) as i:
                for t in range(2):
                    stream(i, t, False)
            for t in range(2):
                stream(KC // 2 - 1, t, True)

            def staged(t):
                act.wait_ge(s_x2t, t + 1)
                if t >= 2:
                    act.wait_ge(s_x2w[t % 2], 16 * (t // 2))
                copy(x2_st[t % 2][:], ps[:, 3]).then_inc(s_x2s, 1)

            def gate_silu(z):
                act.wait_ge(s_ev, evacuated(B0 + E_G + z))
                nc.scalar.activation(gate[:, z, :], gate[:, z, :], ACT.Silu).then_inc(s_gsilu, 1)

            squares = [acc, sq[0], acc_q, sq[1], sq[0]]
            for e in range(2, N_B):
                b_weight_hi(e)
                if e == 3:
                    act.wait_ge(s_rt, 2)
                    copy(r_bc[:], ps[:, 3]).then_inc(s_rsb, 1)
                done = e - 2
                for z in ([0, 1] if e == 4 else [] if done < E_Q or done >= E_G else [done - 1]):
                    act.wait_ge(s_ev, evacuated(B0 + Z_TILES[z]))
                    if z == 0:
                        act.wait_ge(s_ss, 1)
                    if z == 4:
                        act.wait_ge(s_cacc, 1)
                    nc.scalar.activation(squares[z][:], zc[:, z, :], ACT.Square).then_inc(s_csq, 1)
                if 4 <= e < 8:
                    staged(2 * (e - 4))
                    staged(2 * (e - 4) + 1)
                if e == 6:
                    act.wait_ge(s_tab, 8)
                    nc.scalar.activation(tq[1][0:2 * ROPE, :], angle[0:2 * ROPE, :], ACT.Sin
                                         ).then_inc(s_sin, 1)
                if e == 8:
                    gate_silu(0)
            for k in range(CKV):
                act.wait_ge(s_cn, k + 1)
                copy(ckv_h[:, k, :], zc[:, k, :]).then_inc(s_chi, 1)
            gate_silu(1)
            act.wait_ge(s_u, 12 * 16)
            copy(u_h[:], u_raw[:]).then_inc(s_uhi, 1)
            for k in range(CQ):
                act.wait_ge(s_cn, CKV + k + 1)
                if k == 0:
                    for w in s_x2w:
                        act.wait_ge(w, 16 * TB // 2)
                copy(cq_h[:, k, :], zc[:, CKV + k, :]).then_inc(s_chi, 1)
            gate_silu(2)
            act.wait_ge(s_tile, tile_done(LAST))
            act.wait_ge(s_krp, 1)
            copy(k_h[0][NOPE:P, :], ps[NOPE:P, 3]).then_inc(s_krhi, 1)
            copy(k_h[1][0:NOPE, :], ps[0:NOPE, 3]).then_inc(s_krhi, 1)

            def proj_evac(name, c):
                if name not in BY_ACT:
                    return
                half = int(name[-1])
                bank = PRO_BANKS[name] if c is None else 7
                src = ps[:, bank // 2, bank % 2 * HALF:(bank % 2 + 1) * HALF]
                act.wait_ge(s_pj, pj_count(c, name))
                if c is not None and name == "k0":
                    act.wait_ge(s_splo, split_done(c, "ko"))
                if c is not None and name == "vt0":
                    act.wait_ge(s_splo, split_done(c, "vo"))
                if name[:2] == "vt":
                    dst = v_f[:, 4 * half:4 * half + 4, :].rearrange("p a b -> p (a b)")
                else:
                    dst = (k_f if name[0] == "k" else v_t)[:, half * HALF:(half + 1) * HALF]
                copy(dst, src).then_inc(s_pja, 1)

            def split_hi(what):
                odd = 1 if what[1] == "o" else 0
                rows = slice(NOPE, P) if odd else slice(0, NOPE)
                if what[0] == "q":
                    op = copy(q_h[odd][:], q_f[odd][:])
                elif what[0] == "k":
                    op = copy(k_h[odd][rows, :], k_f[rows, :])
                else:
                    op = copy(vv[odd][:, :, 0:VH], v_f[:, :, odd * VH:(odd + 1) * VH])
                op.then_inc(s_sphi, 1)

            def exps(number, c, step, q):
                h, g = STEPS[step % 8]
                width = (g + 1) * 2 * P
                act.wait_ge(s_mx, 16 * c + (number + 1))
                slot = 2 * (step % 2) + q
                nc.scalar.activation(prob[step % 2][q][:, 0:width], ps[:, q, 0:width], ACT.Exp,
                                     bias=smaxn[:, slot:slot + 1], scale=SCALE,
                                     accum_out=rsum[:, h, 2 * g + q:2 * g + q + 1]).then_inc(s_exp, 1)

            act.wait_ge(s_pjv, dve_count(None, "qe1"))
            split_hi("qe")
            proj_evac("k0", None)
            proj_evac("k1", None)
            act.wait_ge(s_pja, act_count(None, "k1"))
            split_hi("ke")
            proj_evac("v0", None)
            proj_evac("v1", None)
            gate_silu(3)
            exps(0, 0, 0, 0)
            proj_evac("vt0", None)
            exps(1, 0, 0, 1)
            proj_evac("vt1", None)
            act.wait_ge(s_pja, act_count(None, "vt1"))
            split_hi("ve")

            def attention(c, last):
                def o_low(step):
                    act.wait_ge(s_pv, 8 * c + (step + 1))
                    copy(o_lo[:], ps[VH:P, 3, 0:2 * P]).then_inc(s_om, 1)

                def wb_hi(k):
                    act.wait_ge(s_wb[k % 2], 16 * (k // 2 + 1))
                    copy(wb_h[:, k, :], wb_raw[k % 2][:]).then_inc(s_wbh, 1)

                for step, (h, g) in enumerate(STEPS):
                    before, after = units_of(step, last)

                    def hi(i):
                        n = t_before(step) + i
                        act.wait_ge(s_t, 20 * c + (n + 1))
                        copy(pt_h[step % 2][:, 2 * i:2 * i + 2, :].rearrange("p a b -> p (a b)"),
                             ps[:, 2, n % 2 * HALF:(n % 2 + 1) * HALF]).then_inc(s_th, 1)

                    nxt = next_scores(step, last)

                    def next_exp(q):
                        number = nxt[2]
                        if q == 0 and number == 16:
                            act.wait_ge(s_rr, c + 1)
                        exps(number + q, c, step + 1, q)

                    for i in range(min(2, g + 1)):
                        hi(i)
                    if step == 6:
                        next_exp(0)
                        next_exp(1)
                    for name in before:
                        proj_evac(name, c)
                    for i in range(2, g + 1):
                        if i == 3:
                            next_exp(0)
                            next_exp(1)
                        hi(i)
                    if step == 0:
                        if not last:
                            act.wait_ge(s_u, 192 * c + 384)
                            act.wait_ge(s_pj, 12 * c + 10)
                            copy(u_h[:], u_raw[:]).then_inc(s_uhi, 1)
                        act.wait_ge(s_pja, 6 * c + 6)
                        split_hi("ko")
                        split_hi("vo")
                    if step == 1:
                        act.wait_ge(s_pjv, 6 * c + 4)
                        split_hi("qo")
                    if step == 3 and not last:
                        act.wait_ge(s_s, 16 * c + 8)
                        act.wait_ge(s_pja, act_count(c, "k1"))
                        split_hi("ke")
                    if step == 4 and not last:
                        act.wait_ge(s_pjv, dve_count(c, "qe1"))
                        split_hi("qe")
                    if step == 7 and not last:
                        act.wait_ge(s_pja, act_count(c, "vt1"))
                        split_hi("ve")
                    if last and step == 3:
                        wb_hi(2)
                    if last and step == 5:
                        wb_hi(3)
                    if nxt is not None and g != 3 and step != 6:
                        next_exp(0)
                        if step == 7:
                            o_low(6)
                        next_exp(1)
                    if 1 <= step < 7 or (last and step == 7):
                        o_low(step - 1)
                    if last and step in (1, 2):
                        wb_hi(step - 1)
                    for name in after:
                        proj_evac(name, c)
                    if step == 7:
                        o_low(step)
                    if last and step == 7:
                        act.wait_ge(s_s, 16 * PAIRS)
                        act.wait_ge(s_og, PAIRS + 1)
                        copy(og_h3[:], og[:, PAIRS - 1, :]).then_inc(s_ogh, 1)

            with act.Fori(0, PAIRS - 1) as c:
                attention(c, False)
            attention(PAIRS - 1, True)

            def scaled(i):
                act.wait_ge(s_fr, i + 1)
                copy(x3[LAST_ORDER[i]][:], x3[LAST_ORDER[i]][:], scale=rms[:, i:i + 1]
                     ).then_inc(s_ya, 1)

            for i, t in enumerate(LAST_ORDER):
                for half in range(2):
                    cols = slice(half * HALF, (half + 1) * HALF)
                    n = 2 * i + half
                    act.wait_ge(s_x3, n + 1)
                    if n >= 2:
                        act.wait_ge(s_x3q, n - 1)
                    nc.scalar.activation(x3_sq[:, cols], x3[t][:, cols], ACT.Square,
                                         accum_out=ssq[:, n:n + 1]).then_inc(s_x3q, 1)
                if i - 1 in BY_POOL:
                    scaled(i - 1)

        @block.gpsimd
        def _(pool):
            def rsqrt(first, n, waited):
                pool.wait_ge(s_ms, waited)
                nc.gpsimd.tensor_tensor(rms[:, first:first + n], msq[:, first:first + n],
                                        cst[:, C_POW:C_POW + 1].broadcast_to([P, n]),
                                        ALU.pow).then_inc(s_pow, 1)

            def weight_gain(n, fill, slot, gain):
                pool.wait_ge(s_raw[slot], fill)
                nc.gpsimd.tensor_tensor(raw[:, slot], raw[:, slot],
                                        gain.unsqueeze(2).broadcast_to([P, KC, P]), ALU.mult
                                        ).then_inc(s_wg, 1)

            pool.wait_ge(s_gt, 1)
            weight_gain(0, 16, 0, g_a)
            weight_gain(1, 16, 1, g_a)
            pool.wait_ge(s_const, 16 * CONSTS)
            rsqrt(0, TB, 1)
            with pool.Fori(0, KC - 1) as j:
                for t in range(4):
                    weight_gain(4 * j + 2 + t, 32 * j + 16 * (t // 2 + 2), t % 2, g_a)
            weight_gain(N_A - 2, fills(N_A - 2), 0, g_a)
            weight_gain(N_A - 1, fills(N_A - 1), 1, g_a)
            pool.wait_ge(s_wg, N_A)
            for n in (OUT0, OUT0 + 1):
                pool.wait_ge(s_raw[n % 2], fills(n))
                pool.sem_inc(s_wg, 1)
            pool.wait_ge(s_gt, 2)
            for e in range(N_B):
                n = B0 + e
                weight_gain(n, fills(n), n % 2, b_tiles[e][2])
                if e == 1:
                    rsqrt(0, TB, 2)
            rsqrt(0, 2 * TB, 4)

            def split_lo(what, number):
                odd = 1 if what[1] == "o" else 0
                rows = slice(NOPE, P) if odd else slice(0, NOPE)
                pool.wait_ge(s_sphi, number + 1)
                if not isinstance(number, int) or number > 0:
                    pool.wait_ge(s_splo, number)
                if what[0] == "q":
                    dst, src, hi = q_l[odd][:], q_f[odd][:], q_h[odd][:]
                elif what[0] == "k":
                    dst, src, hi = k_l[odd][rows, :], k_f[rows, :], k_h[odd][rows, :]
                else:
                    dst, src = vv[odd][:, :, VH:2 * VH], v_f[:, :, odd * VH:(odd + 1) * VH]
                    hi = vv[odd][:, :, 0:VH]
                nc.gpsimd.tensor_tensor(dst, src, hi.bitcast(F32), ALU.subtract).then_inc(s_splo, 1)

            for number, what in enumerate(("qe", "ke", "ve")):
                split_lo(what, number)

            def widen(c, done):
                pool.wait_ge(s_rr, c + 1)
                pool.wait_ge(s_splo, done)
                wide = [P, TB, 2, VH]
                nc.gpsimd.tensor_tensor(
                    rs_wide[:], rrec[:].rearrange("p h t -> p t h").unsqueeze(3).broadcast_to(wide),
                    ones.unsqueeze(2).unsqueeze(3).broadcast_to(wide), ALU.mult).then_inc(s_rsw, 1)

            with pool.Fori(0, PAIRS - 1) as c:
                for number, what in enumerate(("ko", "vo", "qo", "ke", "qe")):
                    split_lo(what, 6 * c + (3 + number))
                widen(c, 6 * c + 8)
                pool.wait_ge(s_rsw, c + 1)
                split_lo("ve", 6 * c + 8)
                pool.wait_ge(s_pjv, dve_count(c, "r1"))
                pool.wait_ge(s_o, 8 * c + 9)
                nc.gpsimd.tensor_tensor(og[:, c, :], o_t[:], gs[:], ALU.mult).then_inc(s_og, 1)
                pool.wait_ge(s_og, c + 2)
            for number, what in enumerate(("ko", "vo", "qo")):
                split_lo(what, 6 * (PAIRS - 1) + 3 + number)
            for k in range(GC):
                pool.wait_ge(s_wbh, k + 1)
                nc.gpsimd.tensor_tensor(wb_l[:, k, :], wb_raw[k % 2][:], wb_h[:, k, :].bitcast(F32),
                                        ALU.subtract).then_inc(s_wbl, 1)
            widen(PAIRS - 1, 6 * PAIRS)
            for i in range(TB):
                pool.wait_ge(s_fms, i + 1)
                nc.gpsimd.tensor_tensor(rms[:, i:i + 1], msq[:, TB + i:TB + i + 1],
                                        cst[:, C_POW:C_POW + 1], ALU.pow).then_inc(s_fr, 1)
                if i - 1 in BY_POOL:
                    pool.wait_ge(s_ya, BY_POOL.index(i - 1) + 1)
                    if i == BY_POOL[0] + 1:
                        pool.wait_ge(s_gf, 16)
                    if i - 1 >= 4:
                        pool.wait_ge(s_out[(i - 1) % 4], 16)
                    nc.gpsimd.tensor_tensor(y_out[(i - 1) % 4][:], x3[LAST_ORDER[i - 1]][:], g_f[:],
                                            ALU.mult).then_inc(s_yp, 1)

        @block.vector
        def _(dve):
            tt, ts, stt = nc.vector.tensor_tensor, nc.vector.tensor_scalar, nc.vector.scalar_tensor_tensor

            def weight_lo(n, slot):
                dve.wait_ge(s_whi, n + 1)
                tt(w_l[:, slot], raw[:, slot], w_h[:, slot].bitcast(F32), ALU.subtract
                   ).then_inc(s_wlo, 1)

            def mean_square(src, first, n, width):
                ts(msq[:, first:first + n], src, 1.0 / width, EPS, ALU.mult, ALU.add).then_inc(s_ms, 1)

            def widen(wide, first, waited):
                dve.wait_ge(s_pow, waited)
                nc.vector.tensor_copy(wide[:], rms[:, first:first + TB].unsqueeze(2)
                                      .broadcast_to([P, TB, P])).then_inc(s_rw, 1)

            dve.sem_inc(s_wlo, 2)
            dve.sem_inc(s_ev, 3)
            dve.sem_inc(s_tl, 2)
            dve.sem_inc(s_o, 1)
            dve.sem_inc(s_og, 1)
            nc.vector.memset(v[:, 0:CONV_WIDTH - 1], 0.0).then_inc(s_init, 1)

            def x_lo(u):
                half, k = u // KC, u % KC
                cols = slice(half * HALF, (half + 1) * HALF)
                bank = ps[:, 2 + u % 4 // 2, u % 2 * HALF:(u % 2 + 1) * HALF]
                dve.wait_ge(s_xhi, u + 1)
                tt(act_l[:, k, cols], bank, act_h[:, k, cols].bitcast(F32), ALU.subtract
                   ).then_inc(s_xlo, 1)

            weight_lo(0, 0)
            for u in range(KC):
                x_lo(u)
            weight_lo(1, 1)
            for u in range(KC, KC + KC // 2):
                x_lo(u)
            dve.wait_ge(s_const, 16 * CONSTS)
            nc.vector.tensor_copy(identb[:], ident).then_inc(s_init, 1)
            nc.vector.tensor_copy(maskb[:].rearrange("p a b -> p (a b)"), cst[:, C_MASK:C_END]
                                  ).then_inc(s_init, 1)
            dve.wait_ge(s_xsq, TB)
            mean_square(ssq[:, 0:TB], 0, TB, D)
            for u in range(KC + KC // 2, 2 * KC):
                x_lo(u)
            widen(r_wide, 0, 1)
            dve.wait_ge(s_rsb, 1)
            tt(r2_bc[:], r_bc[:], r_bc[:], ALU.mult).then_inc(s_ev, 1)

            with dve.Fori(0, KC) as j:
                dve.wait_ge(s_tile, tile_done(4 * j))
                dve.wait_ge(s_ev, evacuated(4 * j - 1))
                tt(cr[:], ps[:, 0], r2_bc[:], ALU.mult).then_inc(s_ev, 1)
                weight_lo(4 * j + 2, 0)
                dve.wait_ge(s_tile, tile_done(4 * j + 1))
                dve.wait_ge(s_ev, evacuated(4 * j))
                tt(v[:, 2:2 + S], ps[:, 1], cr[:], ALU.mult).then_inc(s_ev, 1)
                weight_lo(4 * j + 3, 1)
                dve.wait_ge(s_ev, evacuated(4 * j + 1))
                ts(cv[:], v[:, 0:S], conv_w[:, 0, bass.ds(j, 1)], None, ALU.mult).then_inc(s_cv, 1)
                for w in range(1, CONV_WIDTH):
                    dve.wait_ge(s_cv, 5 * j + w)
                    stt(cv[:], v[:, w:w + S], conv_w[:, w, bass.ds(j, 1)], cv[:], ALU.mult, ALU.add
                        ).then_inc(s_cv, 1)
                dve.wait_ge(s_tile, tile_done(4 * j + 2))
                tt(gr[:], ps[:, 2], r_bc[:], ALU.mult).then_inc(s_ev, 1)
                weight_lo(4 * j + 4, 0)
                dve.wait_ge(s_cv, 5 * j + 3)
                tt(cv[:], cv[:], r_bc[:], ALU.mult).then_inc(s_cv, 1)
                dve.wait_ge(s_silu, j + 1)
                dve.wait_ge(s_cv, 5 * j + 4)
                tt(cv[:], cv[:], sg[:], ALU.mult).then_inc(s_cv, 1)
                dve.wait_ge(s_tile, tile_done(4 * j + 3))
                dve.wait_ge(s_cv, 5 * j + 5)
                tt(cv[:], cv[:], ps[:, 3], ALU.mult).then_inc(s_ev, 1)
                weight_lo(4 * j + 5, 1)
                dve.wait_ge(s_yhi, j + 1)
                tt(y_l[:, j, :], cv[:], y_h[:, j, :].bitcast(F32), ALU.subtract).then_inc(s_ylo, 1)

            nc.vector.memset(acc[:], 0.0).then_inc(s_acc, 2)

            def stream(i, t):
                n0, m = OUT0 + t, 2 * i + t
                tt(xt[:, m, :], act_h[:, m, :].bitcast(F32), act_l[:, m, :].bitcast(F32), ALU.add
                   ).then_inc(s_xr, 1)
                dve.wait_ge(s_xr, m + 1)
                dve.wait_ge(s_tile, tile_done(2 * i + n0))
                tt(xt[:, m, :], xt[:, m, :], ps[:, t], ALU.add).then_inc(s_ev, 1)
                weight_lo(2 * i + n0 + 2, t)
                dve.wait_ge(s_x2hi, m + 1)
                tt(act_l[:, m, :], xt[:, m, :], act_h[:, m, :].bitcast(F32), ALU.subtract
                   ).then_inc(s_x2lo, 1)
                dve.wait_ge(s_x2sq, m + 1)
                dve.wait_ge(s_acc, m + 2)
                tt(acc[:], acc[:], sq[t][:], ALU.add).then_inc(s_acc, 1)

            with dve.Fori(0, KC // 2) as i:
                for t in range(2):
                    stream(i, t)

            dve.wait_ge(s_ss, 1)
            mean_square(ps[:, 3, 0:TB], 0, TB, D)
            weight_lo(B0 + 2, 0)
            widen(r_wide, 0, 2)
            weight_lo(B0 + 3, 1)
            dve.wait_ge(s_rsb, 2)

            def evacuate(e):
                pair = ps[:, e % 3]
                dve.wait_ge(s_tile, tile_done(B0 + e))
                if e == E_ROPE:
                    tt(zk[:], pair[0:2 * ROPE, :], r_bc[0:2 * ROPE, :], ALU.mult).then_inc(s_ev, 1)
                elif e < E_G:
                    tt(zc[:, Z_TILES.index(e), :], pair, r_bc[:], ALU.mult).then_inc(s_ev, 1)
                else:
                    tt(gate[:, e - E_G, :], pair, r_bc[:], ALU.mult).then_inc(s_ev, 1)

            def sum_squares(into, frm, squares_done):
                dve.wait_ge(s_csq, squares_done)
                if squares_done == 5:
                    dve.wait_ge(s_cacc, 2)
                tt(into[:], into[:], frm[:], ALU.add).then_inc(s_cacc, 1)

            def table_step(op):
                op.then_inc(s_tab, 1)
                table[0] += 1
                dve.wait_ge(s_tab, table[0])

            rows = slice(0, 2 * ROPE)
            freq = cst[rows, C_FREQ:C_FREQ + 1]

            def whole_turns():
                dve.wait_ge(s_pos, 16)
                table_step(nc.vector.tensor_copy(pos_f[rows, :], pos_i[rows, :]))
                table_step(ts(pos_f[rows, :], pos_f[rows, :], freq, None, ALU.mult))
                table_step(ts(turns[rows, :], pos_f[rows, :], 1 / (2 * np.pi),
                              cst[rows, C_TURN:C_TURN + 1], ALU.mult, ALU.add))
                table_step(ts(turns[rows, :], turns[rows, :], ROUND, ROUND, ALU.add, ALU.subtract))

            def reduced():
                for i, part in enumerate((TWO_PI_A, TWO_PI_B, TWO_PI_C)):
                    src = pos_f if i == 0 else angle
                    table_step(stt(angle[rows, :], turns[rows, :], -part, src[rows, :],
                                   ALU.mult, ALU.add))
                table_step(ts(angle[rows, :], angle[rows, :], cst[rows, C_PHASE:C_PHASE + 1], PI_IN,
                              ALU.add, ALU.min))

            def rotary_tables():
                dve.wait_ge(s_sin, 1)
                nc.vector.tensor_copy(tq[0][NOPE:P, :], tq[1][rows, :]).then_inc(s_tab, 1)
                nc.vector.memset(tq[0][0:NOPE, :], 1.0).then_inc(s_tab, 1)
                nc.vector.memset(tq[1][NOPE:P, :], 1.0).then_inc(s_tab, 1)
                dve.wait_ge(s_ev, evacuated(B0 + E_ROPE))
                tt(zk[:], zk[:], tq[1][rows, :], ALU.mult).then_inc(s_kr, 1)

            table = [0]
            evacuate(0)
            evacuate(1)
            whole_turns()
            for e in range(4, N_B):
                evacuate(e - 2)
                weight_lo(B0 + e, (B0 + e) % 2)
                if e == 4:
                    reduced()
                if e == 5:
                    sum_squares(acc, sq[0], 2)
                if e == 6:
                    sum_squares(acc_q, sq[1], 4)
                if e == 7:
                    sum_squares(acc_q, sq[0], 5)
                    rotary_tables()
                if e == 8:
                    dve.wait_ge(s_ss, 2)
                    mean_square(ps[:, 3, 0:TB], 0, TB, KV_RANK)
                    mean_square(ps[:, 3, TB:2 * TB], TB, TB, Q_RANK)
                    widen(rk_wide, 0, 3)
                    widen(rq_wide, TB, 3)
            dve.wait_ge(s_rt, 3)
            for k in range(CKV):
                stt(zc[:, k, :], zc[:, k, :], g_ckv[:, k:k + 1], ps[:, 3], ALU.mult, ALU.mult
                    ).then_inc(s_cn, 1)
            for k in range(CKV):
                dve.wait_ge(s_chi, k + 1)
                tt(ckv_l[:, k, :], zc[:, k, :], ckv_h[:, k, :].bitcast(F32), ALU.subtract
                   ).then_inc(s_clo, 1)
            dve.wait_ge(s_rt, 4)
            for k in range(CQ):
                stt(zc[:, CKV + k, :], zc[:, CKV + k, :], g_q[:, k:k + 1], ps[:, 3], ALU.mult, ALU.mult
                    ).then_inc(s_cn, 1)
            dve.wait_ge(s_uhi, 1)
            tt(u_l[:], u_raw[:], u_h[:].bitcast(F32), ALU.subtract).then_inc(s_ulo, 1)
            evacuate(8)
            for k in range(CQ):
                dve.wait_ge(s_chi, CKV + k + 1)
                if k == 0:
                    for w in s_x2w:
                        dve.wait_ge(w, 16 * TB // 2)
                tt(cq_l[k][:], zc[:, CKV + k, :], cq_h[:, k, :].bitcast(F32), ALU.subtract
                   ).then_inc(s_clo, 1)
            evacuate(9)
            def proj_evac(name, c, last=False):
                if name[0] == "f":
                    n = int(name[1:])
                    part = x3[n // 2][:, n % 2 * HALF:(n % 2 + 1) * HALF]
                    dve.wait_ge(s_f, n + 1)
                    dve.wait_ge(s_x2r[n // 2], 16)
                    tt(part, part, ps[:, 3, HALF:], ALU.add).then_inc(s_fx, 1)
                    return
                if name not in BY_DVE:
                    return
                half = int(name[-1])
                cols = slice(half * HALF, (half + 1) * HALF)
                bank = PRO_BANKS[name] if c is None else 7
                src = ps[:, bank // 2, bank % 2 * HALF:(bank % 2 + 1) * HALF]
                dve.wait_ge(s_pj, pj_count_last(name) if last else pj_count(c, name))
                if name[0] == "r":
                    tt(gs[:, cols], src, gate[:, c, cols], ALU.mult).then_inc(s_pjv, 1)
                    return
                odd = 1 if name[1] == "o" else 0
                if c is not None and half == 0:
                    dve.wait_ge(s_splo, split_done(c, "qo" if odd else "qe"))
                tt(q_f[odd][:, cols], src, tq[odd][:, cols], ALU.mult).then_inc(s_pjv, 1)

            def row_max(number, c, step, q):
                slot = 2 * (step % 2) + q
                g = STEPS[step % 8][1]
                dve.wait_ge(s_s, 16 * c + (number + 1))
                nc.vector.reduce_max(smax[:, slot:slot + 1], ps[:, q, 0:(g + 1) * 2 * P], AX_X
                                     ).then_inc(s_mxr, 1)
                dve.wait_ge(s_mxr, 16 * c + (number + 1))
                ts(smaxn[:, slot:slot + 1], smax[:, slot:slot + 1], -SCALE, None, ALU.mult
                   ).then_inc(s_mx, 1)

            proj_evac("qe0", None)
            dve.wait_ge(s_krhi, 2)
            tt(k_l[0][NOPE:P, :], ps[NOPE:P, 3], k_h[0][NOPE:P, :].bitcast(F32), ALU.subtract
               ).then_inc(s_krlo, 1)
            proj_evac("qe1", None)
            tt(k_l[1][0:NOPE, :], ps[0:NOPE, 3], k_h[1][0:NOPE, :].bitcast(F32), ALU.subtract
               ).then_inc(s_krlo, 1)
            proj_evac("qo0", None)
            row_max(0, 0, 0, 0)
            row_max(1, 0, 0, 1)
            proj_evac("qo1", None)

            def attention(c, last):
                def o_add(step):
                    h, g = STEPS[step]
                    if step == 0:
                        dve.wait_ge(s_og, c + 1)
                    dve.wait_ge(s_om, 8 * c + (step + 1))
                    tt(o_t[h * VH:(h + 1) * VH, g * 2 * P:(g + 1) * 2 * P], ps[0:VH, 3, 0:2 * P],
                       o_lo[:], ALU.add).then_inc(s_o, 1)

                def og_hi(k):
                    dve.wait_ge(s_og, k + 2)
                    nc.vector.tensor_copy(og_h[:, k, :], og[:, k, :]).then_inc(s_ogh, 1)

                def og_lo(k):
                    dve.wait_ge(s_ogh, k + 1)
                    hi, to = (og_h3[:], og_l3[:]) if k == GC - 1 else (og_h[:, k, :], og_l[:, k, :])
                    tt(to, og[:, k, :], hi.bitcast(F32), ALU.subtract).then_inc(s_ogl, 1)

                for step, (h, g) in enumerate(STEPS):
                    nxt = next_scores(step, last)
                    before, after = units_of(step, last)

                    def lo(i):
                        n = t_before(step) + i
                        dve.wait_ge(s_th, 20 * c + (n + 1))
                        dst = pt_l[step % 2][:, 2 * i:2 * i + 2, :].rearrange("p a b -> p (a b)")
                        hi = pt_h[step % 2][:, 2 * i:2 * i + 2, :].rearrange("p a b -> p (a b)")
                        tt(dst, ps[:, 2, n % 2 * HALF:(n % 2 + 1) * HALF], hi.bitcast(F32),
                           ALU.subtract).then_inc(s_tl, 1)

                    if step == 7:
                        dve.wait_ge(s_exp, 16 * c + 16)
                        nc.vector.reciprocal(rrec[:], rsum[:]).then_inc(s_rr, 1)
                    for i in range(min(2, g + 1)):
                        lo(i)
                    if nxt is not None:
                        row_max(nxt[2], c, step + 1, 0)
                        row_max(nxt[2] + 1, c, step + 1, 1)
                    for name in before:
                        proj_evac(name, c, last)
                    for i in range(2, g + 1):
                        lo(i)
                    if step == 0 and not last:
                        dve.wait_ge(s_uhi, c + 2)
                        tt(u_l[:], u_raw[:], u_h[:].bitcast(F32), ALU.subtract).then_inc(s_ulo, 1)
                    if last and step == 1:
                        og_hi(0)
                        og_lo(0)
                        og_hi(1)
                    if last and step == 2:
                        dve.wait_ge(s_splo, split_done(c, "qo"))
                        og_lo(1)
                        og_hi(2)
                    if last and step == 3:
                        og_lo(2)
                    if step >= 1:
                        o_add(step - 1)
                    for name in after[:1]:
                        proj_evac(name, c, last)
                    if step == 7:
                        o_add(step)
                    for name in after[1:]:
                        proj_evac(name, c, last)
                if last:
                    dve.wait_ge(s_pjv, dve_count(c, "r1", last))
                    dve.wait_ge(s_o, 8 * c + 9)
                    tt(og[:, c, :], o_t[:], gs[:], ALU.mult).then_inc(s_og, 1)
                    og_lo(3)

            dve.wait_ge(s_gsilu, GC)
            with dve.Fori(0, PAIRS - 1) as c:
                attention(c, False)
            attention(PAIRS - 1, True)

            def normed(i, cols):
                if i in BY_POOL:
                    return
                dve.wait_ge(s_fr, i + 1)
                if i == 0:
                    dve.wait_ge(s_gf, 16)
                if i >= 4:
                    dve.wait_ge(s_out[i % 4], 16)
                stt(y_out[i % 4][:, cols], x3[LAST_ORDER[i]][:, cols], rms[:, i:i + 1], g_f[:, cols],
                    ALU.mult, ALU.mult).then_inc(s_y, 1)

            dve.wait_ge(s_fx, 2 * EARLY)
            for i, t in enumerate(LAST_ORDER):
                dve.wait_ge(s_x2r[t], 16)
                for half in range(2):
                    cols = slice(half * HALF, (half + 1) * HALF)
                    dve.wait_ge(s_fin, 2 * i + half + 1)
                    tt(x3[t][:, cols], x3[t][:, cols], ps[:, i % 2, cols], ALU.add
                       ).then_inc(s_x3, 1)
                if i >= 1:
                    normed(i - 1, slice(0, D))
                dve.wait_ge(s_x3q, 2 * i + 1)
                ts(msq[:, i:i + 1], ssq[:, 2 * i:2 * i + 1], 1.0 / D, EPS, ALU.mult, ALU.add
                   ).then_inc(s_fm, 1)
                dve.wait_ge(s_x3q, 2 * i + 2)
                dve.wait_ge(s_fm, i + 1)
                stt(msq[:, TB + i:TB + i + 1], ssq[:, 2 * i + 1:2 * i + 2], 1.0 / D, msq[:, i:i + 1],
                    ALU.mult, ALU.add).then_inc(s_fms, 1)
            normed(TB - 1, slice(0, HALF))
            normed(TB - 1, slice(HALF, D))


_INS = ["x", "positions", "a_norm", "a_w_in", "a_conv", "a_w_out", "kv_norm", "w_dkv", "ckv_norm",
        "w_ukv", "b_norm", "b_w_in", "b_q_norm", "b_w_uq", "b_w_out", "final_norm"]


def kernel(**inputs):
    import concourse.bacc as bacc
    from concourse.bass_utils import run_bass_kernel_spmd

    nc = bacc.Bacc("TRN2", target_bir_lowering=False, num_devices=1, dynamic_dma_scratch_size=1024)
    given = {name: np.ascontiguousarray(inputs[name]) for name in _INS}
    given["const"] = constants()
    arrays, args = {}, []
    for name, a in given.items():
        arrays[f"in_{name}"] = a
        args.append(nc.dram_tensor(f"in_{name}", a.shape, mybir.dt.from_np(a.dtype),
                                   kind="ExternalInput").ap())
    args.append(nc.dram_tensor("out", (1, S, D), F32, kind="ExternalOutput").ap())
    trunk(nc, *args)
    r = run_bass_kernel_spmd(nc, [arrays], core_ids=[0])
    return r.results[0]["out"]
```
